# Optimizing a Trainium2 kernel written in Bass

```python
import math
import jax, jax.numpy as jnp
from jax import lax
import numpy as np
import jax
import jax.numpy as jnp

D_MODEL = 1024
BATCH = 1
SEQ = 512
DEPTH = 2

ATTN_WIDTH = D_MODEL // 2
RNN_WIDTH = D_MODEL - ATTN_WIDTH
DIFF_HEAD_DIM = 64
N_DIFF_HEADS = ATTN_WIDTH // (2 * DIFF_HEAD_DIM)
V_HEAD_DIM = 2 * DIFF_HEAD_DIM
ROT_DIM = DIFF_HEAD_DIM // 4
ROPE_THETA = 500000.0
LRU_BLOCK = 64
N_LRU_BLOCKS = RNN_WIDTH // LRU_BLOCK
CONV_WIDTH = 4
LRU_C = 8.0
D_FF = 4 * D_MODEL
PLE_DIM = 256
Q_BLOCK = 128
EPS = 1e-6
IN_WIDTH = 3 * ATTN_WIDTH + 2 * RNN_WIDTH


def rms_norm(x, g):
    xf = x.astype(jnp.float32)
    y = xf * lax.rsqrt(jnp.mean(xf * xf, axis=-1, keepdims=True) + EPS)
    return (y * g.astype(jnp.float32)).astype(x.dtype)

def partial_rope(x, positions):
    half = ROT_DIM // 2
    inv_freq = ROPE_THETA ** (-jnp.arange(half, dtype=jnp.float32) * 2.0 / ROT_DIM)
    ang = positions.astype(jnp.float32)[..., None] * inv_freq
    cos = jnp.cos(ang)[:, :, None, None, :]
    sin = jnp.sin(ang)[:, :, None, None, :]
    xr = x[..., :ROT_DIM].astype(jnp.float32)
    x1, x2 = xr[..., :half], xr[..., half:]
    rot = jnp.concatenate([x1 * cos - x2 * sin, x2 * cos + x1 * sin], axis=-1)
    return jnp.concatenate([rot.astype(x.dtype), x[..., ROT_DIM:]], axis=-1)

def diff_attention(q, k, v, lam):
    B, S = q.shape[0], q.shape[1]
    nb = S // Q_BLOCK
    scale = DIFF_HEAD_DIM ** -0.5
    qb = q.reshape(B, nb, Q_BLOCK, N_DIFF_HEADS, 2, DIFF_HEAD_DIM).transpose(1, 0, 2, 3, 4, 5)
    q_idx = jnp.arange(S).reshape(nb, Q_BLOCK)
    k_idx = jnp.arange(S)

    def block(args):
        q_blk, qi = args
        s = jnp.einsum('bqhcd,bkhcd->bhcqk', q_blk, k).astype(jnp.float32) * scale
        mask = qi[:, None] >= k_idx[None, :]
        s = jnp.where(mask, s, -jnp.inf)
        pr = jax.nn.softmax(s, axis=-1)
        attn = pr[:, :, 0] - lam * pr[:, :, 1]
        return jnp.einsum('bhqk,bkhe->bqhe', attn.astype(v.dtype), v)

    out = lax.map(block, (qb, q_idx))
    return out.transpose(1, 0, 2, 3, 4).reshape(B, S, N_DIFF_HEADS, V_HEAD_DIM)

def causal_depthwise_conv(x, w, b):
    y = lax.conv_general_dilated(
        x, w[:, None, :].astype(x.dtype), window_strides=(1,),
        padding=[(CONV_WIDTH - 1, 0)],
        dimension_numbers=('NWC', 'WIO', 'NWC'),
        feature_group_count=x.shape[-1])
    return y + b

def rg_lru(x, w_a, b_a, w_x, b_x, lam_param):
    B, S, _ = x.shape
    xb = x.reshape(B, S, N_LRU_BLOCKS, LRU_BLOCK)
    r = jax.nn.sigmoid((jnp.einsum('bsgi,gij->bsgj', xb, w_a).reshape(B, S, RNN_WIDTH) + b_a).astype(jnp.float32))
    i = jax.nn.sigmoid((jnp.einsum('bsgi,gij->bsgj', xb, w_x).reshape(B, S, RNN_WIDTH) + b_x).astype(jnp.float32))
    log_a = -LRU_C * r * jax.nn.softplus(-lam_param.astype(jnp.float32))
    a = jnp.exp(log_a)
    b = jnp.sqrt(-jnp.expm1(2.0 * log_a)) * (i * x.astype(jnp.float32))

    def combine(left, right):
        a_l, b_l = left
        a_r, b_r = right
        return a_l * a_r, a_r * b_l + b_r

    _, h = lax.associative_scan(combine, (a, b), axis=1)
    return h.astype(x.dtype)

def first_inputs(seed: int = 0) -> dict:
    key = jax.random.key(seed)
    ks = jax.random.split(key, 24)
    f32 = jnp.float32
    nrm = lambda k, shape, s: jax.random.normal(k, shape, f32) * s
    gain = lambda k, shape: 1.0 + 0.05 * jax.random.normal(k, shape, f32)
    a0 = jax.random.uniform(ks[15], (DEPTH, RNN_WIDTH), f32, 0.9, 0.999)
    s0 = a0 ** (1.0 / LRU_C)
    lru_lambda = jnp.log(s0) - jnp.log1p(-s0)
    positions = jnp.broadcast_to(jnp.arange(SEQ, dtype=jnp.int32)[None, :], (BATCH, SEQ))
    return {
        'x': nrm(ks[0], (BATCH, SEQ, D_MODEL), 1.0),
        'p': nrm(ks[1], (DEPTH, BATCH, SEQ, PLE_DIM), 1.0),
        'positions': positions,
        'w_in': nrm(ks[2], (DEPTH, D_MODEL, IN_WIDTH), D_MODEL ** -0.5),
        'w_out': nrm(ks[3], (DEPTH, D_MODEL, D_MODEL), D_MODEL ** -0.5),
        'g_mix': gain(ks[4], (DEPTH, D_MODEL)),
        'g_subln': gain(ks[5], (DEPTH, V_HEAD_DIM)),
        'lam_q': nrm(ks[6], (DEPTH, 2, DIFF_HEAD_DIM), 0.1),
        'lam_k': nrm(ks[7], (DEPTH, 2, DIFF_HEAD_DIM), 0.1),
        'conv_w': nrm(ks[8], (DEPTH, CONV_WIDTH, RNN_WIDTH), CONV_WIDTH ** -0.5),
        'conv_b': nrm(ks[9], (DEPTH, RNN_WIDTH), 0.01),
        'w_gate_a': nrm(ks[10], (DEPTH, N_LRU_BLOCKS, LRU_BLOCK, LRU_BLOCK), LRU_BLOCK ** -0.5),
        'b_gate_a': nrm(ks[11], (DEPTH, RNN_WIDTH), 0.01),
        'w_gate_x': nrm(ks[12], (DEPTH, N_LRU_BLOCKS, LRU_BLOCK, LRU_BLOCK), LRU_BLOCK ** -0.5),
        'b_gate_x': nrm(ks[13], (DEPTH, RNN_WIDTH), 0.01),
        'lru_lambda': lru_lambda,
        'g_mlp': gain(ks[14], (DEPTH, D_MODEL)),
        'w_mlp_in': nrm(ks[16], (DEPTH, D_MODEL, D_FF), D_MODEL ** -0.5),
        'w_mlp_out': nrm(ks[17], (DEPTH, D_FF, D_MODEL), D_FF ** -0.5),
        'g_ple': gain(ks[18], (DEPTH, D_MODEL)),
        'w_ple_gate': nrm(ks[19], (DEPTH, D_MODEL, D_MODEL), D_MODEL ** -0.5),
        'w_ple_proj': nrm(ks[20], (DEPTH, PLE_DIM, D_MODEL), PLE_DIM ** -0.5),
        'g_final': gain(ks[21], (D_MODEL,)),
    }

def first_block(x, p, positions, w_in, w_out, g_mix, g_subln, lam_q, lam_k, conv_w, conv_b,
              w_gate_a, b_gate_a, w_gate_x, b_gate_x, lru_lambda, g_mlp, w_mlp_in, w_mlp_out,
              g_ple, w_ple_gate, w_ple_proj, g_final):
    B, S, _ = x.shape
    h = x
    A, R = ATTN_WIDTH, RNN_WIDTH
    for l in range(DEPTH):
        hn = rms_norm(h, g_mix[l])
        proj = hn @ w_in[l]
        q, k, v, xr, gr = jnp.split(proj, [A, 2 * A, 3 * A, 3 * A + R], axis=-1)
        q = partial_rope(q.reshape(B, S, N_DIFF_HEADS, 2, DIFF_HEAD_DIM), positions)
        k = partial_rope(k.reshape(B, S, N_DIFF_HEADS, 2, DIFF_HEAD_DIM), positions)
        v = v.reshape(B, S, N_DIFF_HEADS, V_HEAD_DIM)
        lam_init = 0.8 - 0.6 * math.exp(-0.3 * l)
        dots = jnp.sum(lam_q[l].astype(jnp.float32) * lam_k[l].astype(jnp.float32), axis=-1)
        lam = jnp.exp(dots[0]) - jnp.exp(dots[1]) + lam_init
        o = diff_attention(q, k, v, lam)
        o = (rms_norm(o, g_subln[l]) * (1.0 - lam_init)).reshape(B, S, A)
        xc = causal_depthwise_conv(xr, conv_w[l], conv_b[l])
        y = rg_lru(xc, w_gate_a[l], b_gate_a[l], w_gate_x[l], b_gate_x[l], lru_lambda[l])
        y = y * jax.nn.gelu(gr)
        h = h + jnp.concatenate([o, y], axis=-1) @ w_out[l]
        hm = rms_norm(h, g_mlp[l])
        h = h + jnp.square(jax.nn.relu(hm @ w_mlp_in[l])) @ w_mlp_out[l]
        gate = jax.nn.sigmoid(rms_norm(h, g_ple[l]) @ w_ple_gate[l])
        h = h + gate * (p[l] @ w_ple_proj[l])
    return rms_norm(h, g_final)


GRID_W = 64
CTX_LEN = 256
N_MIXERS = 3
F32 = jnp.float32

M_EXPAND = 2
M_DI = M_EXPAND * D_MODEL
M_HEADDIM = 64
M_NH = M_DI // M_HEADDIM
M_NG = 8
M_HPG = M_NH // M_NG
M_NS = 128
M_CONV_W = 5
M_CHUNK = 128
M_CONV_CH = M_DI + 2 * M_NG * M_NS
M_IN = M_DI + M_CONV_CH + 2 * M_NH

A_HEADDIM = 64
A_NH = D_MODEL // A_HEADDIM
A_NKV = 4
A_REP = A_NH // A_NKV
A_W = A_NH * A_HEADDIM
A_KW = A_NKV * A_HEADDIM
A_IN = 2 * A_W + 2 * A_KW
A_QBLOCK = 128
ROPE_BASE = 10000.0

S_DI = D_MODEL
S_GROUP = 16
S_NG = S_DI // S_GROUP
S_P = 64

N_A = (DEPTH + N_MIXERS - 1) // N_MIXERS
N_B = (DEPTH + N_MIXERS - 2) // N_MIXERS
N_C = DEPTH // N_MIXERS


def rmsnorm(x, w):
    xf = x.astype(F32)
    y = xf * lax.rsqrt(jnp.mean(xf * xf, axis=-1, keepdims=True) + EPS)
    return (y * w.astype(F32)).astype(x.dtype)

def dwconv_centred(u, w, b):
    pad = w.shape[0] // 2
    out = lax.conv_general_dilated(u, w[:, None, :], window_strides=(1,), padding=[(pad, pad)],
                                   dimension_numbers=('NWC', 'WIO', 'NWC'),
                                   feature_group_count=u.shape[-1])
    return out + b

def ssd_scan(xs, dt, a, bm, cm, init_state, need_y=True):
    bsz, L = xs.shape[:2]
    nc = L // M_CHUNK

    def chunks(t):
        return t.astype(F32).reshape((bsz, nc, M_CHUNK) + t.shape[2:])

    xc, dtc, bc, cc = chunks(xs), chunks(dt), chunks(bm), chunks(cm)
    la_cum = jnp.cumsum(dtc * a, axis=2)
    to_end = jnp.exp(la_cum[:, :, -1:] - la_cum) * dtc
    states = jnp.einsum('bcsgn,bcsgr,bcsgrp->bcgrpn', bc, to_end, xc)
    chunk_decay = jnp.exp(la_cum[:, :, -1])

    def step(carry, inp):
        st, dec = inp
        return carry * dec[..., None, None] + st, carry

    final, prev = lax.scan(step, init_state.astype(F32),
                           (jnp.moveaxis(states, 1, 0), jnp.moveaxis(chunk_decay, 1, 0)))
    if not need_y:
        return None, final
    prev = jnp.moveaxis(prev, 0, 1)
    causal = jnp.tril(jnp.ones((M_CHUNK, M_CHUNK), dtype=bool))[:, :, None, None]
    seg = la_cum[:, :, :, None] - la_cum[:, :, None, :]
    decay = jnp.exp(jnp.where(causal, seg, -jnp.inf))
    cb = jnp.einsum('bclgn,bcsgn->bclsg', cc, bc)
    w = cb[..., None] * decay * dtc[:, :, None]
    y_diag = jnp.einsum('bclsgr,bcsgrp->bclgrp', w, xc)
    y_off = jnp.einsum('bclgn,bcgrpn,bclgr->bclgrp', cc, prev, jnp.exp(la_cum))
    return (y_diag + y_off).reshape(xs.shape), final

def mamba_mixer(h_ctx, h_lat, in_w, conv_w, conv_b, a_log, dt_bias, d_skip, norm_w, out_w, ctx_out):
    a = -jnp.exp(a_log.astype(F32)).reshape(2, M_NG, M_HPG)
    dtb = dt_bias.astype(F32).reshape(2, M_NG, M_HPG)

    def project(h):
        bsz, L, _ = h.shape
        z, xbc, dt = jnp.split(h @ in_w, [M_DI, M_DI + M_CONV_CH], axis=-1)
        xbc = jax.nn.silu(dwconv_centred(xbc, conv_w, conv_b))
        xs, bm, cm = jnp.split(xbc, [M_DI, M_DI + M_NG * M_NS], axis=-1)
        xs = xs.reshape(bsz, L, M_NG, M_HPG, M_HEADDIM)
        bm = bm.reshape(bsz, L, M_NG, M_NS)
        cm = cm.reshape(bsz, L, M_NG, M_NS)
        dt = jax.nn.softplus(dt.astype(F32).reshape(bsz, L, 2, M_NG, M_HPG) + dtb)
        return z, xs, bm, cm, dt

    zc, xc, bc, cc, dtc = project(h_ctx)
    zl, xl, bl, cl, dtl = project(h_lat)
    bsz = h_lat.shape[0]
    zero = jnp.zeros((bsz, M_NG, M_HPG, M_HEADDIM, M_NS), F32)
    rev = lambda t: jnp.flip(t, axis=1)
    yc_f, st_f = ssd_scan(xc, dtc[:, :, 0], a[0], bc, cc, zero, ctx_out)
    yl_f, _ = ssd_scan(xl, dtl[:, :, 0], a[0], bl, cl, st_f)
    yc_b, st_b = ssd_scan(rev(xc), rev(dtc[:, :, 1]), a[1], rev(bc), rev(cc), zero, ctx_out)
    yl_b, _ = ssd_scan(rev(xl), rev(dtl[:, :, 1]), a[1], rev(bl), rev(cl), st_b)
    dsk = d_skip.astype(F32).reshape(M_NG, M_HPG, 1)

    def finish(y, xs, z):
        b_, L = xs.shape[:2]
        y = (y + dsk * xs.astype(F32)).reshape(b_, L, M_DI).astype(z.dtype)
        return rmsnorm(y * jax.nn.silu(z), norm_w) @ out_w

    o_lat = finish(yl_f + rev(yl_b), xl, zl)
    o_ctx = finish(yc_f + rev(yc_b), xc, zc) if ctx_out else None
    return o_ctx, o_lat

def axial_rope_tables(L):
    rows = L // GRID_W
    r_idx, c_idx = jnp.meshgrid(jnp.arange(rows), jnp.arange(GRID_W), indexing='ij')
    r_idx = r_idx.reshape(-1).astype(F32)
    c_idx = c_idx.reshape(-1).astype(F32)
    half = A_HEADDIM // 2
    inv = ROPE_BASE ** (-jnp.arange(0, half, 2, dtype=F32) / half)
    ang = jnp.concatenate([r_idx[:, None] * inv, c_idx[:, None] * inv], axis=-1)
    return jnp.cos(ang), jnp.sin(ang)

def apply_rope(t, cos, sin):
    b_, L, h, d = t.shape
    q = d // 4
    tf = t.astype(F32).reshape(b_, L, h, 2, 2, q)
    t1, t2 = tf[..., 0, :], tf[..., 1, :]
    cs = cos.reshape(1, L, 1, 2, q)
    sn = sin.reshape(1, L, 1, 2, q)
    out = jnp.stack([t1 * cs - t2 * sn, t1 * sn + t2 * cs], axis=-2)
    return out.reshape(b_, L, h, d).astype(t.dtype)

def attend(q, k, v):
    bsz, lq = q.shape[:2]
    q = q.reshape(bsz, lq, A_NKV, A_REP, A_HEADDIM)
    s = jnp.einsum('bqgrd,bkgd->bgrqk', q, k).astype(F32) * (A_HEADDIM ** -0.5)
    p = jax.nn.softmax(s, axis=-1).astype(v.dtype)
    o = jnp.einsum('bgrqk,bkgd->bqgrd', p, v)
    return o.reshape(bsz, lq, A_W)

def attn_mixer(h_ctx, h_lat, in_w, q_norm, k_norm, out_w, ctx_out):
    def project(h):
        bsz, L, _ = h.shape
        q, k, v, g = jnp.split(h @ in_w, [A_W, A_W + A_KW, A_W + 2 * A_KW], axis=-1)
        q = rmsnorm(q.reshape(bsz, L, A_NH, A_HEADDIM), q_norm)
        k = rmsnorm(k.reshape(bsz, L, A_NKV, A_HEADDIM), k_norm)
        v = v.reshape(bsz, L, A_NKV, A_HEADDIM)
        return q, k, v, g

    qc, kc, vc, gc = project(h_ctx)
    ql, kl, vl, gl = project(h_lat)
    bsz, L = h_lat.shape[:2]
    cos, sin = axial_rope_tables(L)
    ql = apply_rope(ql, cos, sin)
    kl = apply_rope(kl, cos, sin)
    k_all = jnp.concatenate([kc, kl], axis=1)
    v_all = jnp.concatenate([vc, vl], axis=1)
    nblk = L // A_QBLOCK
    q_blocks = jnp.moveaxis(ql.reshape(bsz, nblk, A_QBLOCK, A_NH, A_HEADDIM), 1, 0)
    ol = lax.map(lambda qb: attend(qb, k_all, v_all), q_blocks)
    ol = jnp.moveaxis(ol, 0, 1).reshape(bsz, L, A_W)
    o_lat = (ol * jax.nn.silu(gl)) @ out_w
    o_ctx = (attend(qc, kc, vc) * jax.nn.silu(gc)) @ out_w if ctx_out else None
    return o_ctx, o_lat

def s5_discretize(lam_re, lam_im, log_step, b_re, b_im):
    lr, li = lam_re.astype(F32), lam_im.astype(F32)
    step = jnp.exp(log_step.astype(F32))[:, None]
    mag = jnp.exp(lr * step)
    abar_re, abar_im = mag * jnp.cos(li * step), mag * jnp.sin(li * step)
    den = lr * lr + li * li
    nr, ni = abar_re - 1.0, abar_im
    coef_re = ((nr * lr + ni * li) / den)[..., None]
    coef_im = ((ni * lr - nr * li) / den)[..., None]
    br, bi = b_re.astype(F32), b_im.astype(F32)
    return abar_re, abar_im, coef_re * br - coef_im * bi, coef_re * bi + coef_im * br

def complex_affine_combine(e1, e2):
    a1r, a1i, b1r, b1i = e1
    a2r, a2i, b2r, b2i = e2
    return (a1r * a2r - a1i * a2i, a1r * a2i + a1i * a2r,
            a2r * b1r - a2i * b1i + b2r, a2r * b1i + a2i * b1r + b2i)

def s5_scan(u, abar_re, abar_im, bbar_re, bbar_im, init_re, init_im):
    L = u.shape[1]
    bu_re = jnp.einsum('blgh,gph->lbgp', u, bbar_re)
    bu_im = jnp.einsum('blgh,gph->lbgp', u, bbar_im)
    bu_re = bu_re.at[0].add(abar_re * init_re - abar_im * init_im)
    bu_im = bu_im.at[0].add(abar_re * init_im + abar_im * init_re)
    a_re = jnp.broadcast_to(abar_re, (L, 1) + abar_re.shape)
    a_im = jnp.broadcast_to(abar_im, (L, 1) + abar_im.shape)
    _, _, x_re, x_im = lax.associative_scan(complex_affine_combine, (a_re, a_im, bu_re, bu_im), axis=0)
    return x_re, x_im

def s5_mixer(h_ctx, h_lat, in_w, lam_re, lam_im, log_step, b_re, b_im, c_re, c_im,
             d_skip, glu_w, glu_b, out_w, ctx_out):
    bsz = h_lat.shape[0]
    disc = [s5_discretize(lam_re[k], lam_im[k], log_step[k], b_re[k], b_im[k]) for k in range(2)]
    cr, ci = c_re.astype(F32), c_im.astype(F32)

    def readout(x_re, x_im, k):
        return jnp.einsum('lbgp,ghp->blgh', x_re, cr[k]) - jnp.einsum('lbgp,ghp->blgh', x_im, ci[k])

    uc, zc = jnp.split(h_ctx @ in_w, 2, axis=-1)
    ul, zl = jnp.split(h_lat @ in_w, 2, axis=-1)
    grp = lambda u: u.astype(F32).reshape(u.shape[0], u.shape[1], S_NG, S_GROUP)
    rev = lambda t: jnp.flip(t, axis=1)
    ucg, ulg = grp(uc), grp(ul)
    zero = jnp.zeros((bsz, S_NG, S_P), F32)
    xr, xi = s5_scan(ucg, *disc[0], zero, zero)
    yc = readout(xr, xi, 0) if ctx_out else None
    xr, xi = s5_scan(ulg, *disc[0], xr[-1], xi[-1])
    yl = readout(xr, xi, 0)
    xr, xi = s5_scan(rev(ucg), *disc[1], zero, zero)
    if ctx_out:
        yc = yc + rev(readout(xr, xi, 1))
    xr, xi = s5_scan(rev(ulg), *disc[1], xr[-1], xi[-1])
    yl = yl + rev(readout(xr, xi, 1))
    dsk = d_skip.astype(F32)

    def finish(y, u, z):
        b_, L = u.shape[:2]
        y = (y.reshape(b_, L, S_DI) + dsk * u.astype(F32)).astype(z.dtype)
        y = jax.nn.gelu(y)
        y = y * jax.nn.sigmoid(y @ glu_w + glu_b)
        return (y * jax.nn.silu(z)) @ out_w

    o_lat = finish(yl, ul, zl)
    o_ctx = finish(yc, uc, zc) if ctx_out else None
    return o_ctx, o_lat

def second_inputs(seed: int = 0) -> dict:
    key = jax.random.key(seed)
    ks = iter(jax.random.split(key, 48))
    nrm = lambda shape, scale: jax.random.normal(next(ks), shape, F32) * scale
    gain = lambda shape: 1.0 + nrm(shape, 0.02)
    inp = {}
    inp['x'] = nrm((BATCH, SEQ, D_MODEL), 1.0)
    inp['c'] = nrm((BATCH, D_MODEL), 1.0)
    inp['ctx'] = nrm((BATCH, CTX_LEN, D_MODEL), 1.0)
    inp['c_ctx'] = nrm((D_MODEL,), 1.0)
    inp['norm_w'] = gain((DEPTH, D_MODEL))
    inp['mod_w'] = nrm((DEPTH, D_MODEL, 3 * D_MODEL), 0.5 * D_MODEL ** -0.5)
    inp['mod_b'] = nrm((DEPTH, 3 * D_MODEL), 0.02)
    inp['final_norm_w'] = gain((D_MODEL,))
    inp['m_in_w'] = nrm((N_A, D_MODEL, M_IN), D_MODEL ** -0.5)
    inp['m_conv_w'] = nrm((N_A, M_CONV_W, M_CONV_CH), M_CONV_W ** -0.5)
    inp['m_conv_b'] = nrm((N_A, M_CONV_CH), 0.02)
    inp['m_a_log'] = jnp.log(jax.random.uniform(next(ks), (N_A, 2, M_NH), F32, 1.0, 16.0))
    dt0 = jnp.exp(jax.random.uniform(next(ks), (N_A, 2, M_NH), F32, math.log(1e-3), math.log(1e-1)))
    inp['m_dt_bias'] = dt0 + jnp.log(-jnp.expm1(-dt0))
    inp['m_d'] = 1.0 + nrm((N_A, M_NH), 0.1)
    inp['m_norm_w'] = gain((N_A, M_DI))
    inp['m_out_w'] = nrm((N_A, M_DI, D_MODEL), M_DI ** -0.5)
    inp['a_in_w'] = nrm((N_B, D_MODEL, A_IN), D_MODEL ** -0.5)
    inp['a_q_norm'] = gain((N_B, A_HEADDIM))
    inp['a_k_norm'] = gain((N_B, A_HEADDIM))
    inp['a_out_w'] = nrm((N_B, A_W, D_MODEL), A_W ** -0.5)
    inp['s_in_w'] = nrm((N_C, D_MODEL, 2 * S_DI), D_MODEL ** -0.5)
    inp['s_lambda_re'] = -0.5 + nrm((N_C, 2, S_NG, S_P), 0.01)
    inp['s_lambda_im'] = math.pi * jnp.arange(S_P, dtype=F32) + nrm((N_C, 2, S_NG, S_P), 0.01)
    inp['s_log_step'] = jax.random.uniform(next(ks), (N_C, 2, S_NG), F32, math.log(1e-3), math.log(1e-1))
    inp['s_b_re'] = nrm((N_C, 2, S_NG, S_P, S_GROUP), (2 * S_GROUP) ** -0.5)
    inp['s_b_im'] = nrm((N_C, 2, S_NG, S_P, S_GROUP), (2 * S_GROUP) ** -0.5)
    inp['s_c_re'] = nrm((N_C, 2, S_NG, S_GROUP, S_P), S_P ** -0.5)
    inp['s_c_im'] = nrm((N_C, 2, S_NG, S_GROUP, S_P), S_P ** -0.5)
    inp['s_d'] = nrm((N_C, S_DI), 1.0)
    inp['s_glu_w'] = nrm((N_C, S_DI, S_DI), S_DI ** -0.5)
    inp['s_glu_b'] = nrm((N_C, S_DI), 0.02)
    inp['s_out_w'] = nrm((N_C, S_DI, D_MODEL), S_DI ** -0.5)
    return inp

def second_block(x, c, ctx, c_ctx, norm_w, mod_w, mod_b, final_norm_w,
              m_in_w, m_conv_w, m_conv_b, m_a_log, m_dt_bias, m_d, m_norm_w, m_out_w,
              a_in_w, a_q_norm, a_k_norm, a_out_w,
              s_in_w, s_lambda_re, s_lambda_im, s_log_step, s_b_re, s_b_im, s_c_re, s_c_im,
              s_d, s_glu_w, s_glu_b, s_out_w):
    h_lat, h_ctx = x, ctx
    sc, scc = jax.nn.silu(c), jax.nn.silu(c_ctx)
    for i in range(DEPTH):
        kind, j = i % N_MIXERS, i // N_MIXERS
        ctx_out = i < DEPTH - 1
        sh, scl, gt = jnp.split(sc @ mod_w[i] + mod_b[i], 3, axis=-1)
        shc, sclc, gtc = jnp.split(scc @ mod_w[i] + mod_b[i], 3, axis=-1)
        in_lat = rmsnorm(h_lat, norm_w[i]) * (1.0 + scl[:, None]) + sh[:, None]
        in_ctx = rmsnorm(h_ctx, norm_w[i]) * (1.0 + sclc) + shc
        if kind == 0:
            o_ctx, o_lat = mamba_mixer(in_ctx, in_lat, m_in_w[j], m_conv_w[j], m_conv_b[j], m_a_log[j],
                                       m_dt_bias[j], m_d[j], m_norm_w[j], m_out_w[j], ctx_out)
        elif kind == 1:
            o_ctx, o_lat = attn_mixer(in_ctx, in_lat, a_in_w[j], a_q_norm[j], a_k_norm[j], a_out_w[j], ctx_out)
        else:
            o_ctx, o_lat = s5_mixer(in_ctx, in_lat, s_in_w[j], s_lambda_re[j], s_lambda_im[j], s_log_step[j],
                                    s_b_re[j], s_b_im[j], s_c_re[j], s_c_im[j], s_d[j], s_glu_w[j],
                                    s_glu_b[j], s_out_w[j], ctx_out)
        h_lat = h_lat + gt[:, None] * o_lat
        if ctx_out:
            h_ctx = h_ctx + gtc * o_ctx
    return rmsnorm(h_lat, final_norm_w)


def setup_inputs(seed=0):
    out = dict(first_inputs(seed))
    for name, value in second_inputs(seed + 1).items():
        if name != "x":
            out[name + "_2"] = value
    return out


def reference(
    x, p, positions, w_in, w_out, g_mix, g_subln, lam_q, lam_k, conv_w, conv_b, w_gate_a,
    b_gate_a, w_gate_x, b_gate_x, lru_lambda, g_mlp, w_mlp_in, w_mlp_out, g_ple, w_ple_gate,
    w_ple_proj, g_final, c_2, ctx_2, c_ctx_2, norm_w_2, mod_w_2, mod_b_2, final_norm_w_2,
    m_in_w_2, m_conv_w_2, m_conv_b_2, m_a_log_2, m_dt_bias_2, m_d_2, m_norm_w_2, m_out_w_2,
    a_in_w_2, a_q_norm_2, a_k_norm_2, a_out_w_2, s_in_w_2, s_lambda_re_2, s_lambda_im_2,
    s_log_step_2, s_b_re_2, s_b_im_2, s_c_re_2, s_c_im_2, s_d_2, s_glu_w_2, s_glu_b_2,
    s_out_w_2,
):
    x = first_block(
        x, p, positions, w_in, w_out, g_mix, g_subln, lam_q, lam_k, conv_w, conv_b, w_gate_a,
        b_gate_a, w_gate_x, b_gate_x, lru_lambda, g_mlp, w_mlp_in, w_mlp_out, g_ple, w_ple_gate,
        w_ple_proj, g_final,
    )
    return second_block(
        x, c_2, ctx_2, c_ctx_2, norm_w_2, mod_w_2, mod_b_2, final_norm_w_2, m_in_w_2,
        m_conv_w_2, m_conv_b_2, m_a_log_2, m_dt_bias_2, m_d_2, m_norm_w_2, m_out_w_2, a_in_w_2,
        a_q_norm_2, a_k_norm_2, a_out_w_2, s_in_w_2, s_lambda_re_2, s_lambda_im_2, s_log_step_2,
        s_b_re_2, s_b_im_2, s_c_re_2, s_c_im_2, s_d_2, s_glu_w_2, s_glu_b_2, s_out_w_2,
    )


_drawn_inputs = setup_inputs


def setup_inputs(seed=0):
    import zlib

    import numpy as np

    out = dict(_drawn_inputs(seed))
    spreads = {}
    factors = {'lam_q': 4.287,
     'b_gate_a': 8.0,
     'b_gate_x': 8.0,
     'g_ple': 7.429,
     'ctx_2': 4.517,
     'norm_w_2': 6.307,
     'final_norm_w_2': 23.142,
     'm_conv_b_2': 7.127,
     'm_d_2': 200.0,
     'm_norm_w_2': 8.0,
     'a_q_norm_2': 8.0,
     'a_k_norm_2': 8.0}
    for name, (base, spread) in spreads.items():
        noise = np.random.default_rng([zlib.crc32(name.encode()), seed]).standard_normal(out[name].shape)
        drawn = base * np.exp(spread * noise) if base else spread * noise
        out[name] = jnp.asarray(drawn.astype(out[name].dtype))
    for name, factor in factors.items():
        out[name] = (out[name] * factor).astype(out[name].dtype)
    return out
```

```python
import math
from contextlib import ExitStack

import numpy as np
import concourse.bass as bass
from concourse import mybir

F32 = mybir.dt.float32
F32R = mybir.dt.float32r
BF16 = mybir.dt.bfloat16
I32 = mybir.dt.int32
ALU = mybir.AluOpType
ACT = mybir.ActivationFunctionType
AX = mybir.AxisListType

P = 128
DEPTH = 2
D = 1024
KB = D // P
S = 512
TILE = 2048
TM = 256
EPS = 1e-6

HEADS = 4
ROT = 16
DFF = 4096
CHUNKS = DFF // D
MIX_TILES = 10
MOD_IN_LAYER = 11
LAYER_TILES = MIX_TILES + MOD_IN_LAYER + 4 + 8 * CHUNKS + 1 + 4
C_GMIX, C_GMLP, C_GPLE, C_GSUB, C_CW, C_CB, C_BA, C_BX, C_LRU, C_LQ, C_LK, C_LI, C_1LI = (
    0, 8, 16, 24, 25, 41, 45, 49, 53, 57, 59, 61, 62)
NLP = 63
XR, GR, Q0, K0, V0 = 0, 4, 8, 12, 16
CTX = 256
T = CTX + S
HALF = T // 2
GROUPS, HPG, HD, NS = 8, 4, 64, 128
MDI = GROUPS * HPG * HD
CHUNK = 128
NC = T // CHUNK
CTX_CHUNKS = CTX // CHUNK
TAPS, CW = 5, T + 2
KVH, REP = 4, 4
T_LAYERS = DEPTH * LAYER_TILES
T_MOD22, T_MOD23, T_DT, T_XS0, T_BC0, T_G0 = (T_LAYERS + n for n in range(6))
G_TILES = 4
T_ATT = T_G0 + G_TILES * GROUPS - 2
C2_GF, C2_NW, C2_MB, C2_FN, C2_CP, C2_MN, C2_DTB, C2_QN, C2_KN = 0, 8, 24, 72, 80, 272, 288, 289, 290
NP2 = 291
K_G, K_NB, K_EXLA, K_TE, K_DEC = (2 * NC * n for n in range(5))
TWO_PI_1, TWO_PI_2 = 6.28125, 0.0019350051879882812
TWO_PI_3 = 2 * math.pi - TWO_PI_1 - TWO_PI_2
MAGIC = 12582912.0


def sbuf_map(nc, top):
    base = 16 * 1024 + 128
    def at(name, kib, shape, dt=F32):
        return nc.alloc_sbuf_tensor_at(name, shape, dt, offset=base + int(kib * 1024))
    return at


class Chain:

    def __init__(self, eng, sem, base=0):
        self.eng, self.sem, self.base, self.n = eng, sem, base, 0

    def __call__(self, ins):
        self.n += 1
        ins.then_inc(self.sem, 1)
        self.eng.wait_ge(self.sem, self.base + self.n)


def build(nc, io, stage=2):
    NT = io["wstream"].shape[0]
    at = sbuf_map(nc, None)

    wraw = at("wraw", 0, [P, 2, TILE])
    whi = at("whi", 16, [P, 2, TILE], F32R)
    wlo = at("wlo", 32, [P, 2, TILE], F32R)
    h = at("h", 48, [P, KB, S])
    uhi = at("uhi", 64, [P, KB, S], F32R)
    ulo = at("ulo", 80, [P, KB, S], F32R)
    proj = at("proj", 96, [P, 20, S])
    hidhi = at("hidhi", 96, [P, KB, S], F32R)
    hidlo = at("hidlo", 112, [P, KB, S], F32R)
    phi = at("phi", 128, [P, 2, S], F32R)
    plo = at("plo", 132, [P, 2, S], F32R)
    oyhi = at("oyhi", 136, [P, KB, S], F32R)
    oylo = at("oylo", 152, [P, KB, S], F32R)
    pp = at("pp", 168, [P, KB, S])
    pT = at("pT", 184, [P, 2, S])
    gw = at("gw", 188, [P, 8, P])
    acc2 = at("acc2", 192, [P, 2, S])
    rstd = at("rstd", 196, [P, S])
    ropeC = at("ropeC", 198, [P, S])
    ropeS = at("ropeS", 200, [P, S])
    ident = at("ident", 202, [P, P])
    rperm = at("rperm", 202.5, [P, P])
    ones = at("ones", 203, [P, P])
    identb = at("identb", 203.5, [P, P], BF16)
    maskb = at("maskb", 203.75, [P, P], BF16)
    lpall = at("lpall", 204, [P, DEPTH, NLP])
    lp = at("lp", 204.5, [P, NLP])
    small = at("small", 204.75, [P, 64])
    modsb = at("modsb", 205, [P, 48, 2])
    cvec = at("cvec", 205.375, [P, KB, 2])
    cvhi = at("cvhi", 205.5, [P, 2 * KB + P - 2], F32R)
    cvlo = at("cvlo", 206.125, [P, 2 * KB + P - 2], F32R)
    misc = at("misc", 206.75, [P, 16])
    modrow = at("modrow", 206.8125, [2, TM])
    xc = at("xc", 136, [P, 4, S])
    gi = at("gi", 152, [P, 4, S])
    asq = at("asq", 160, [P, 4, S])
    ga = at("ga", 168, [P, 4, S])
    gt = at("gt", 176, [P, 4, S])
    vtok = at("vtok", 64, [P, 4, S])
    pexp = at("pexp", 72, [P, 2, 2, S])
    patt = at("patt", 80, [P, 2, S])
    pattT = at("pattT", 84, [P, 2, S])
    osb = at("osb", 88, [P, HEADS, S])
    osq = at("osq", 128, [P, HEADS, S])
    orst = at("orst", 136, [P, HEADS, S])
    rtmp = at("rtmp", 192, [P, 2, S])
    sqmlp = at("sqmlp", 168, [P, 2, S])
    sqple = at("sqple", 136, [P, 2, S])
    hm = [at(f"hm{i}", 168 + 4 * i, [P, 2, S]) for i in range(2)]
    hsq = [at(f"hsq{i}", 176 + 4 * i, [P, 2, S]) for i in range(2)]
    gm = [at(f"gm{i}", 96 + 4 * i, [P, 2, S]) for i in range(2)]
    gth = [at(f"gth{i}", 104 + 4 * i, [P, 2, S]) for i in range(2)]
    posi = at("posi", 96, [P, S], I32)
    maskf = at("maskf", 104, [P, P])
    angt = [at(f"angt{i}", 98 + 2 * i, [P, S]) for i in range(3)]

    inhi = at("inhi", 48, [P, KB, T], F32R)
    inlo = at("inlo", 72, [P, KB, T], F32R)
    oacc = at("oacc", 96, [P, KB, T])
    hres = at("hres", 144, [P, KB, T])
    sqb = at("sqb", 120, [P, KB, T])
    tin = at("tin", 168, [P, 2, T])
    masktmp = at("masktmp", 174, [P, 2, P])
    convd = at("convd", 120, [P, 4, 772])
    ck = at("ck", 132.125, [P, T])
    raw = [at(f"raw{i}", 135.125 + 3.125 * i, [P, 776]) for i in range(2)]
    zs = at("zs", 141.375, [P, 2, T])
    uh = at("uh", 147.375, [P, 2, T], F32R)
    ul = at("ul", 153.375, [P, 2, T], F32R)
    ast = at("ast", 159.375, [P, 10, 256])
    xcb = at("xcb", 169.375, [P, NC, 384])
    sqz = at("sqz", 169.375, [P, 2, T])
    ebuf = at("ebuf", 178.375, [P, 2, HPG, P])
    btok = at("btok", 178.375, [P, NC, NS])
    xte = at("xte", 182.375, [P, 2, HPG, HD])
    wdec = at("wdec", 184.375, [P, HPG, P])
    offs = at("offs", 186.375, [P, 2, HPG, HD])
    stmp = at("stmp", 188.375, [P, HPG, HD])
    acc = at("acc", 189.375, [P, T])
    rs2 = at("rs2", 186.375, [P, T])
    tab = at("tab", 192.375, [P, 10 * NC, 32])
    triF = at("triF", 199.875, [P, P])
    triB = at("triB", 200.375, [P, P])
    drow = at("drow", 200.875, [P, 32])
    modv = [at(f"modv{i}", 201 + 0.1875 * i, [P, 24, 2]) for i in range(2)]
    modA = at("modA", 201.375, [P, KB, 2])
    arow = at("arow", 201.5, [P, 64])
    mask2 = at("mask2", 202.5, [P, 2, P], BF16)
    p2 = at("p2", 203.75, [P, NP2])
    tabg = at("tabg", 205.5, [P, 10 * NC, HPG])
    cpg = at("cpg", 206.4375, [P, 24])
    mng = at("mng", 206.5625, [P, 2])
    dtw = [at(f"dtw{i}", 174 + 1.5 * i, [P, NC, 64]) for i in range(8)]
    dtT = at("dtT", 171, [64, T])
    qb_ = at("qb", 120, [P, KB, S])
    kf = at("kf", 136, [P, 2, T])
    vf = at("vf", 142, [P, 2, T])
    gs = at("gs", 148, [P, KB, S])
    qsq = at("qsq", 164, [P, KB, S])
    ksq = at("ksq", 180, [P, 2, T])
    cosT = at("cosT", 190, [P, S])
    sinT = at("sinT", 192, [P, S])
    rt2 = at("rt2", 194, [P, 2, S])
    bones = at("bones", 198, [P, P])
    perm2 = at("perm2", 198.5, [P, P])
    ohi = at("ohi", 48, [P, KB, S], F32R)
    olo = at("olo", 64, [P, KB, S], F32R)
    vtok2 = at("vtok2", 80, [P, NC, 256])
    vaug = at("vaug", 86, [P, NC, P])
    kk = at("kk", 89, [64, T])
    nmx = at("nmx", 92, [P, 2, 4, 2])
    nm4 = at("nm4", 92.125, [P, 2, 4])
    K1 = [at(f"K1{i}", 164 + 6 * i, [P, T], F32R) for i in range(2)]
    K2 = [at(f"K2{i}", 167 + 6 * i, [P, T], F32R) for i in range(2)]
    Q1 = [at(f"Q1{i}", 176 + 4 * i, [P, S], F32R) for i in range(2)]
    Q2 = [at(f"Q2{i}", 178 + 4 * i, [P, S], F32R) for i in range(2)]
    qq = at("qq", 92.5, [64, S])
    pT2 = at("pT2", 184, [P, NC, S])
    osum = at("osum", 196, [P, S])
    hback = at("hback", 120, [P, KB, T])
    sq4 = at("sq4", 144, [P, KB, T])
    rs5 = at("rs5", 190, [P, S])
    hfin = at("hfin", 120, [P, KB, S])

    hspill = nc.dram_tensor("hspill", (P, KB, T), F32, kind="Internal").ap() if stage > 1 else None

    ps = nc.alloc_psum_tensor("ps", [P, 8, 512], F32)
    TWO = lambda s: ps[:, 2 * s:2 * s + 2, :]

    def sem(name):
        return nc.alloc_semaphore(name)

    wfree, wsplit, tile_done, pool_go, wraw_read = (sem(n) for n in (
        "wfree", "wsplit", "tile_done", "pool_go", "wraw_read"))
    wland = [sem(f"wland{i}") for i in range(2)]
    cst = sem("cst_loaded")
    init_a, init_d = sem("init_a"), sem("init_d")
    layer_go = sem("layer_go")
    lw = [sem(f"layer_weights{i}") for i in range(2)]
    LN = ["lp_copied", "lsp", "lsa", "dots_r", "lam_r", "uhi_r", "ulo_r", "sq_r", "acc_r", "ssq_r", "sqrt_r", "rstd_r",
          "h_r", "d_step", "a_step", "mod_row", "mod_T", "mod_ev", "proj_r", "xc_r", "gate_ps", "gate_t", "lru_a",
          "lru_d", "rope_ps", "rope_rd", "rope_r", "v_ps", "v_r", "qk_r", "nmax_r", "exp_r", "att_r", "attT_r",
          "attTc", "pv_r", "o_r", "oss_r", "orst_r", "on_r", "ohi_r", "oy_r", "yhi_r", "m_r", "sqh_r", "hlo_r",
          "pp_ps", "phi_r", "p_r", "pp_r", "g_r", "gth_r", "layer_done"]
    Ls = {n: sem("L_" + n) for n in LN}
    lo_num, hi_num = Ls[LN[0]].num, Ls[LN[-1]].num
    assert hi_num - lo_num == len(LN) - 1
    out_s = sem("out_stored")
    ld2, ldc, spill, ld3, ldm = sem("params2_loaded"), sem("ctx_loaded"), sem("residual_dma"), sem("att_tables"), sem("d_loaded")
    a2, d2 = sem("act_step2"), sem("dve_step2")
    m_row, m_T, m_ev = sem("mod2_row"), sem("mod2_T"), sem("mod2_ev")
    n_sq, n_ss, n_rt, n_rs, n_x = sem("norm_squares"), sem("norm_sums"), sem("norm_root"), sem("norm_rstd"), sem("norm_x")
    in_t, in_hi, in_lo = sem("in_value"), sem("in_hi"), sem("in_lo")
    dt_p, dt_a, dt_d = sem("dt_pe"), sem("dt_act"), sem("dt_dve")
    blk_ps = sem("block_sums")
    z_t, z_rd, x_rd, o_rd = sem("z_tanh"), sem("z_read"), sem("conv_in_read"), sem("out_read")
    cv_c, cv_t, cv_r, pads = sem("conv_done"), sem("conv_tanh"), sem("conv_silu"), sem("pads_zero")
    pre_ps, tok_r, ck_r, tabg_r = sem("tokens_turned"), sem("tokens_held"), sem("C_held"), sem("group_tables")
    xte_r, st_ps, sc_r, scan_r = sem("x_to_end"), sem("chunk_states"), sem("states_held"), sem("states_scanned")
    la_ps, ex_r, off_ps, offs_r = sem("log_decay"), sem("decay"), sem("off_sums"), sem("off_held")
    W_r, y_ps, y_rd = sem("weights_ready"), sem("y_sums"), sem("y_read")
    uh_r, u_r, sqz_r, acc_r2 = sem("u_hi"), sem("u_ready"), sem("y_squares"), sem("y_squares_added")
    a_rd, g_t, g_rd, ln_r, rsh_r = sem("kvq_read"), sem("g_tanh"), sem("g_read"), sem("head_log"), sem("head_rstd")
    qn_r, rp_ps, rp_rd, rp_r = sem("qk_normed"), sem("rope2_sums"), sem("rope2_read"), sem("rope2_done")
    ssh, vt_ps, vt_r = sem("head_sums"), sem("v_turned"), sem("v_held")
    k_hi, k_lo, q_hi, q_lo, va_r = sem("k_hi"), sem("k_lo"), sem("q_hi"), sem("q_lo"), sem("v_of_head")
    s_ps, mx_r, mx_ps, mxh_r, mxl_r = sem("scores"), sem("max_ready"), sem("max_row"), sem("max_hi"), sem("max_lo")
    sT_ps, p_r2, o_ps, o_ev, oy2 = sem("scoresT"), sem("probs"), sem("head_out"), sem("head_out_read"), sem("o_gated")
    oh_r, ol_r, hf_r, fin = sem("o_hi"), sem("o_lo"), sem("final_h"), sem("final_out")

    g_step, h_step = sem("group_step"), sem("heads_step")
    act_go = sem("act_go")
    mxf_r = sem("head_max_ready")
    SLOT_F = {0: 0, 1: 1, 2: 2, 3: 3, 4: 4}
    SLOT_B = {0: 5, 1: 6, 3: 7, 4: 8, 5: 9}
    PREV_F = [None, 0, 1, 2, 3, 4]
    PREV_B = [SLOT_B[1], None, SLOT_B[3], SLOT_B[4], SLOT_B[5], SLOT_B[0]]

    CREDIT = 2

    def first_tile(l):
        return l * LAYER_TILES

    block = nc.Block()
    ctx = ExitStack()
    ctx.enter_context(block)

    @block.sync
    def _(sp):
        for dst, name in ((h, "x"), (cvec, "cvec"), (lpall, "lparams")):
            sp.dma_start(dst[:, :, :], io[name]).then_inc(cst, 16)
        for dst, a, b in ((ident, 0, 128), (rperm, 128, 256), (misc, 256, 272), (maskf, 272, 400)):
            sp.dma_start(dst[:, :], io["consts"][:, a:b]).then_inc(cst, 16)
        sp.dma_start(posi[:, :], io["positions"].partition_broadcast(P)).then_inc(cst, 16)
        with sp.Fori(0, NT // 2) as i:
            for s in range(2):
                sp.wait_ge(wfree, i * 2 + (s + 1))
                sp.dma_start(wraw[:, s, :], io["wstream"][bass.ds(i * 2 + s, 1), :, :].rearrange("a p n -> p (a n)")
                             ).then_inc(wland[s], 16)
        if stage == 1:
            sp.wait_ge(layer_go, DEPTH)
            sp.dma_start(io["out"], h[:, :, :]).then_inc(out_s, 16)
            sp.wait_ge(out_s, 16)
        else:
            sp.wait_ge(fin, KB)
            sp.dma_start(io["out"], hfin[:, :, :]).then_inc(out_s, 16)
            sp.wait_ge(out_s, 16)

    @block.gpsimd
    def _(pool):
        pool.sem_inc(wfree, CREDIT)
        with pool.Fori(0, NT // 2) as i:
            for s in range(2):
                pool.wait_ge(wland[s], i * 16 + 16)
                pool.wait_ge(tile_done, i * 2 + (s + 1))
                pool.sem_inc(pool_go, 1)
                pool.tensor_scalar(whi[:, s, :], wraw[:, s, :], 1.0, 0.0, ALU.mult, ALU.add).then_inc(wraw_read, 1)
                pool.wait_ge(wraw_read, i * 2 + (s + 1))
                pool.tensor_tensor(wlo[:, s, :], wraw[:, s, :], whi[:, s, :].bitcast(F32), ALU.subtract
                                   ).then_inc(wsplit, 1)
                pool.wait_ge(wsplit, i * 2 + (s + 1))
                pool.sem_inc(wfree, 1)

    T_OUT, T_MOD10, T_MLP = 20, 24, 25
    T_PP = T_MLP + 8 * CHUNKS
    T_GATE = T_PP + 1

    @block.tensor
    def _(pe):
        L = Ls
        pe.sem_inc(tile_done, CREDIT)
        pe.wait_ge(init_d, INIT_D)
        pe.wait_ge(init_a, INIT_A)

        def tile_wait(l, k):
            pe.wait_ge(wsplit, l * LAYER_TILES + (k + 1))

        released = [None, None]

        def banks_wait(s, read):
            if released[s]:
                pe.wait_ge(L[released[s][0]], released[s][1])
            released[s] = read

        def tile(l, k, bank, hi, lo, read, korder=range(KB), kwait=None):
            w = k % 2
            tile_wait(l, k)
            banks_wait(bank, read)
            for m in range(2):
                n = 0
                for kb in korder:
                    if m == 0 and kwait:
                        kwait(kb)
                    c = kb * TM + m * P
                    for a, b in ((whi, hi), (wlo, hi), (whi, lo)):
                        mm = pe.matmul(ps[:, 2 * bank + m, :], a[:, w, c:c + P], b[:, kb, :],
                                       start=(n == 0), stop=(n == 3 * KB - 1))
                        n += 1
            mm.then_inc(tile_done, 1)

        def norm_sum(n):
            pe.wait_ge(L["acc_r"], 3 * n)
            if n > 1:
                pe.wait_ge(L["sqrt_r"], n - 1)
            for m in range(2):
                mm = pe.matmul(ps[:, 4, :], ones[:, :], acc2[:, m, :], start=(m == 0), stop=(m == 1))
            mm.then_inc(L["ssq_r"], 1)

        def mod_tile(l, k, j):
            w = k % 2
            tile_wait(l, k)
            if j:
                pe.wait_ge(L["mod_ev"], j)
            n = 0
            for kb in range(KB):
                for a, b in ((cvhi, whi), (cvlo, whi), (cvhi, wlo)):
                    mm = pe.matmul(ps[:, 5, 0:TM], a[:, 2 * kb:2 * kb + P],
                                   b[:, w, kb * TM:(kb + 1) * TM], start=(n == 0), stop=(n == 3 * KB - 1))
                    n += 1
            mm.then_inc(tile_done, 1)

        def mod_turn(j):
            pe.wait_ge(L["mod_row"], j + 1)
            for m in range(2):
                mm = pe.transpose(ps[:, 5, 2 * m:2 * m + 2], modrow[:, m * P:(m + 1) * P], ident[0:2, 0:2])
            mm.then_inc(L["mod_T"], 1)

        with pe.Fori(0, DEPTH) as l:
            released[:] = [None, None]
            pe.wait_ge(L["lsp"], 1)
            pe.matmul(ps[:, 6, 0:2], ones[:, :], small[:, 0:2], start=True, stop=True).then_inc(L["dots_r"], 1)
            norm_sum(1)

            def pair(j):
                tile(l, 2 * j, j % 2, uhi, ulo, ("proj_r", j + 1),
                     kwait=(lambda kb: pe.wait_ge(L["ulo_r"], kb + 1)) if j == 0 else None)
                if j:
                    mod_turn(j - 1)
                mod_tile(l, 2 * j + 1, j)

            for j in range(4):
                pair(j)
            pe.wait_ge(L["xc_r"], 4)
            pe.wait_ge(lw[0], l * 16 + 16)
            for n in range(8):
                if n >= 2:
                    pe.wait_ge(L["gate_t"], n - 1)
                elif n == 0:
                    pe.wait_ge(L["lam_r"], 1)
                pe.matmul(ps[:, 6 + n % 2, :], gw[:, n, :], xc[:, n % 4, :], start=True, stop=True
                          ).then_inc(L["gate_ps"], 1)
            for j in range(4, 8):
                pair(j)

            rope_n = [0]

            def rope(m):
                n = rope_n[0]
                rope_n[0] += 1
                pe.wait_ge(L["rope_rd"], n - 1) if n >= 2 else pe.wait_ge(L["gate_t"], 8)
                pe.wait_ge(L["proj_r"], m // 2 + 1)
                pe.matmul(ps[:, 6 + n % 2, :], rperm[:, :], proj[:, m, :], start=True, stop=True
                          ).then_inc(L["rope_ps"], 1)

            for m in range(Q0, Q0 + 4):
                rope(m)
            for j in range(8, 10):
                pair(j)
            mod_turn(9)
            for m in range(K0, K0 + 4):
                rope(m)
            for t in range(4):
                pe.wait_ge(L["proj_r"], 10)
                for hd in range(HEADS):
                    mm = pe.transpose(ps[:, t, hd * P:(hd + 1) * P], proj[:, V0 + hd, t * P:(t + 1) * P], ident[:, :])
                mm.then_inc(L["v_ps"], 1)
            units = [(hd, qb) for hd in range(HEADS) for qb in range(4)]

            def scores(n):
                hd, qb = units[n]
                p, w = n % 2, (qb + 1) * P
                if n < 2:
                    pe.wait_ge(L["v_r"], 2 * n + 2)
                else:
                    pe.wait_ge(L["exp_r"], 2 * (n - 1))
                pe.wait_ge(L["rope_r"], 8)
                for c in range(2):
                    q = proj[64 * c:64 * c + 64, Q0 + hd, qb * P:(qb + 1) * P]
                    pe.matmul(ps[:, 2 * p + c, 0:w], q, proj[64 * c:64 * c + 64, K0 + hd, 0:w], start=True, stop=False)
                    mm = pe.matmul(ps[:, 2 * p + c, qb * P:w], identb[:, :], maskb[:, :], start=False, stop=True)
                mm.then_inc(L["qk_r"], 1)

            def turn(n):
                hd, qb = units[n]
                pe.wait_ge(L["att_r"], n + 1)
                pe.wait_ge(L["attTc"], n - 1) if n >= 2 else pe.wait_ge(L["rope_rd"], 8)
                for kb in range(qb + 1):
                    mm = pe.transpose(ps[:, 6 + n % 2, kb * P:(kb + 1) * P], patt[:, n % 2, kb * P:(kb + 1) * P],
                                      ident[:, :])
                mm.then_inc(L["attT_r"], 1)

            def values(n):
                hd, qb = units[n]
                pe.wait_ge(L["attTc"], n + 1)
                if qb == 0:
                    if hd >= 2:
                        pe.wait_ge(L["o_r"], 2 * (hd - 1))
                    elif hd == 0:
                        pe.wait_ge(L["sqrt_r"], 1)
                    else:
                        pe.wait_ge(L["mod_ev"], 10)
                for kb in range(qb + 1):
                    mm = pe.matmul(ps[:, 4 + hd % 2, qb * P:(qb + 1) * P], vtok[:, kb, hd * P:(hd + 1) * P],
                                   pattT[:, n % 2, kb * P:(kb + 1) * P], start=(kb == 0), stop=(kb == qb))
                mm.then_inc(L["pv_r"], 1)

            N = len(units)
            scores(0)
            for n in range(N):
                if n + 1 < N:
                    scores(n + 1)
                turn(n)
                if n:
                    values(n - 1)
            values(N - 1)
            for hd in range(HEADS):
                pe.wait_ge(L["o_r"], 2 * (hd + 1))
                if hd == 0:
                    pe.wait_ge(L["exp_r"], 2 * N)
                pe.matmul(ps[:, hd, :], ones[:, :], osq[:, hd, :], start=True, stop=True).then_inc(L["oss_r"], 1)
            for j in range(4):
                if j == 0:
                    released[:] = [("orst_r", 1)] * 2

                def owait(kb):
                    if kb == 4:
                        pe.wait_ge(L["oy_r"], 1)
                    if kb < 4:
                        pe.wait_ge(L["oy_r"], kb + 2)
                tile(l, T_OUT + j, j % 2, oyhi, oylo, ("h_r", j + 1), korder=[4, 5, 6, 7, 0, 1, 2, 3], kwait=owait if j == 0 else None)
            mod_tile(l, T_MOD10, 10)
            norm_sum(2)
            mod_turn(10)
            b = 0
            for c in range(CHUNKS):
                for j in range(4):
                    tile(l, T_MLP + 8 * c + j, b % 2, uhi, ulo, ("m_r", 4 * c + j + 1),
                         kwait=(lambda kb: pe.wait_ge(L["ulo_r"], KB + kb + 1)) if c == 0 and j == 0 else None)
                    b += 1
                for j in range(4):
                    tile(l, T_MLP + 8 * c + 4 + j, b % 2, hidhi, hidlo, ("h_r", 4 + 4 * c + j + 1),
                         kwait=(lambda kb: pe.wait_ge(L["hlo_r"], 4 * c + kb // 2 + 1)) if j == 0 else None)
                    b += 1
            tile_wait(l, T_PP)
            pe.wait_ge(L["p_r"], 1)
            for g in range(4):
                banks_wait(g % 2, ("pp_r", g + 1))
                for m in range(2):
                    n = 0
                    for kb in range(2):
                        c = kb * D + (2 * g + m) * P
                        for x, y in ((whi, phi), (wlo, phi), (whi, plo)):
                            mm = pe.matmul(ps[:, 2 * (g % 2) + m, :], x[:, T_PP % 2, c:c + P], y[:, kb, :],
                                           start=(n == 0), stop=(n == 5))
                            n += 1
                mm.then_inc(L["pp_ps"] if g < 3 else tile_done, 1)
            norm_sum(3)
            for j in range(4):
                tile(l, T_GATE + j, j % 2, uhi, ulo, ("g_r", j + 1),
                     kwait=(lambda kb: pe.wait_ge(L["ulo_r"], 2 * KB + kb + 1)) if j == 0 else None)
            pe.wait_ge(tile_done, l * LAYER_TILES + (LAYER_TILES + CREDIT))
            pe.sem_inc(L["layer_done"], 1)
            pe.wait_ge(layer_go, l + 1)

        if stage == 1:
            return

        def done_wait(k):
            pe.wait_ge(tile_done, k + (1 + CREDIT))

        def norm_sums(n, sq, src, t):
            if n > 1:
                pe.wait_ge(n_rt, n - 1)
            for half in range(2 if t > 512 else 1):
                w = HALF if t > 512 else t
                for b in range(KB):
                    if half == 0 and b % 4 == 0:
                        pe.wait_ge(n_sq, 2 * (sq - 1) + b // 4 + 1)
                    mm = pe.matmul(ps[:, 6 + half, 0:w], ones[:, :], src[:, b, half * w:(half + 1) * w],
                                   start=(b == 0), stop=(b == KB - 1))
            mm.then_inc(n_ss, 1)

        for j in range(2):
            k = T_MOD22 + j
            pe.wait_ge(wsplit, k + 1)
            if j:
                pe.wait_ge(m_ev, j)
            n = 0
            for kb in range(KB):
                for a, b in ((cvhi, whi), (cvlo, whi), (cvhi, wlo)):
                    mm = pe.matmul(ps[:, 5, 0:TM], a[:, 2 * kb:2 * kb + P],
                                   b[:, k % 2, kb * TM:(kb + 1) * TM], start=(n == 0), stop=(n == 3 * KB - 1))
                    n += 1
            mm.then_inc(tile_done, 1)
            if j == 0:
                norm_sums(1, 1, sqb, S)
            pe.wait_ge(m_row, j + 1)
            for m in range(2):
                mm = pe.transpose(ps[:, 5, 2 * m:2 * m + 2], modrow[:, m * P:(m + 1) * P], ident[0:2, 0:2])
            mm.then_inc(m_T, 1)
        norm_sums(2, 2, sqb, T)

        pair = [0]

        def dense(s, off, width, src, kbs, last, read, kwait=None):
            hi, lo = src
            if read:
                read()
            q = 2 * pair[0]
            pair[0] ^= 1
            n, N = 0, 3 * len(kbs)
            for i, kb in enumerate(kbs):
                if kwait:
                    kwait(kb)
                c = off(i)
                for a, b in ((whi, hi), (wlo, hi), (whi, lo)):
                    for half in range(2):
                        mm = pe.matmul(ps[0:width, q + half, 0:HALF], a[:, s, c:c + width],
                                       b[:, kb, half * HALF:(half + 1) * HALF], start=(n == 0), stop=(n == N - 1))
                    n += 1
            mm.then_inc(tile_done if last else blk_ps, 1)

        IN, U = (inhi, inlo), (uh, ul)
        EIGHT = range(KB)

        def wait_split(k):
            pe.wait_ge(wsplit, k + 1)

        pe.wait_ge(m_ev, 2)
        pe.wait_ge(ld2, 6 * 16)
        wait_split(T_DT)
        dense(T_DT % 2, lambda i: i * 64, 64, IN, EIGHT, True, None, lambda kb: pe.wait_ge(in_lo, kb + 1))

        def turn_dt():
            pe.wait_ge(dt_d, 1)
            for c in range(NC):
                mm = pe.transpose(ps[:, 4, c * 64:(c + 1) * 64], dtT[:, c * P:(c + 1) * P], ident[0:64, 0:64])
            mm.then_inc(dt_p, 1)

        wait_split(T_XS0)
        dense(T_XS0 % 2, lambda i: i * TM, P, IN, EIGHT, False, None)
        turn_dt()
        dense(T_XS0 % 2, lambda i: i * TM + P, P, IN, EIGHT, True, lambda: pe.wait_ge(dt_d, 1))
        wait_split(T_BC0)
        dense(T_BC0 % 2, lambda i: i * TM, P, IN, EIGHT, False, lambda: pe.wait_ge(x_rd, 1))
        pe.wait_ge(dt_d, DT_G)
        for d, tri in enumerate((triF, triB)):
            pe.matmul(ps[:, 5, 0:384].rearrange("p (c n) -> p c n", c=NC)[:, :, 32 * d:32 * d + 32], tri[:, :],
                      tab[:, K_G:K_G + 2 * NC, :].rearrange("p (c d) r -> p d c r", d=2)[:, d], start=True, stop=True)
        pe.matmul(ps[:, 6, 0:384], ones[:, :], tab[:, K_G:K_G + 2 * NC, :].rearrange("p c r -> p (c r)"),
                  start=True, stop=True).then_inc(dt_p, 1)
        dense(T_BC0 % 2, lambda i: i * TM + P, P, IN, EIGHT, True, lambda: pe.wait_ge(x_rd, 2))

        def group(g, last):
            kt = g * G_TILES + T_G0
            nb = 3 if last else 10
            blk0 = g * 10 + 2

            def last_reads():
                pe.wait_ge(x_rd, g * 4 + 4)
                pe.wait_ge(o_rd, g * 8 + 8)
            pe.wait_ge(cv_r, g * 4 + 4)
            pe.wait_ge(y_rd, g * 6 + 6)
            for c in range(NC):
                q = 4 + c % 4
                if c >= 4:
                    pe.wait_ge(tok_r, g * 6 + (c - 3))
                else:
                    pe.wait_ge(y_rd, g * 6 + 6)
                t0 = c * P + (2 if c >= CTX_CHUNKS else 0)
                for b in range(2):
                    pe.transpose(ps[:, q, b * P:(b + 1) * P], convd[:, b, t0:t0 + P], ident[:, :])
                pe.matmul(ps[:, q, 256:384], convd[:, 2, t0:t0 + P], convd[:, 3, t0:t0 + P], start=True, stop=True)
                pe.transpose(ps[:, q, 384:512], convd[:, 2, t0:t0 + P], ident[:, :]).then_inc(pre_ps, 1)
            wait_split(kt)
            dense(T_G0 % 2, lambda i: i * TM, P, IN, EIGHT, False, last_reads)
            for c in range(NC):
                pe.wait_ge(xte_r, g * 6 + (c + 1))
                if c < 4:
                    pe.wait_ge(tok_r, g * 6 + (c + 3))
                else:
                    pe.wait_ge(sc_r, g * 6 + (c - 3))
                for d in range(2):
                    if (d, c) in ((0, 5), (1, 2)):
                        continue
                    mm = pe.matmul(ps[:, 4 + (c + 2) % 4, d * 256:(d + 1) * 256], btok[:, c, :],
                                   xte[:, d, :, :].rearrange("p r n -> p (r n)"), start=True, stop=True)
                mm.then_inc(st_ps, 1)
            dense(T_G0 % 2, lambda i: i * TM + P, P, IN, EIGHT, True, None)

            def log_decay(c):
                pe.wait_ge(sc_r, g * 6 + 6) if c == 0 else pe.wait_ge(ex_r, g * 6 + c)
                pe.wait_ge(tabg_r, g + 1)
                for d, tri in enumerate((triF, triB)):
                    pe.matmul(ps[:, 4 + d, :], identb[:, :], mask2[:, d:d + 1, :].broadcast_to([P, HPG, P]),
                              start=True, stop=False)
                    for r in range(HPG):
                        mm = pe.matmul(ps[:, 4 + d, r * P:(r + 1) * P],
                                       tabg[:, K_G + 2 * c + d, r:r + 1].broadcast_to([P, P]), tri[:, :],
                                       start=False, stop=(r == HPG - 1))
                mm.then_inc(la_ps, 1)

            def off_part(c):
                pe.wait_ge(scan_r, g + 1)
                pe.wait_ge(ck_r, g + 1)
                if c:
                    pe.wait_ge(offs_r, g * 6 + c)
                for d, slot in enumerate((PREV_F[c], PREV_B[c])):
                    if slot is not None:
                        mm = pe.matmul(ps[:, 6, d * 256:(d + 1) * 256], ck[:, c * P:(c + 1) * P], ast[:, slot, :],
                                       start=True, stop=True)
                mm.then_inc(off_ps, 1)

            def y_part(c):
                pe.wait_ge(offs_r, g * 6 + (c + 1))
                pe.wait_ge(W_r, g * 6 + (c + 1))
                pe.wait_ge(y_rd, g * 6 + (6 + c))
                base = (c % 2) * 256
                for b in range(2):
                    q = base + b * P
                    pe.matmul(ps[:, 7, q:q + P], offs[:, 0, 2 * b:2 * b + 2, :].rearrange("p r n -> p (r n)"), ident[:, :],
                              start=True, stop=False)
                    for r in range(2):
                        x0 = (2 * b + r) * HD
                        mm = pe.matmul(ps[64 * r:64 * r + 64, 7, q:q + P], xcb[:, c, x0:x0 + HD], wdec[:, 2 * b + r, :],
                                       start=False, stop=True)
                mm.then_inc(y_ps, 1)

            if not last:
                xs, bc = (T_G0 + 1) % 2, (T_G0 + 2) % 2
                between = {
                    0: (lambda: wait_split(kt + 1), xs, 0, False, lambda: pe.wait_ge(z_rd, g * 2 + 1)),
                    1: (None, xs, P, True, lambda: pe.wait_ge(z_rd, g * 2 + 2)),
                    2: (lambda: wait_split(kt + 2), bc, 0, False, lambda: pe.wait_ge(x_rd, g * 4 + 5)),
                    4: (None, bc, P, True, lambda: pe.wait_ge(x_rd, g * 4 + 6))}
            log_decay(0)
            off_part(0)
            for c in range(NC):
                if not last and c in between:
                    w, k, o, end, read = between[c]
                    if w:
                        w()
                    dense(k, lambda i: i * TM + o, P, IN, EIGHT, end, read)
                if c + 1 < NC:
                    log_decay(c + 1)
                y_part(c)
                if c + 1 < NC:
                    off_part(c + 1)
            k = 1 if last else 3
            wait_split(kt + k)
            pe.wait_ge(u_r, g * 2 + 2)
            for j in range(KB):
                if j >= 2:
                    read = lambda: pe.wait_ge(o_rd, g * 8 + (8 + j - 1))
                elif last:
                    read = lambda: pe.wait_ge(z_rd, g * 2 + 1 + j)
                else:
                    read = lambda: pe.wait_ge(x_rd, g * 4 + (7 + j))
                dense((T_G0 + k) % 2, lambda i: i * D + j * P, P, U, range(2), j == KB - 1, read)

        with pe.Fori(0, GROUPS - 1) as g:
            group(g, False)
        group(GROUPS - 1, True)

        pe.wait_ge(acc_r2, GROUPS + 1)
        pe.wait_ge(y_rd, 6 * GROUPS + 6)
        for half in range(2):
            mm = pe.matmul(ps[:, 6 + half, 0:HALF], ones[:, :], acc[:, half * HALF:(half + 1) * HALF],
                           start=True, stop=True)
        mm.then_inc(n_ss, 1)
        norm_sums(4, 3, sq4, T)

        pe.wait_ge(o_rd, 8 * GROUPS + 8)
        pair[0] = 0
        for m, k in ((0, 0), (1, 0), (0, 1), (1, 1)):
            if m == 0:
                wait_split(T_ATT + k)
            u = 2 * k + m
            dense((T_ATT + k) % 2, lambda i: i * TM + m * P, P, IN, EIGHT, m == 1,
                  (lambda: pe.wait_ge(a_rd, u - 1)) if u >= 2 else None,
                  (lambda kb: pe.wait_ge(in_lo, KB + kb + 1)) if u == 0 else None)

        def lat_tile(k, unit, src, t0, read, kwait=None):
            hi, lo = src
            wait_split(k)
            read()
            q = 2 * (unit % 2)
            for m in range(2):
                n = 0
                for kb in EIGHT:
                    if kwait and m == 0:
                        kwait(kb)
                    c = kb * TM + m * P
                    for a, b in ((whi, hi), (wlo, hi), (whi, lo)):
                        mm = pe.matmul(ps[:, q + m, :], a[:, k % 2, c:c + P], b[:, kb, t0:t0 + S],
                                       start=(n == 0), stop=(n == 3 * KB - 1))
                        n += 1
            mm.then_inc(tile_done, 1)

        def q_tile(j):
            lat_tile(T_ATT + 2 + j, j, IN, CTX, lambda: pe.wait_ge(a_rd, 3 + j))

        def head_sums_q(b0):
            pe.wait_ge(a_rd, 4 + b0 // 2 + 2)
            pe.wait_ge(ln_r, 1 + b0 // 4)
            for b in range(4):
                mm = pe.matmul(ps[:, 4 + b, :], bones[:, :], qsq[:, b0 + b, :], start=True, stop=True)
            mm.then_inc(ssh, 1)

        q_tile(0)
        q_tile(1)
        pe.wait_ge(ld3, 16 * 4)
        pe.wait_ge(a_rd, 2)
        pe.wait_ge(n_rt, 4)
        for m in range(2):
            for half in range(2):
                mm = pe.matmul(ps[:, 4 + 2 * m + half, 0:HALF], bones[:, :], ksq[:, m, half * HALF:(half + 1) * HALF],
                               start=True, stop=True)
        mm.then_inc(ssh, 1)
        q_tile(2)
        head_sums_q(0)
        q_tile(3)
        head_sums_q(4)
        for j in range(4):
            lat_tile(T_ATT + 6 + j, j, IN, CTX,
                     lambda: pe.wait_ge(a_rd, 7 + j) if j < 2 else pe.wait_ge(g_rd, j - 1))
        pe.wait_ge(ln_r, 3)
        for n in range(10):
            pe.wait_ge(qn_r, 1 if n < 2 else 2 + (n - 2) // 4)
            if n >= 4:
                pe.wait_ge(rp_rd, n - 3)
            src = kf[:, n, CTX:T] if n < 2 else qb_[:, n - 2, :]
            pe.matmul(ps[:, 4 + n % 4, :], perm2[:, :], src, start=True, stop=True).then_inc(rp_ps, 1)
        pe.wait_ge(g_rd, 4)
        for c in range(NC):
            if c >= 4:
                pe.wait_ge(vt_r, c - 3)
            for b in range(2):
                mm = pe.transpose(ps[:, c % 4, b * P:(b + 1) * P], vf[:, b, c * P:(c + 1) * P], ident[:, :])
            mm.then_inc(vt_ps, 1)
        pe.wait_ge(vt_r, NC)
        pe.wait_ge(rp_rd, 10)

        with pe.Fori(0, 2) as i:
            def score_max(h):
                j, p = h // REP, h % 2
                if h % REP == 0:
                    pe.wait_ge(k_lo, i * 2 + (j + 1))
                pe.wait_ge(q_lo, i * 8 + (h + 1))
                for t in range(4):
                    q = 2 * (t % 2)
                    n = 4 * h + t
                    if n >= 2:
                        pe.wait_ge(mx_r, i * 32 + (n - 1))
                    for half in range(2):
                        ks = slice(half * HALF, (half + 1) * HALF)
                        pe.matmul(ps[:, q + half, 0:HALF], Q1[p][:, t * P:(t + 1) * P], K1[j][:, ks],
                                  start=True, stop=False)
                        mm = pe.matmul(ps[:, q + half, 0:HALF], Q2[p][0:64, t * P:(t + 1) * P], K2[j][0:64, ks],
                                       start=False, stop=True)
                    mm.then_inc(s_ps, 1)

            def attend(h):
                j, p = h // REP, h % 2
                for t in range(4):
                    if t == 0:
                        pe.wait_ge(mxf_r, i * 8 + (h + 1))
                        if h:
                            pe.wait_ge(mxl_r, i * 8 + h)
                    mm = pe.matmul(ps[:, 4, t * P:(t + 1) * P], nm4[:, p, t:t + 1].broadcast_to([P, P]), ident[:, :],
                                   start=True, stop=True)
                mm.then_inc(mx_ps, 1)
                if h + 1 < 8:
                    score_max(h + 1)
                pe.wait_ge(mxl_r, i * 8 + (h + 1))

                def pv(kb):
                    pe.wait_ge(p_r2, i * 48 + (6 * h + kb + 1))
                    if kb == 0:
                        pe.wait_ge(va_r, i * 2 + (j + 1))
                        if h:
                            pe.wait_ge(o_ev, i * 8 + h)
                    mm = pe.matmul(ps[:, 7, :], vaug[:, kb, :], pT2[:, kb, :], start=(kb == 0), stop=(kb == NC - 1))
                    return mm
                for kb in range(NC):
                    n = 6 * h + kb
                    if n >= 2:
                        pe.wait_ge(p_r2, i * 48 + (n - 1))
                    pe.matmul(ps[:, 5 + kb % 2, :], K1[j][:, kb * P:(kb + 1) * P], Q1[p][:, :], start=True, stop=False)
                    pe.matmul(ps[:, 5 + kb % 2, :], K2[j][:, kb * P:(kb + 1) * P], Q2[p][:, :], start=False, stop=True
                              ).then_inc(sT_ps, 1)
                    if kb:
                        pv(kb - 1)
                pv(NC - 1).then_inc(o_ps, 1)

            score_max(0)
            for h in range(8):
                attend(h)
        for j in range(4):
            lat_tile(T_ATT + 10 + j, j, (ohi, olo), 0, (lambda: pe.wait_ge(hf_r, j - 1)) if j >= 2 else (
                lambda: pe.wait_ge(mx_r, 64)), (lambda kb: pe.wait_ge(ol_r, kb + 1)) if j == 0 else None)
        norm_sums(5, 4, sqb, S)

    @block.scalar
    def _(act):
        L = Ls
        A = act.activation
        act.wait_ge(cst, CST)
        A(small[:, 0:16], cvec[:, :, :].rearrange("p a b -> p (a b)"), ACT.Tanh, scale=0.5).then_inc(init_a, 1)
        act.wait_ge(init_d, D_ANGLE)
        A(ropeS[:, :], angt[0][:, :], ACT.Sin).then_inc(init_a, 1)
        A(ropeC[:, :], angt[0][:, :], ACT.Abs).then_inc(init_a, 1)
        act.wait_ge(init_a, 3)
        A(ropeC[:, :], ropeC[:, :], ACT.Sin, scale=-1.0, bias=misc[:, 2:3]).then_inc(init_a, 1)
        act.wait_ge(init_d, D_SILU)
        A(cvhi[:, 0:2 * KB], cvec[:, :, :].rearrange("p a b -> p (a b)"), ACT.Copy).then_inc(init_a, 1)
        act.wait_ge(init_d, INIT_D)

        with act.Fori(0, DEPTH) as l:
            st = Chain(act, L["a_step"])

            def tile_wait(k):
                act.wait_ge(tile_done, l * LAYER_TILES + (k + 1 + CREDIT))

            act.dma_start(gw[:, :, :], io["gates"][bass.ds(l, 1)].rearrange("a p j n -> p (a j) n")).then_inc(lw[0], 16)
            act.dma_start(pT[:, :, :], io["pT"][bass.ds(l, 1)].rearrange("a p j n -> p (a j) n")).then_inc(lw[1], 16)
            act.wait_ge(L["lp_copied"], 1)
            st(A(small[:, 4:8], lp[:, C_LRU:C_LRU + 4], ACT.Abs))
            A(small[:, 8:12], small[:, 4:8], ACT.Exp, scale=-1.0).then_inc(L["lsa"], 1)

            def prepare(n, j, g, tmp, h_at):
                if h_at:
                    act.wait_ge(L["h_r"], h_at)
                if j == 0 and n > 1:
                    act.wait_ge(L["ssq_r"], n - 1)
                if j > 1:
                    act.wait_ge(L["acc_r"], 3 * (n - 1) + j - 1)
                A((tmp if j else acc2)[:, :, :], h[:, 2 * j:2 * j + 2, :], ACT.Square).then_inc(L["sq_r"], 1)
                for b in (2 * j, 2 * j + 1):
                    A(uhi[:, b, :], h[:, b, :], ACT.Copy, scale=lp[:, g + b:g + b + 1]).then_inc(L["uhi_r"], 1)

            def norm_root(n):
                act.wait_ge(L["ssq_r"], n)
                if n > 1:
                    act.wait_ge(L["rstd_r"], n - 1)
                A(rstd[:, :], ps[:, 4, :], ACT.Sqrt, scale=1.0 / D, bias=misc[:, 0:1]).then_inc(L["sqrt_r"], 1)

            def mod_row(j, k):
                tile_wait(k)
                if j:
                    act.wait_ge(L["mod_T"], j)
                A(modrow[:, :], ps[0:2, 5, 0:TM], ACT.Copy).then_inc(L["mod_row"], 1)

            def mod_cols(j):
                act.wait_ge(L["mod_T"], j + 1)
                A(modsb[:, bass.ds(l * (2 * MOD_IN_LAYER) + 2 * j, 2), :].rearrange("p a b -> p (a b)"),
                  ps[:, 5, 0:4], ACT.Copy).then_inc(L["mod_ev"], 1)

            for j in range(4):
                prepare(1, j, C_GMIX, sqmlp, 0)
            act.wait_ge(L["dots_r"], 1)
            A(small[:, 2:4], ps[:, 6, 0:2], ACT.Exp).then_inc(L["lam_r"], 1)
            norm_root(1)
            mod_row(0, 1)
            for j in range(1, 4):
                mod_cols(j - 1)
                mod_row(j, 2 * j + 1)
            for b in range(2):
                act.wait_ge(L["proj_r"], 3 + b)
                A(gt[:, 2 * b:2 * b + 2, :], proj[:, GR + 2 * b:GR + 2 * b + 2, :], ACT.Square).then_inc(L["lru_a"], 1)
            act.wait_ge(L["lsp"], 2)
            for n in range(8):
                act.wait_ge(L["gate_ps"], n + 1)
                A((ga if n < 4 else gi)[:, n % 4, :], ps[:, 6 + n % 2, :], ACT.Tanh, scale=0.5,
                  bias=small[:, 16 + n:17 + n]).then_inc(L["gate_t"], 1)
            act.wait_ge(L["lru_d"], 1)
            A(gt[:, :, :], gt[:, :, :], ACT.Tanh).then_inc(L["lru_a"], 1)
            act.wait_ge(L["lru_d"], 2)
            st(A(gt[:, :, :], ga[:, :, :], ACT.Tanh, scale=-1.0))
            st(A(ga[:, :, :], ga[:, :, :], ACT.Exp))
            A(asq[:, :, :], ga[:, :, :], ACT.Square).then_inc(L["lru_a"], 1)
            mod_cols(3)
            mod_row(4, 9)
            act.wait_ge(L["lru_d"], 3)
            A(gt[:, :, :], gt[:, :, :], ACT.Sqrt, scale=0.25).then_inc(L["lru_a"], 1)
            for j in range(5, 7):
                mod_cols(j - 1)
                mod_row(j, 2 * j + 1)
            act.wait_ge(L["lru_d"], 4)
            A(oyhi[:, 4:8, :], ga[:, :, :], ACT.Copy).then_inc(L["yhi_r"], 1)
            for j in range(7, 10):
                mod_cols(j - 1)
                mod_row(j, 2 * j + 1)
            mod_cols(9)
            for t in range(4):
                act.wait_ge(L["v_ps"], t + 1)
                A(vtok[:, t, :], ps[:, t, :], ACT.Copy).then_inc(L["v_r"], 1)

            def exps(n):
                p, w = n % 2, (n % 4 + 1) * P
                act.wait_ge(L["nmax_r"], n + 1)
                if n >= 2:
                    act.wait_ge(L["att_r"], n - 1)
                for c in range(2):
                    A(pexp[:, p, c, 0:w], ps[:, 2 * p + c, 0:w], ACT.Exp, bias=small[:, 44 + 2 * p + c:45 + 2 * p + c],
                      accum_out=small[:, 48 + 2 * p + c:49 + 2 * p + c]).then_inc(L["exp_r"], 1)

            def head_out(hd):
                act.wait_ge(L["pv_r"], 4 * hd + 4)
                A(osb[:, hd, :], ps[:, 4 + hd % 2, :], ACT.Copy).then_inc(L["o_r"], 1)
                A(osq[:, hd, :], ps[:, 4 + hd % 2, :], ACT.Square).then_inc(L["o_r"], 1)

            exps(0)
            for n in range(16):
                if n + 1 < 16:
                    exps(n + 1)
                act.wait_ge(L["attT_r"], n + 1)
                if n >= 2:
                    act.wait_ge(L["pv_r"], n - 1)
                w = (n % 4 + 1) * P
                A(pattT[:, n % 2, 0:w], ps[:, 6 + n % 2, 0:w], ACT.Copy).then_inc(L["attTc"], 1)
                if n % 4 == 0 and n:
                    head_out(n // 4 - 1)
            head_out(3)
            act.wait_ge(L["oss_r"], 4)
            A(orst[:, :, :], ps[:, 0:4, :], ACT.Ln, scale=1.0 / P, bias=misc[:, 0:1]).then_inc(L["orst_r"], 1)
            act.wait_ge(L["orst_r"], 1)
            A(orst[:, :, :], orst[:, :, :], ACT.Exp, scale=-0.5).then_inc(L["orst_r"], 1)
            for hd in range(HEADS):
                act.wait_ge(L["on_r"], hd + 1)
                A(oyhi[:, hd, :], osb[:, hd, :], ACT.Copy).then_inc(L["ohi_r"], 1)
            for j in range(4):
                prepare(2, j, C_GMLP, sqmlp, j + 1)
            mod_row(10, T_MOD10)
            mod_cols(10)
            norm_root(2)
            act.wait_ge(lw[1], l * 16 + 16)
            A(phi[:, :, :], pT[:, :, :], ACT.Copy).then_inc(L["phi_r"], 1)
            for c in range(CHUNKS):
                for j in range(4):
                    n = 4 * c + j
                    act.wait_ge(L["m_r"], n + 1)
                    if n >= 2:
                        act.wait_ge(L["hlo_r"], n - 1)
                    A(hsq[n % 2][:, :, :], hm[n % 2][:, :, :], ACT.Square).then_inc(L["sqh_r"], 1)
                    A(hidhi[:, 2 * j:2 * j + 2, :], hm[n % 2][:, :, :], ACT.Square).then_inc(L["sqh_r"], 1)
            for j in range(4):
                prepare(3, j, C_GPLE, sqple, 4 + 4 * (CHUNKS - 1) + j + 1)
            for g in range(4):
                act.wait_ge(L["pp_ps"], g + 1) if g < 3 else tile_wait(T_PP)
                A(pp[:, 2 * g:2 * g + 2, :], TWO(g % 2), ACT.Copy).then_inc(L["pp_r"], 1)
            norm_root(3)
            for j in range(4):
                act.wait_ge(L["g_r"], j + 1)
                A(gth[j % 2][:, :, :], gm[j % 2][:, :, :], ACT.Tanh, scale=0.5).then_inc(L["gth_r"], 1)
            act.wait_ge(L["gth_r"], 4)
            act.sem_inc(L["layer_done"], 1)
            act.wait_ge(layer_go, l + 1)

        if stage == 1:
            return

        def done_wait(k):
            act.wait_ge(tile_done, k + (1 + CREDIT))

        def halves(x):
            return x.rearrange("p (a n) -> p a n", a=2)

        for dst, src in ((p2[:, :], io["params2"]), (triF[:, :], io["consts2"][:, 0:128]),
                         (triB[:, :], io["consts2"][:, 128:256]),
                         (masktmp[:, :, :].rearrange("p a b -> p (a b)"), io["consts2"][:, 256:512]),
                         (drow[:, :], io["m_d"].partition_broadcast(P)),
                         (arow[:, :], io["m_a_log"].partition_broadcast(P))):
            act.dma_start(dst, src).then_inc(ld2, 16)
        act.dma_start(hres[:, :, 0:CTX], io["ctx"]).then_inc(ldc, 16)
        for j in range(2):
            A(sqb[:, 4 * j:4 * j + 4, 0:S], h[:, 4 * j:4 * j + 4, :], ACT.Square).then_inc(n_sq, 1)

        def mod2_row(j):
            done_wait(T_MOD22 + j)
            if j:
                act.wait_ge(m_T, 1)
            A(modrow[:, :], ps[0:2, 5, 0:TM], ACT.Copy).then_inc(m_row, 1)

        def mod2_cols(j):
            act.wait_ge(m_T, j + 1)
            A(modsb[:, 44 + 2 * j:46 + 2 * j, :].rearrange("p a b -> p (a b)"), ps[:, 5, 0:4], ACT.Copy
              ).then_inc(m_ev, 1)

        def root(n, dst, src, scale):
            act.wait_ge(n_ss, n)
            if n > 1:
                act.wait_ge(n_rs, n - 1)
            A(dst, src, ACT.Sqrt, scale=scale, bias=misc[:, 0:1]).then_inc(n_rt, 1)

        mod2_row(0)
        root(1, rstd[:, :], ps[:, 6, :], 1.0 / D)
        mod2_cols(0)
        mod2_row(1)
        mod2_cols(1)
        act.wait_ge(ldc, 16)
        for j in range(2):
            act.wait_ge(n_x, 4 * j + 4)
            A(sqb[:, 4 * j:4 * j + 4, :], hres[:, 4 * j:4 * j + 4, :], ACT.Square).then_inc(n_sq, 1)
        act.dma_start(hspill, hres[:, :, :]).then_inc(spill, 16)
        both = ps[:, 6:8, 0:HALF]
        root(2, halves(rs2[:, :]), both, 1.0 / D)

        def make_in(i):
            for b in range(KB):
                act.wait_ge(in_t, KB * i + b + 1)
                A(inhi[:, b, :], tin[:, b % 2, :], ACT.Copy).then_inc(in_hi, 1)
        make_in(0)

        def copy_in(s, b, blk, tile_no):
            if b % 2 == 0:
                act.wait_ge(blk_ps, blk)
            else:
                done_wait(tile_no)
            if b >= 2:
                act.wait_ge(cv_r, s * 4 + (b - 1))
            q = 2 - 2 * (b % 2)
            r = raw[b % 2]
            A(r[:, 2:2 + CTX], ps[:, q, 0:CTX], ACT.Copy)
            A(r[:, 4 + CTX:4 + HALF], ps[:, q, CTX:HALF], ACT.Copy)
            A(r[:, 4 + HALF:4 + T], ps[:, q + 1, 0:HALF], ACT.Copy).then_inc(x_rd, 1)

        def conv_tanh(s, b):
            act.wait_ge(cv_c, s * 4 + (b + 1))
            A(raw[b % 2][:, 2:2 + CTX], convd[:, b, 0:CTX], ACT.Tanh)
            A(raw[b % 2][:, 4 + CTX:4 + T], convd[:, b, 2 + CTX:2 + T], ACT.Tanh).then_inc(cv_t, 1)

        act.wait_ge(dt_d, 2)
        A(dtw[1][:, :, :], dtw[0][:, :, :], ACT.Abs).then_inc(dt_a, 1)
        act.wait_ge(dt_a, 1)
        A(dtw[1][:, :, :], dtw[1][:, :, :], ACT.Exp, scale=-1.0).then_inc(dt_a, 1)
        A(arow[:, :], arow[:, :], ACT.Exp).then_inc(dt_a, 1)
        act.wait_ge(pads, 1)
        copy_in(0, 0, 1, None)
        copy_in(0, 1, None, T_XS0)
        conv_tanh(0, 0)
        conv_tanh(0, 1)
        copy_in(0, 2, 2, None)
        act.wait_ge(dt_d, DT_C)
        flat = lambda k: tab[:, k:k + 2 * NC, :].rearrange("p c r -> p (c r)")
        w = lambda n: dtw[n][:, :, :].rearrange("p c r -> p (c r)")
        A(w(6), w(6), ACT.Ln).then_inc(dt_a, 1)
        A(flat(K_EXLA), w(3), ACT.Exp)
        A(flat(K_DEC), w(4), ACT.Exp)
        A(w(5), w(5), ACT.Exp).then_inc(dt_a, 1)
        copy_in(0, 3, None, T_BC0)
        conv_tanh(0, 2)
        conv_tanh(0, 3)
        act.wait_ge(spill, 16)

        def group(g, last):
            kt = g * G_TILES + T_G0
            blk0 = g * 10 + 2
            act.wait_ge(cv_r, g * 4 + 4)
            act.wait_ge(y_rd, g * 6 + 6)
            A(ck[:, 0:CTX], convd[:, 3, 0:CTX], ACT.Copy)
            A(ck[:, CTX:T], convd[:, 3, CTX + 2:T + 2], ACT.Copy).then_inc(ck_r, 1)
            act.wait_ge(acc_r2, g + 1)
            for c in range(NC):
                act.wait_ge(pre_ps, g * 6 + (c + 1))
                A(xcb[:, c, :], ps[:, 4 + c % 4, 0:384], ACT.Copy)
                A(btok[:, c, :], ps[:, 4 + c % 4, 384:512], ACT.Copy).then_inc(tok_r, 1)

            def z_tanh(b):
                if b == 0:
                    act.wait_ge(blk_ps, blk0 + 1)
                else:
                    done_wait(kt)
                q = 2 - 2 * b
                A(halves(zs[:, b, :]), ps[:, q:q + 2, 0:HALF], ACT.Tanh, scale=0.5).then_inc(z_t, 1)

            z_tanh(0)
            for c in range(NC):
                act.wait_ge(st_ps, g * 6 + (c + 1))
                q = 4 + (c + 2) % 4
                for slots, d in ((SLOT_F, 0), (SLOT_B, 1)):
                    if c in slots:
                        ins = A(ast[:, slots[c], :], ps[:, q, d * 256:(d + 1) * 256], ACT.Copy)
                ins.then_inc(sc_r, 1)
            z_tanh(1)

            def decays(c):
                act.wait_ge(la_ps, g * 6 + (c + 1))
                if c:
                    act.wait_ge(W_r, g * 6 + c)
                for d in range(2):
                    for r in range(HPG):
                        ins = A(ebuf[:, d, r, :], ps[:, 4 + d, r * P:(r + 1) * P], ACT.Exp,
                                bias=tabg[:, K_NB + 2 * c + d, r:r + 1])
                ins.then_inc(ex_r, 1)

            s1 = g + 1
            decays(0)
            decays(1)
            if not last:
                copy_in(s1, 0, blk0 + 2, None)
            decays(2)
            if not last:
                conv_tanh(s1, 0)
                copy_in(s1, 1, None, kt + 1)
            decays(3)
            if not last:
                conv_tanh(s1, 1)
                copy_in(s1, 2, blk0 + 3, None)
            decays(4)
            if not last:
                conv_tanh(s1, 2)
                copy_in(s1, 3, None, kt + 2)
            decays(5)
            act.wait_ge(tile_done, kt + CREDIT)
            for half in range(2):
                act.wait_ge(y_rd, g * 6 + (6 + 3 * half + 3))
                for m in range(2):
                    ins = A(uh[:, m, half * HALF:(half + 1) * HALF], zs[:, m, half * HALF:(half + 1) * HALF],
                            ACT.Copy, scale=mng[:, m:m + 1])
                ins.then_inc(uh_r, 1)
            A(sqz[:, :, :], zs[:, :, :], ACT.Square).then_inc(sqz_r, 1)
            if not last:
                conv_tanh(s1, 3)

        with act.Fori(0, GROUPS - 1) as g:
            group(g, False)
        group(GROUPS - 1, True)

        act.wait_ge(u_r, 2 * GROUPS)
        act.wait_ge(sqz_r, GROUPS)
        act.dma_start(hback[:, :, :], hspill).then_inc(spill, 16)
        root(3, halves(rs2[:, :]), both, 1.0 / MDI)
        act.wait_ge(n_rt, 3)
        for dst, src in ((bones, io["consts2"][:, 512:640]), (perm2, io["consts2"][:, 640:768]),
                         (cosT, io["axial"][0]), (sinT, io["axial"][1])):
            act.dma_start(dst[:, :], src).then_inc(ld3, 16)
        for j in range(2):
            act.wait_ge(n_x, KB + 4 * j + 4)
            A(sq4[:, 4 * j:4 * j + 4, :], oacc[:, 4 * j:4 * j + 4, :], ACT.Square).then_inc(n_sq, 1)
        root(4, halves(rs2[:, :]), both, 1.0 / D)
        make_in(1)
        blk0 = 2 + 10 * (GROUPS - 1) + 8
        for n in range(4):
            k, m = n // 2, n % 2
            act.wait_ge(blk_ps, blk0 + k + 1) if m == 0 else done_wait(T_ATT + k)
            src = ps[:, 2 * m:2 * m + 2, 0:HALF]
            ins = A(halves((vf if k else kf)[:, m, :]), src, ACT.Copy)
            if k == 0:
                ins = A(halves(ksq[:, m, :]), src, ACT.Square)
            ins.then_inc(a_rd, 1)

        def q_tile(j):
            done_wait(T_ATT + 2 + j)
            A(qb_[:, 2 * j:2 * j + 2, :], TWO(j % 2), ACT.Copy)
            A(qsq[:, 2 * j:2 * j + 2, :], TWO(j % 2), ACT.Square).then_inc(a_rd, 1)

        q_tile(0)
        q_tile(1)
        act.wait_ge(ssh, 1)
        k4 = ksq[:, :, :].rearrange("p m (a n) -> p (m a) n", a=2)
        A(k4, ps[:, 4:8, 0:HALF], ACT.Ln, scale=1.0 / HD, bias=misc[:, 0:1]).then_inc(ln_r, 1)
        q_tile(2)
        q_tile(3)
        for n in range(2):
            act.wait_ge(ssh, 2 + n)
            A(qsq[:, 4 * n:4 * n + 4, :], ps[:, 4:8, :], ACT.Ln, scale=1.0 / HD, bias=misc[:, 0:1]).then_inc(ln_r, 1)
        act.wait_ge(ln_r, 3)
        A(ksq[:, :, :], ksq[:, :, :], ACT.Exp, scale=-0.5).then_inc(rsh_r, 1)
        for n in range(2):
            A(qsq[:, 4 * n:4 * n + 4, :], qsq[:, 4 * n:4 * n + 4, :], ACT.Exp, scale=-0.5).then_inc(rsh_r, 1)
        for j in range(4):
            done_wait(T_ATT + 6 + j)
            A(gs[:, 2 * j:2 * j + 2, :], TWO(j % 2), ACT.Tanh, scale=0.5).then_inc(g_t, 1)
        for c in range(NC):
            act.wait_ge(vt_ps, c + 1)
            A(vtok2[:, c, :], ps[:, c % 4, 0:256], ACT.Copy).then_inc(vt_r, 1)
        act.wait_ge(rp_r, 10)
        act.wait_ge(vt_r, NC)

        with act.Fori(0, 2) as i:
            def split_q(hq):
                p, r0 = hq % 2, 64 * (hq % 2)
                src = qb_[r0:r0 + 64, bass.ds(i * 4 + hq // 2, 1), :].rearrange("p a n -> p (a n)")
                if hq:
                    act.wait_ge(q_lo, i * 8 + hq)
                if hq > 1:
                    act.wait_ge(o_ps, i * 8 + (hq - 1))
                act.sem_inc(act_go, 1)
                A(qq[:, :], src, ACT.Copy)
                A(Q1[p][0:64, :], src, ACT.Copy)
                A(Q1[p][64:128, :], src, ACT.Copy).then_inc(q_hi, 1)

            def ones_and_v(j):
                if j:
                    act.wait_ge(o_ps, i * 8 + 4 * j)
                act.sem_inc(act_go, 1)
                A(vaug[:, :, 0:64], vtok2[:, :, bass.ds(i * 128 + 64 * j, 64)], ACT.Copy).then_inc(va_r, 1)

            def o_hi(b):
                act.wait_ge(oy2, i * 4 + (b + 1))
                act.sem_inc(act_go, 1)
                A(ohi[:, bass.ds(i * 4 + b, 1), :], qb_[:, bass.ds(i * 4 + b, 1), :], ACT.Copy).then_inc(oh_r, 1)

            for j in range(2):
                src = kf[64 * j:64 * j + 64, bass.ds(i, 1), :].rearrange("p a n -> p (a n)")
                if j:
                    act.wait_ge(k_lo, i * 2 + j)
                act.sem_inc(act_go, 1)
                A(kk[:, :], src, ACT.Copy)
                A(K1[j][0:64, :], src, ACT.Copy)
                A(K2[j][0:64, :], src, ACT.Copy).then_inc(k_hi, 1)
            ones_and_v(0)
            split_q(0)
            for hq in range(8):
                p = hq % 2
                if hq + 1 < 8:
                    split_q(hq + 1)
                act.wait_ge(mx_ps, i * 8 + (hq + 1))
                A(Q2[p][64:128, :], ps[64:128, 4, :], ACT.Copy).then_inc(mxh_r, 1)
                if hq:
                    act.wait_ge(o_ps, i * 8 + hq)
                for kb in range(NC):
                    act.wait_ge(sT_ps, i * 48 + (6 * hq + kb + 1))
                    A(pT2[:, kb, :], ps[:, 5 + kb % 2, :], ACT.Exp).then_inc(p_r2, 1)
                if hq % 2 == 0:
                    if hq:
                        o_hi(hq // 2 - 1)
                act.wait_ge(o_ps, i * 8 + (hq + 1))
                r0 = 64 * p
                act.sem_inc(act_go, 1)
                A(qb_[r0:r0 + 64, bass.ds(i * 4 + hq // 2, 1), :].rearrange("p a n -> p (a n)"), ps[0:64, 7, :],
                  ACT.Copy)
                A(osum[r0:r0 + 64, :], ps[64:128, 7, :], ACT.Copy).then_inc(o_ev, 1)
                if hq == 3:
                    ones_and_v(1)
            o_hi(3)

        for n in range(2):
            act.wait_ge(hf_r, 2 * n + 2)
            A(sqb[:, 4 * n:4 * n + 4, 0:S], oacc[:, 4 * n:4 * n + 4, CTX:T], ACT.Square).then_inc(n_sq, 1)
        root(5, rs5[:, :], ps[:, 6, :], 1.0 / D)

    @block.vector
    def _(dve):
        L = Ls
        V = dve
        st = Chain(dve, init_d)
        st(V.memset(ones[:, :], 1.0))
        dve.wait_ge(cst, CST)
        st(V.tensor_copy(identb[:, :], ident[:, :]))
        st(V.tensor_copy(maskb[:, :], maskf[:, :]))
        st(V.tensor_copy(angt[0][:, :], posi[:, :]))
        st(V.tensor_scalar(angt[0][:, :], angt[0][:, :], misc[:, 1:2], None, ALU.mult))
        st(V.tensor_scalar(angt[1][:, :], angt[0][:, :], 1.0 / (2 * math.pi), MAGIC, ALU.mult, ALU.add))
        st(V.tensor_scalar(angt[1][:, :], angt[1][:, :], MAGIC, None, ALU.subtract))
        for part in (TWO_PI_1, TWO_PI_2, TWO_PI_3):
            st(V.scalar_tensor_tensor(out=angt[0][:, :], in0=angt[1][:, :], scalar=-part, in1=angt[0][:, :],
                                      op0=ALU.mult, op1=ALU.add))
        st(V.tensor_scalar(angt[0][:, :], angt[0][:, :], 3.1415925, -3.1415925, ALU.min, ALU.max))
        assert st.n == D_ANGLE
        dve.wait_ge(init_a, 1)
        cv = cvec[:, :, :].rearrange("p a b -> p (a b)")
        st(V.scalar_tensor_tensor(out=cv, in0=small[:, 0:16], scalar=1.0, in1=cv, op0=ALU.add, op1=ALU.mult))
        st(V.tensor_scalar(cv, cv, 0.5, None, ALU.mult))
        assert st.n == D_SILU
        dve.wait_ge(init_a, INIT_A)
        st(V.tensor_tensor(cvlo[:, 0:2 * KB], cv, cvhi[:, 0:2 * KB].bitcast(F32), ALU.subtract))
        st(V.memset(cvhi[:, 2 * KB:].bitcast(F32), 0.0))
        st(V.memset(cvlo[:, 2 * KB:].bitcast(F32), 0.0))
        st(V.tensor_scalar(ropeS[:, :], ropeS[:, :], misc[:, 3:4], None, ALU.mult))
        assert st.n == INIT_D

        with dve.Fori(0, DEPTH) as l:
            st = Chain(dve, L["d_step"])

            def tile_wait(k):
                dve.wait_ge(tile_done, l * LAYER_TILES + (k + 1 + CREDIT))

            st(V.tensor_copy(lp[:, :], lpall[:, bass.ds(l, 1), :].rearrange("p a n -> p (a n)")))
            dve.sem_inc(L["lp_copied"], 1)
            V.tensor_tensor(small[:, 0:2], lp[:, C_LQ:C_LQ + 2], lp[:, C_LK:C_LK + 2], ALU.mult).then_inc(L["lsp"], 1)

            def prepare(n, j, g, tmp):
                for b in (2 * j, 2 * j + 1):
                    dve.wait_ge(L["uhi_r"], KB * (n - 1) + b + 1)
                    V.scalar_tensor_tensor(out=ulo[:, b, :], in0=h[:, b, :], scalar=lp[:, g + b:g + b + 1],
                                           in1=uhi[:, b, :].bitcast(F32), op0=ALU.mult, op1=ALU.subtract
                                           ).then_inc(L["ulo_r"], 1)
                if j:
                    dve.wait_ge(L["sq_r"], 4 * (n - 1) + j + 1)
                    if j > 1:
                        dve.wait_ge(L["acc_r"], 3 * (n - 1) + j - 1)
                    V.tensor_tensor(acc2[:, :, :], acc2[:, :, :], tmp[:, :, :], ALU.add).then_inc(L["acc_r"], 1)

            def norm_recip(n):
                dve.wait_ge(L["sqrt_r"], n)
                V.reciprocal(rstd[:, :], rstd[:, :]).then_inc(L["rstd_r"], 1)
                dve.wait_ge(L["rstd_r"], n)

            rstd2 = rstd[:, :].unsqueeze(1).broadcast_to([P, 2, S])

            for j in range(4):
                prepare(1, j, C_GMIX, sqmlp)
            dve.wait_ge(L["lsa"], 1)
            softplus(V, st, small[:, 12:16], small[:, 8:12], small[:, 28:32], small[:, 32:36], small[:, 36:40])
            st(V.tensor_scalar(small[:, 28:32], lp[:, C_LRU:C_LRU + 4], -1.0, 0.0, ALU.mult, ALU.max))
            st(V.tensor_tensor(small[:, 12:16], small[:, 12:16], small[:, 28:32], ALU.add))
            st(V.tensor_scalar(small[:, 24:28], small[:, 12:16], -4.0, None, ALU.mult))
            V.tensor_scalar(small[:, 16:24], lp[:, C_BA:C_BA + 8], 0.5, None, ALU.mult).then_inc(L["lsp"], 1)
            dve.wait_ge(L["lam_r"], 1)
            st(V.tensor_tensor(small[:, 40:41], small[:, 3:4], small[:, 2:3], ALU.subtract))
            st(V.tensor_tensor(small[:, 40:41], small[:, 40:41], lp[:, C_LI:C_LI + 1], ALU.subtract))
            st(V.tensor_tensor(small[:, 41:42], lp[:, C_GSUB:C_GSUB + 1], lp[:, C_1LI:C_1LI + 1], ALU.mult))
            norm_recip(1)

            def mix_out(j):
                tile_wait(2 * j)
                V.tensor_tensor(proj[:, 2 * j:2 * j + 2, :], TWO(j % 2), rstd2, ALU.mult).then_inc(L["proj_r"], 1)

            def conv(b):
                x = proj[:, XR + b, :]
                tap = lambda i: lp[:, C_CW + 4 * i + b:C_CW + 4 * i + b + 1]
                st(V.tensor_scalar(xc[:, b, :], x, tap(3), lp[:, C_CB + b:C_CB + b + 1], ALU.mult, ALU.add))
                for i in (1, 2, 3):
                    ins = V.scalar_tensor_tensor(out=xc[:, b, i:], in0=x[:, 0:S - i], scalar=tap(3 - i),
                                                 in1=xc[:, b, i:], op0=ALU.mult, op1=ALU.add)
                    if i < 3:
                        st(ins)
                ins.then_inc(L["xc_r"], 1)

            mix_out(0)
            dve.wait_ge(L["proj_r"], 1)
            conv(0)
            conv(1)
            mix_out(1)
            dve.wait_ge(L["proj_r"], 2)
            conv(2)
            conv(3)
            mix_out(2)
            mix_out(3)
            c0 = math.sqrt(2 / math.pi)
            dve.wait_ge(L["lru_a"], 2)
            st(V.tensor_scalar(gt[:, :, :], gt[:, :, :], 0.044715 * c0, c0, ALU.mult, ALU.add))
            V.tensor_tensor(gt[:, :, :], gt[:, :, :], proj[:, GR:GR + 4, :], ALU.mult).then_inc(L["lru_d"], 1)
            for b in range(4):
                dve.wait_ge(L["gate_t"], b + 1)
                st(V.tensor_scalar(ga[:, b, :], ga[:, b, :], small[:, 24 + b:25 + b], small[:, 24 + b:25 + b],
                                   ALU.mult, ALU.add))
            dve.wait_ge(L["lru_a"], 3)
            V.scalar_tensor_tensor(out=proj[:, GR:GR + 4, :], in0=gt[:, :, :], scalar=1.0, in1=proj[:, GR:GR + 4, :],
                                   op0=ALU.add, op1=ALU.mult).then_inc(L["lru_d"], 1)
            dve.wait_ge(L["gate_t"], 8)
            st(V.scalar_tensor_tensor(out=xc[:, :, :], in0=gi[:, :, :], scalar=1.0, in1=xc[:, :, :],
                                      op0=ALU.add, op1=ALU.mult))
            mix_out(4)
            dve.wait_ge(L["lru_a"], 4)
            V.scalar_tensor_tensor(out=gt[:, :, :], in0=asq[:, :, :], scalar=1.0, in1=gt[:, :, :],
                                   op0=ALU.add, op1=ALU.mult).then_inc(L["lru_d"], 1)
            mix_out(5)
            dve.wait_ge(L["lru_a"], 5)
            st(V.tensor_tensor(xc[:, :, :], gt[:, :, :], xc[:, :, :], ALU.mult))
            for b in range(4):
                ins = V.tensor_tensor_scan(asq[:, b, :], ga[:, b, :], xc[:, b, :], 0.0, ALU.mult, ALU.add)
                if b < 3:
                    ins.then_inc(L["d_step"], 1)
                    st.n += 1
                else:
                    st(ins)
            V.scalar_tensor_tensor(out=ga[:, :, :], in0=asq[:, :, :], scalar=0.5, in1=proj[:, GR:GR + 4, :],
                                   op0=ALU.mult, op1=ALU.mult).then_inc(L["lru_d"], 1)
            mix_out(6)

            rope_n = [0]

            def rope(m, scale):
                n = rope_n[0]
                rope_n[0] += 1
                dve.wait_ge(L["rope_ps"], n + 1)
                V.scalar_tensor_tensor(out=rtmp[:, n % 2, :], in0=ps[:, 6 + n % 2, :], scalar=scale, in1=ropeS[:, :],
                                       op0=ALU.mult, op1=ALU.mult).then_inc(L["rope_rd"], 1)
                st(V.scalar_tensor_tensor(out=proj[:, m, :], in0=proj[:, m, :], scalar=scale, in1=ropeC[:, :],
                                          op0=ALU.mult, op1=ALU.mult))
                dve.wait_ge(L["rope_rd"], n + 1)
                V.tensor_tensor(proj[:, m, :], proj[:, m, :], rtmp[:, n % 2, :], ALU.add).then_inc(L["rope_r"], 1)

            dve.wait_ge(L["yhi_r"], 1)
            dve.wait_ge(L["lru_d"], 4)
            V.tensor_tensor(oylo[:, 4:8, :], ga[:, :, :], oyhi[:, 4:8, :].bitcast(F32), ALU.subtract
                            ).then_inc(L["oy_r"], 1)
            mix_out(7)
            for m in range(Q0, Q0 + 4):
                rope(m, 0.125)
            mix_out(8)
            mix_out(9)
            for m in range(K0, K0 + 4):
                rope(m, 1.0)

            def nmax(n):
                p, w = n % 2, (n % 4 + 1) * P
                dve.wait_ge(L["qk_r"], n + 1)
                if n >= 2:
                    dve.wait_ge(L["exp_r"], 2 * (n - 1))
                V.tensor_reduce(small[:, 44 + 2 * p:46 + 2 * p], ps[:, 2 * p:2 * p + 2, 0:w], AX.X, ALU.max,
                                negate=True).then_inc(L["nmax_r"], 1)

            def combine(n):
                p, w = n % 2, (n % 4 + 1) * P
                dve.wait_ge(L["exp_r"], 2 * n + 2)
                if n >= 2:
                    dve.wait_ge(L["att_r"], n - 1)
                r1, r2 = 52 + 2 * p, 53 + 2 * p
                st(V.reciprocal(small[:, r1:r2 + 1], small[:, 48 + 2 * p:50 + 2 * p]))
                st(V.tensor_tensor(small[:, r2:r2 + 1], small[:, r2:r2 + 1], small[:, 40:41], ALU.mult))
                if n >= 2:
                    dve.wait_ge(L["attT_r"], n - 1)
                st(V.tensor_scalar(patt[:, p, 0:w], pexp[:, p, 0, 0:w], small[:, r1:r1 + 1], None, ALU.mult))
                V.scalar_tensor_tensor(out=patt[:, p, 0:w], in0=pexp[:, p, 1, 0:w], scalar=small[:, r2:r2 + 1],
                                       in1=patt[:, p, 0:w], op0=ALU.mult, op1=ALU.add).then_inc(L["att_r"], 1)

            nmax(0)
            for n in range(16):
                if n + 1 < 16:
                    nmax(n + 1)
                combine(n)
            dve.wait_ge(L["orst_r"], 2)
            for hd in range(HEADS):
                V.scalar_tensor_tensor(out=osb[:, hd, :], in0=osb[:, hd, :], scalar=small[:, 41:42],
                                       in1=orst[:, hd, :], op0=ALU.mult, op1=ALU.mult).then_inc(L["on_r"], 1)
            for hd in range(HEADS):
                dve.wait_ge(L["ohi_r"], hd + 1)
                V.tensor_tensor(oylo[:, hd, :], osb[:, hd, :], oyhi[:, hd, :].bitcast(F32), ALU.subtract
                                ).then_inc(L["oy_r"], 1)

            def add_to_h(j, bank, k, count):
                tile_wait(k)
                V.tensor_tensor(h[:, 2 * j:2 * j + 2, :], h[:, 2 * j:2 * j + 2, :], TWO(bank), ALU.add
                                ).then_inc(L["h_r"], 1)
                dve.wait_ge(L["h_r"], count)

            for j in range(4):
                add_to_h(j, j % 2, T_OUT + j, j + 1)
                prepare(2, j, C_GMLP, sqmlp)
            norm_recip(2)
            dve.wait_ge(L["phi_r"], 1)
            V.tensor_tensor(plo[:, :, :], pT[:, :, :], phi[:, :, :].bitcast(F32), ALU.subtract).then_inc(L["p_r"], 1)
            for c in range(CHUNKS):
                for j in range(4):
                    n = 4 * c + j
                    tile_wait(T_MLP + 8 * c + j)
                    if n >= 2:
                        dve.wait_ge(L["sqh_r"], 2 * (n - 1))
                    V.scalar_tensor_tensor(out=hm[n % 2][:, :, :], in0=TWO(n % 2), scalar=0.0, in1=rstd2,
                                           op0=ALU.max, op1=ALU.mult).then_inc(L["m_r"], 1)
                    dve.wait_ge(L["sqh_r"], 2 * n + 2)
                    V.tensor_tensor(hidlo[:, 2 * j:2 * j + 2, :], hsq[n % 2][:, :, :],
                                    hidhi[:, 2 * j:2 * j + 2, :].bitcast(F32), ALU.subtract).then_inc(L["hlo_r"], 1)
                for j in range(4):
                    add_to_h(j, j % 2, T_MLP + 8 * c + 4 + j, 4 + 4 * c + j + 1)
                    if c == CHUNKS - 1:
                        prepare(3, j, C_GPLE, sqple)
            norm_recip(3)
            for j in range(4):
                tile_wait(T_GATE + j)
                V.tensor_tensor(gm[j % 2][:, :, :], TWO(j % 2), rstd2, ALU.mult).then_inc(L["g_r"], 1)
                dve.wait_ge(L["gth_r"], j + 1)
                if j == 0:
                    dve.wait_ge(L["pp_r"], 4)
                g = gth[j % 2]
                st(V.scalar_tensor_tensor(out=g[:, :, :], in0=g[:, :, :], scalar=1.0, in1=pp[:, 2 * j:2 * j + 2, :],
                                          op0=ALU.add, op1=ALU.mult))
                st(V.scalar_tensor_tensor(out=h[:, 2 * j:2 * j + 2, :], in0=g[:, :, :], scalar=0.5,
                                          in1=h[:, 2 * j:2 * j + 2, :], op0=ALU.mult, op1=ALU.add))
            dve.wait_ge(L["layer_done"], 2)
            dve.sem_clear(range(lo_num, hi_num + 1))
            dve.sem_inc(layer_go, 1)

        if stage == 1:
            return

        def done_wait(k):
            dve.wait_ge(tile_done, k + (1 + CREDIT))

        def halves(x):
            return x.rearrange("p (a n) -> p a n", a=2)

        st = Chain(dve, d2)
        dve.wait_ge(ld2, 6 * 16)
        st(V.tensor_copy(mask2[:, :, :], masktmp[:, :, :]))

        def recip(n, x):
            dve.wait_ge(n_rt, n)
            V.reciprocal(x, x).then_inc(n_rs, 1)
            dve.wait_ge(n_rs, n)

        recip(1, rstd[:, :])
        for b in range(KB):
            V.scalar_tensor_tensor(out=hres[:, b, CTX:T], in0=h[:, b, :], scalar=p2[:, C2_GF + b:C2_GF + b + 1],
                                   in1=rstd[:, :], op0=ALU.mult, op1=ALU.mult).then_inc(n_x, 1)
        dve.wait_ge(m_ev, 2)
        for i in range(2):
            mb = p2[:, C2_MB + 24 * i:C2_MB + 24 * i + 24].unsqueeze(2).broadcast_to([P, 24, 2])
            st(V.tensor_tensor(modv[i][:, :, :], modsb[:, 24 * i:24 * i + 24, :], mb, ALU.add))

        def norm_gain(i):
            nw = p2[:, C2_NW + 8 * i:C2_NW + 8 * i + 8].unsqueeze(2).broadcast_to([P, KB, 2])
            st(V.tensor_scalar(modA[:, :, :], modv[i][:, 8:16, :], 1.0, None, ALU.add))
            st(V.tensor_tensor(modA[:, :, :], modA[:, :, :], nw, ALU.mult))

        SEG = ((0, CTX, 1), (CTX, T, 0))

        def make_in(i, src):
            def lo(b):
                dve.wait_ge(in_hi, KB * i + b + 1)
                V.tensor_tensor(inlo[:, b, :], tin[:, b % 2, :], inhi[:, b, :].bitcast(F32), ALU.subtract
                                ).then_inc(in_lo, 1)
            for b in range(KB):
                if b >= 2:
                    dve.wait_ge(in_lo, KB * i + b - 1)
                st(V.tensor_tensor(tin[:, b % 2, :], src[:, b, :], rs2[:, :], ALU.mult))
                for t0, t1, c in SEG:
                    ins = V.tensor_scalar(tin[:, b % 2, t0:t1], tin[:, b % 2, t0:t1], modA[:, b, c:c + 1],
                                          modv[i][:, b, c:c + 1], ALU.mult, ALU.add)
                ins.then_inc(in_t, 1)
                if b:
                    lo(b - 1)
            lo(KB - 1)

        norm_gain(0)
        recip(2, rs2[:, :])
        make_in(0, hres)
        for r in raw:
            V.memset(r[:, 0:2], 0.0)
            V.memset(r[:, 2 + CTX:4 + CTX], 0.0)
            ins = V.memset(r[:, 4 + T:6 + T], 0.0)
        ins.then_inc(pads, 1)
        for b in range(4):
            st(V.memset(oacc[:, 2 * b:2 * b + 2, :], 0.0))
        st(V.tensor_scalar(p2[:, C2_CP:C2_CP + 192], p2[:, C2_CP:C2_CP + 192], 0.5, None, ALU.mult))
        dt = Chain(dve, dt_d)
        done_wait(T_DT)
        dt(V.tensor_scalar(halves(dtT[:, :]), ps[0:64, 0:2, 0:HALF], p2[0:64, C2_DTB:C2_DTB + 1], None, ALU.add))
        w = lambda n: dtw[n][:, :, :].rearrange("p c r -> p (c r)")
        dve.wait_ge(dt_p, 1)
        dt(V.tensor_copy(w(0), ps[:, 4, 0:384]))
        dve.wait_ge(dt_a, 3)
        softplus(V, dt, w(2), w(1), w(3), w(4), w(5))
        dt(V.tensor_scalar(w(0), w(0), 0.0, None, ALU.max))
        dt(V.tensor_tensor(w(2), w(2), w(0), ALU.add))
        dt(V.scalar_tensor_tensor(out=tab[:, K_G:K_G + 2 * NC, :].rearrange("p (c d) r -> p c (d r)", d=2),
                                  in0=dtw[2][:, :, :], scalar=-1.0, in1=arow[:, :].unsqueeze(1).broadcast_to([P, NC, 64]),
                                  op0=ALU.mult, op1=ALU.mult))
        assert dt.n == DT_G

        def load_params(g, k):
            k(V.tensor_copy(cpg[:, :], p2[:, bass.ds(g * 24 + C2_CP, 24)]))

        def conv(s, b, k):
            dve.wait_ge(x_rd, s * 4 + (b + 1))
            if not isinstance(s, int):
                dve.wait_ge(pre_ps, s * 6)
                dve.wait_ge(ck_r, s)
            o, r = convd[:, b, 0:CW], raw[b % 2]
            q = lambda n: cpg[:, 6 * b + n:6 * b + n + 1]
            k(V.tensor_scalar(o, r[:, 0:CW], q(0), q(5), ALU.mult, ALU.add))
            for n in range(1, TAPS):
                ins = V.scalar_tensor_tensor(out=o, in0=r[:, n:n + CW], scalar=q(n), in1=o, op0=ALU.mult, op1=ALU.add)
                if n < TAPS - 1:
                    k(ins)
            ins.then_inc(cv_c, 1)

        def silu(s, b):
            dve.wait_ge(cv_t, s * 4 + (b + 1))
            V.scalar_tensor_tensor(out=convd[:, b, 0:CW], in0=raw[b % 2][:, 2:2 + CW], scalar=1.0,
                                   in1=convd[:, b, 0:CW], op0=ALU.add, op1=ALU.mult).then_inc(cv_r, 1)

        load_params(0, st)
        conv(0, 0, st)
        conv(0, 1, st)
        silu(0, 0)
        silu(0, 1)
        conv(0, 2, st)
        dve.wait_ge(dt_p, 2)
        dt(V.tensor_copy(w(3), ps[:, 5, 0:384]))
        dt(V.tensor_copy(w(4), ps[:, 6, 0:384]))
        dt(V.tensor_tensor(w(5), w(4), w(3), ALU.subtract))
        dt(V.tensor_scalar(w(6), w(2), 1e-37, None, ALU.max))
        assert dt.n == DT_C
        dve.wait_ge(dt_a, 5)
        flat = lambda k: tab[:, k:k + 2 * NC, :].rearrange("p c r -> p (c r)")
        dt(V.tensor_tensor(flat(K_NB), w(6), w(3), ALU.subtract))
        dt(V.tensor_tensor(flat(K_TE), w(5), w(2), ALU.mult))
        conv(0, 3, st)
        silu(0, 2)
        silu(0, 3)
        V.memset(acc[:, :], 0.0).then_inc(acc_r2, 1)
        dve.sem_inc(y_rd, 6)
        dve.sem_inc(o_rd, 8)
        dve.wait_ge(spill, 16)

        def group(g, last):
            kt = g * G_TILES + T_G0
            k = Chain(dve, g_step, g * GROUP_STEPS)
            k(V.tensor_copy(mng[:, :], p2[:, bass.ds(g * 2 + C2_MN, 2)]))
            V.tensor_copy(tabg[:, :, :], tab[:, :, bass.ds(g * HPG, HPG)]).then_inc(tabg_r, 1)
            dve.wait_ge(tabg_r, g + 1)
            x4 = lambda c: xcb[:, c, 0:256].rearrange("p (r n) -> p r n", r=HPG)
            for c in range(NC):
                dve.wait_ge(tok_r, g * 6 + (c + 1))
                if c:
                    dve.wait_ge(st_ps, g * 6 + c)
                te = tabg[:, K_TE + 2 * c:K_TE + 2 * c + 2, :].unsqueeze(3).broadcast_to([P, 2, HPG, HD])
                V.tensor_tensor(xte[:, :, :, :], x4(c).unsqueeze(1).broadcast_to([P, 2, HPG, HD]), te, ALU.mult
                                ).then_inc(xte_r, 1)

            def z_gate(b):
                dve.wait_ge(z_t, g * 2 + (b + 1))
                q = 2 - 2 * b
                V.scalar_tensor_tensor(out=halves(zs[:, b, :]), in0=halves(zs[:, b, :]), scalar=1.0,
                                       in1=ps[:, q:q + 2, 0:HALF], op0=ALU.add, op1=ALU.mult).then_inc(z_rd, 1)

            steps = [(0, 1, SLOT_F[0], SLOT_F[1]), (0, 2, SLOT_F[1], SLOT_F[2]), (0, 3, SLOT_F[2], SLOT_F[3]),
                     (0, 4, SLOT_F[3], SLOT_F[4]), (1, 0, SLOT_B[1], SLOT_B[0]), (1, 5, SLOT_B[0], SLOT_B[5]),
                     (1, 4, SLOT_B[5], SLOT_B[4]), (1, 3, SLOT_B[4], SLOT_B[3])]
            z_gate(0)
            dve.wait_ge(sc_r, g * 6 + 6)
            a4 = lambda n: ast[:, n, :].rearrange("p (r n) -> p r n", r=HPG)
            for n, (d, c, before, after) in enumerate(steps):
                dec = tabg[:, K_DEC + 2 * c + d, :].unsqueeze(2).broadcast_to([P, HPG, HD])
                k(V.tensor_tensor(stmp[:, :, :], a4(before), dec, ALU.mult))
                ins = V.tensor_tensor(a4(after), a4(after), stmp[:, :, :], ALU.add)
                if n < len(steps) - 1:
                    k(ins)
            ins.then_inc(scan_r, 1)
            dve.wait_ge(scan_r, g + 1)
            z_gate(1)
            dve.wait_ge(z_rd, g * 2 + 2)

            def chunk(c):
                dve.wait_ge(off_ps, g * 6 + (c + 1))
                if c:
                    dve.wait_ge(y_ps, g * 6 + c)
                ds = [d for d, slot in enumerate((PREV_F[c], PREV_B[c])) if slot is not None]
                n, d0 = len(ds), ds[0]
                ex = tabg[:, K_EXLA + 2 * c + d0:K_EXLA + 2 * c + d0 + n, :].unsqueeze(3).broadcast_to([P, n, HPG, HD])
                src = ps[:, 6, d0 * 256:(d0 + n) * 256].rearrange("p (d r n) -> p d r n", d=n, r=HPG)
                k(V.tensor_tensor(offs[:, 0:n, :, :], src, ex, ALU.mult))
                if n == 2:
                    k(V.tensor_tensor(offs[:, 0, :, :], offs[:, 0, :, :], offs[:, 1, :, :], ALU.add))
                dr = drow[:, bass.ds(g * HPG, HPG)].unsqueeze(2).broadcast_to([P, HPG, HD])
                k(V.tensor_tensor(stmp[:, :, :], x4(c), dr, ALU.mult))
                V.tensor_tensor(offs[:, 0, :, :], offs[:, 0, :, :], stmp[:, :, :], ALU.add).then_inc(offs_r, 1)
                dve.wait_ge(ex_r, g * 6 + (c + 1))
                k(V.tensor_tensor(ebuf[:, 0, :, :], ebuf[:, 0, :, :], ebuf[:, 1, :, :], ALU.add))
                cb = xcb[:, c, 256:384].unsqueeze(1).broadcast_to([P, HPG, P])
                V.tensor_tensor(wdec[:, :, :], ebuf[:, 0, :, :], cb, ALU.mult).then_inc(W_r, 1)
                dve.wait_ge(y_ps, g * 6 + (c + 1))
                z = zs[:, :, c * P:(c + 1) * P]
                V.scalar_tensor_tensor(out=z, in0=ps[:, 7, (c % 2) * 256:(c % 2) * 256 + 256]
                                       .rearrange("p (b n) -> p b n", b=2), scalar=0.5, in1=z,
                                       op0=ALU.mult, op1=ALU.mult).then_inc(y_rd, 1)

            def u_lo(half):
                dve.wait_ge(uh_r, g * 2 + (half + 1))
                for m in range(2):
                    cols = slice(half * HALF, (half + 1) * HALF)
                    ins = V.scalar_tensor_tensor(out=ul[:, m, cols], in0=zs[:, m, cols], scalar=mng[:, m:m + 1],
                                                 in1=uh[:, m, cols].bitcast(F32), op0=ALU.mult, op1=ALU.subtract)
                ins.then_inc(u_r, 1)

            s1 = g + 1
            chunk(0)
            chunk(1)
            if not last:
                load_params(s1, k)
                conv(s1, 0, k)
            chunk(2)
            if not last:
                silu(s1, 0)
                conv(s1, 1, k)
            chunk(3)
            if not last:
                silu(s1, 1)
                conv(s1, 2, k)
            chunk(4)
            if not last:
                silu(s1, 2)
            chunk(5)
            u_lo(0)
            u_lo(1)
            if not last:
                conv(s1, 3, k)
            dve.wait_ge(sqz_r, g + 1)
            k(V.tensor_tensor(acc[:, :], acc[:, :], sqz[:, 0, :], ALU.add))
            V.tensor_tensor(acc[:, :], acc[:, :], sqz[:, 1, :], ALU.add).then_inc(acc_r2, 1)
            if not last:
                silu(s1, 3)
            blk = g * 10 + (3 if last else 5)
            for j in range(KB):
                if j < KB - 1:
                    dve.wait_ge(blk_ps, blk + j + 1)
                else:
                    done_wait(kt + (1 if last else 3))
                q = 2 - 2 * (j % 2)
                V.tensor_tensor(halves(oacc[:, j, :]), halves(oacc[:, j, :]), ps[:, q:q + 2, 0:HALF], ALU.add
                                ).then_inc(o_rd, 1)
            dve.wait_ge(o_rd, g * 8 + 16)
            dve.wait_ge(acc_r2, g + 2)
            if not last:
                assert k.n == GROUP_STEPS, k.n

        with dve.Fori(0, GROUPS - 1) as g:
            group(g, False)
        group(GROUPS - 1, True)

        recip(3, rs2[:, :])
        dve.wait_ge(spill, 32)
        for b in range(KB):
            st(V.tensor_tensor(oacc[:, b, :], oacc[:, b, :], rs2[:, :], ALU.mult))
            for t0, t1, c in SEG:
                ins = V.scalar_tensor_tensor(out=oacc[:, b, t0:t1], in0=oacc[:, b, t0:t1], scalar=modv[0][:, 16 + b, c:c + 1],
                                             in1=hback[:, b, t0:t1], op0=ALU.mult, op1=ALU.add)
            ins.then_inc(n_x, 1)
        dve.wait_ge(n_x, 2 * KB)
        norm_gain(1)
        recip(4, rs2[:, :])
        make_in(1, oacc)
        dve.wait_ge(rsh_r, 1)
        for m in range(2):
            ins = V.scalar_tensor_tensor(out=kf[:, m, :], in0=kf[:, m, :], scalar=p2[:, C2_KN:C2_KN + 1],
                                         in1=ksq[:, m, :], op0=ALU.mult, op1=ALU.mult)
        ins.then_inc(qn_r, 1)
        for n in range(2):
            dve.wait_ge(rsh_r, 2 + n)
            V.scalar_tensor_tensor(out=qb_[:, 4 * n:4 * n + 4, :], in0=qb_[:, 4 * n:4 * n + 4, :],
                                   scalar=p2[:, C2_QN:C2_QN + 1], in1=qsq[:, 4 * n:4 * n + 4, :],
                                   op0=ALU.mult, op1=ALU.mult).then_inc(qn_r, 1)
        dve.wait_ge(qn_r, 3)
        for j in range(4):
            dve.wait_ge(g_t, j + 1)
            x = gs[:, 2 * j:2 * j + 2, :]
            V.scalar_tensor_tensor(out=x, in0=x, scalar=1.0, in1=TWO(j % 2), op0=ALU.add, op1=ALU.mult
                                   ).then_inc(g_rd, 1)
        for n in range(10):
            x, f = (kf[:, n, CTX:T], 1.0) if n < 2 else (qb_[:, n - 2, :], HD ** -0.5)
            dve.wait_ge(rp_ps, n + 1)
            V.scalar_tensor_tensor(out=rt2[:, n % 2, :], in0=ps[:, 4 + n % 4, :], scalar=f, in1=sinT[:, :],
                                   op0=ALU.mult, op1=ALU.mult).then_inc(rp_rd, 1)
            st(V.scalar_tensor_tensor(out=x, in0=x, scalar=f, in1=cosT[:, :], op0=ALU.mult, op1=ALU.mult))
            dve.wait_ge(rp_rd, n + 1)
            V.tensor_tensor(x, x, rt2[:, n % 2, :], ALU.add).then_inc(rp_r, 1)
            if n >= 1:
                dve.wait_ge(rp_r, n)
        dve.wait_ge(rp_r, 10)
        dve.wait_ge(vt_r, NC)
        st(V.memset(vaug[:, :, 64:128], 1.0))
        for x in K2:
            st(V.memset(x[64:128, :].bitcast(F32), 0.0))
            st(V.memset(x[64:65, :].bitcast(F32), 1.0))
            st(V.memset(x[96:97, :].bitcast(F32), 1.0))

        with dve.Fori(0, 2) as i:
            k = Chain(dve, h_step, i * HEAD_STEPS)
            for j in range(2):
                dve.wait_ge(k_hi, i * 2 + (j + 1))
                V.tensor_tensor(K1[j][64:128, :], kk[:, :], K1[j][0:64, :].bitcast(F32), ALU.subtract
                                ).then_inc(k_lo, 1)

            def q_split(hq):
                p = hq % 2
                dve.wait_ge(q_hi, i * 8 + (hq + 1))
                V.tensor_tensor(Q2[p][0:64, :], qq[:, :], Q1[p][0:64, :].bitcast(F32), ALU.subtract
                                ).then_inc(q_lo, 1)

            def maxima(hq):
                p = hq % 2
                if hq > 1:
                    dve.wait_ge(mx_ps, i * 8 + (hq - 1))
                for t in range(4):
                    dve.wait_ge(s_ps, i * 32 + (4 * hq + t + 1))
                    q = 2 * (t % 2)
                    V.tensor_reduce(nmx[:, p, t, :], ps[:, q:q + 2, 0:HALF], AX.X, ALU.max).then_inc(mx_r, 1)
                dve.wait_ge(mx_r, i * 32 + (4 * hq + 4))
                V.tensor_reduce(nm4[:, p, :], nmx[:, p, :, :], AX.X, ALU.max, negate=True).then_inc(mxf_r, 1)
                dve.wait_ge(mxf_r, i * 8 + (hq + 1))

            def gated(b):
                dve.wait_ge(o_ev, i * 8 + (2 * b + 2))
                x = qb_[:, bass.ds(i * 4 + b, 1), :].rearrange("p a n -> p (a n)")
                g = gs[:, bass.ds(i * 4 + b, 1), :].rearrange("p a n -> p (a n)")
                k(V.reciprocal(osum[:, :], osum[:, :]))
                k(V.tensor_tensor(x, x, osum[:, :], ALU.mult))
                V.scalar_tensor_tensor(out=x, in0=x, scalar=0.5, in1=g, op0=ALU.mult, op1=ALU.mult).then_inc(oy2, 1)

            def o_lo(b):
                dve.wait_ge(oh_r, i * 4 + (b + 1))
                sl = bass.ds(i * 4 + b, 1)
                V.tensor_tensor(olo[:, sl, :], qb_[:, sl, :], ohi[:, sl, :].bitcast(F32), ALU.subtract).then_inc(ol_r, 1)

            q_split(0)
            maxima(0)
            for hq in range(8):
                p = hq % 2
                if hq + 1 < 8:
                    q_split(hq + 1)
                dve.wait_ge(mxh_r, i * 8 + (hq + 1))
                V.tensor_tensor(Q2[p][96:128, :], ps[96:128, 4, :], Q2[p][96:128, :].bitcast(F32), ALU.subtract
                                ).then_inc(mxl_r, 1)
                if hq + 1 < 8:
                    maxima(hq + 1)
                if hq % 2 == 0 and hq:
                    gated(hq // 2 - 1)
                if hq % 2 == 1 and hq > 1:
                    o_lo(hq // 2 - 1)
            gated(3)
            o_lo(3)
            dve.wait_ge(ol_r, i * 4 + 4)
            assert k.n == HEAD_STEPS, k.n

        for j in range(4):
            done_wait(T_ATT + 10 + j)
            for m in range(2):
                b = 2 * j + m
                ins = V.scalar_tensor_tensor(out=oacc[:, b, CTX:T], in0=ps[:, 2 * (j % 2) + m, :],
                                             scalar=modv[1][:, 16 + b, 0:1], in1=oacc[:, b, CTX:T],
                                             op0=ALU.mult, op1=ALU.add)
            ins.then_inc(hf_r, 1)
        dve.wait_ge(hf_r, 4)
        recip(5, rs5[:, :])
        for b in range(KB):
            V.scalar_tensor_tensor(out=hfin[:, b, :], in0=oacc[:, b, CTX:T], scalar=p2[:, C2_FN + b:C2_FN + b + 1],
                                   in1=rs5[:, :], op0=ALU.mult, op1=ALU.mult).then_inc(fin, 1)

    ctx.close()


D_ANGLE, D_SILU, INIT_D, INIT_A = 11, 13, 17, 5
CST = 16 * 8
DT_G, DT_C = 18, 22
GROUP_STEPS, HEAD_STEPS = 56, 8


def softplus(V, st, out, e, z, z2, p):
    st(V.tensor_scalar(z, e, 2.0, None, ALU.add))
    st(V.reciprocal(z, z))
    st(V.tensor_tensor(z, z, e, ALU.mult))
    st(V.tensor_tensor(z2, z, z, ALU.mult))
    st(V.tensor_scalar(p, z2, 1.0 / 15, None, ALU.mult))
    for n in (13, 11, 9, 7, 5, 3):
        st(V.scalar_tensor_tensor(out=p, in0=p, scalar=1.0 / n, in1=z2, op0=ALU.add, op1=ALU.mult))
    st(V.scalar_tensor_tensor(out=p, in0=p, scalar=1.0, in1=z, op0=ALU.add, op1=ALU.mult))
    st(V.tensor_scalar(out, p, 2.0, None, ALU.mult))


def cut(w):
    k, m = w.shape
    w = w.reshape(k // D, KB, P, m // TM, TM).transpose(0, 3, 2, 1, 4)
    return w.reshape(-1, P, TILE)


def cut_wide(w):
    k, m = w.shape
    return w.reshape(k // TM, 2, P, m).transpose(0, 2, 1, 3).reshape(-1, P, TILE)


def columns(v):
    return v.reshape(-1, P).T


def feature_major(x):
    return np.ascontiguousarray(x.T.reshape(-1, P, x.shape[0]).transpose(1, 0, 2))


def consts():
    c = np.zeros((P, 400), np.float32)
    c[:, 0:128] = np.eye(P)
    for half in (0, 64):
        for i in range(ROT // 2):
            c[half + i, 128 + half + 8 + i] = 1
            c[half + 8 + i, 128 + half + i] = 1
            inv = np.float32(500000.0) ** (-np.float32(i) * np.float32(2.0) / np.float32(ROT))
            c[half + i, 257] = c[half + 8 + i, 257] = inv
            c[half + i, 259], c[half + 8 + i, 259] = -1, 1
    c[:, 256] = EPS
    c[:, 258] = math.pi / 2
    c[:, 272:400] = np.where(np.arange(P)[None, :] > np.arange(P)[:, None], -1e30, 0)
    return c


def layer_tiles(i, l, mods):
    w_in = i["w_in"][l]
    w_in = np.concatenate([w_in[:, 1536:2560], w_in[:, 0:1536]], 1)
    mix, out = cut(w_in), cut(i["w_out"][l])
    up = cut(i["w_mlp_in"][l]).reshape(CHUNKS, 4, P, TILE)
    down = cut(i["w_mlp_out"][l]).reshape(CHUNKS, 4, P, TILE)
    first = np.stack([mix, mods[0:MIX_TILES]], 1).reshape(-1, P, TILE)
    mlp = np.stack([up, down], 1).reshape(-1, P, TILE)
    return [first, out, mods[MIX_TILES:MOD_IN_LAYER], mlp, cut_wide(i["w_ple_proj"][l]), cut(i["w_ple_gate"][l])]


def layer_params(i, l):
    t = np.zeros((P, NLP), np.float32)
    for c, name in ((C_GMIX, "g_mix"), (C_GMLP, "g_mlp"), (C_GPLE, "g_ple"), (C_CB, "conv_b"), (C_BA, "b_gate_a"),
                    (C_BX, "b_gate_x"), (C_LRU, "lru_lambda"), (C_GSUB, "g_subln")):
        v = columns(i[name][l])
        t[:, c:c + v.shape[1]] = v
    for tap in range(4):
        t[:, C_CW + 4 * tap:C_CW + 4 * tap + 4] = columns(i["conv_w"][l, tap])
    for c, name in ((C_LQ, "lam_q"), (C_LK, "lam_k")):
        for n in range(2):
            t[64 * n:64 * n + 64, c + n] = i[name][l, n]
    lam_init = 0.8 - 0.6 * math.exp(-0.3 * l)
    t[:, C_LI], t[:, C_1LI] = lam_init, 1.0 - lam_init
    return t


def gate_blocks(i, l):
    t = np.zeros((P, 8, P), np.float32)
    for n, name in enumerate(("w_gate_a", "w_gate_x")):
        for g in range(8):
            r = 64 * (g % 2)
            t[r:r + 64, 4 * n + g // 2, r:r + 64] = i[name][l, g]
    return t


def second_tiles(i, mods):
    w, out = i["m_in_w_2"][0], cut_wide(i["m_out_w_2"][0])
    conv0 = MDI
    b0, c0, dt0 = 2 * MDI, 2 * MDI + GROUPS * NS, 2 * MDI + 2 * GROUPS * NS
    dt = np.zeros((1, P, TILE), np.float32)
    dt[0, :, 0:KB * 64] = w[:, dt0:].reshape(KB, P, 64).transpose(1, 0, 2).reshape(P, KB * 64)
    z = lambda g: cut(w[:, 256 * g:256 * g + 256])
    x = lambda g: cut(w[:, conv0 + 256 * g:conv0 + 256 * g + 256])
    bc = lambda g: cut(np.concatenate([w[:, b0 + NS * g:b0 + NS * (g + 1)], w[:, c0 + NS * g:c0 + NS * (g + 1)]], 1))
    tiles = [mods[2 * MOD_IN_LAYER:], dt, x(0), bc(0)]
    for g in range(GROUPS):
        tiles.append(z(g))
        if g + 1 < GROUPS:
            tiles += [x(g + 1), bc(g + 1)]
        tiles.append(out[g:g + 1])
    a = i["a_in_w_2"][0]
    a = np.concatenate([a[:, D:D + 512], a[:, 0:D], a[:, D + 512:]], 1)
    tiles += [cut(a), cut(i["a_out_w_2"][0])]
    n = sum(len(t) for t in tiles)
    if n % 2:
        tiles.append(np.zeros((1, P, TILE), np.float32))
    return tiles


def params2(i):
    t = np.zeros((P, NP2), np.float32)
    for c, v in ((C2_GF, i["g_final"]), (C2_NW, i["norm_w_2"].reshape(-1)), (C2_MB, i["mod_b_2"].reshape(-1)),
                 (C2_FN, i["final_norm_w_2"]), (C2_MN, i["m_norm_w_2"][0])):
        v = columns(v)
        t[:, c:c + v.shape[1]] = v
    taps = np.concatenate([i["m_conv_w_2"][0], i["m_conv_b_2"]])
    cols = np.stack([columns(v) for v in taps], 2)
    for g in range(GROUPS):
        for n, b in enumerate((2 * g, 2 * g + 1, 2 * GROUPS + g, 3 * GROUPS + g)):
            c = C2_CP + 24 * g + 6 * n
            t[:, c:c + 6] = cols[:, b]
    t[0:64, C2_DTB] = i["m_dt_bias_2"][0].reshape(-1)
    t[:, C2_QN] = np.tile(i["a_q_norm_2"][0], 2)
    t[:, C2_KN] = np.tile(i["a_k_norm_2"][0], 2)
    return t


def consts2():
    c = np.zeros((P, 768), np.float32)
    a, b = np.arange(P)[:, None], np.arange(P)[None, :]
    c[:, 0:128] = a <= b
    c[:, 128:256] = a >= b
    c[:, 256:384] = np.where(a <= b, 0, -1e30)
    c[:, 384:512] = np.where(a >= b, 0, -1e30)
    c[:, 512:640] = a // 64 == b // 64
    c[:, 640:768] = (a ^ 16) == b
    return c


def axial():
    half = 32
    inv = np.float32(10000.0) ** (-np.arange(0, half, 2, dtype=np.float32) / np.float32(half))
    d = np.arange(P) % 64
    t = np.arange(S)
    pos = np.where((d // 32 == 0)[:, None], (t // 64)[None, :], (t % 64)[None, :]).astype(np.float32)
    ang = pos * inv[d % 16][:, None]
    sign = np.where(d % 32 < 16, -1, 1)[:, None]
    return np.stack([np.cos(ang), sign * np.sin(ang)]).astype(np.float32)


def host_arrays(i):
    i = {k: np.asarray(v) for k, v in i.items()}
    mods = np.concatenate([cut(i["mod_w_2"][0]), cut(i["mod_w_2"][1])])
    tiles = []
    for l in range(DEPTH):
        tiles += layer_tiles(i, l, mods[l * MOD_IN_LAYER:(l + 1) * MOD_IN_LAYER])
    a = {
        "wstream": tiles,
        "x": feature_major(i["x"][0]),
        "positions": i["positions"].reshape(S),
        "cvec": np.ascontiguousarray(np.stack([columns(i["c_2"][0]), columns(i["c_ctx_2"])], 2)),
        "lparams": np.ascontiguousarray(np.stack([layer_params(i, l) for l in range(DEPTH)], 1)),
        "gates": np.stack([gate_blocks(i, l) for l in range(DEPTH)]),
        "pT": np.stack([feature_major(i["p"][l, 0]) for l in range(DEPTH)]),
        "consts": consts(),
        "ctx": feature_major(i["ctx_2"][0]),
        "m_d": i["m_d_2"][0],
        "m_a_log": i["m_a_log_2"][0].reshape(-1),
        "params2": params2(i),
        "consts2": consts2(),
        "axial": axial(),
    }
    tiles += second_tiles(i, mods)
    a["wstream"] = np.concatenate(a["wstream"])
    return a


def kernel(**inputs):
    import concourse.bacc as bacc
    from concourse.bass_utils import run_bass_kernel_spmd

    arrays = host_arrays(inputs)
    nc = bacc.Bacc("TRN2", target_bir_lowering=False, num_devices=1)
    io = {n: nc.dram_tensor(f"in_{n}", a.shape, mybir.dt.from_np(a.dtype), kind="ExternalInput").ap()
          for n, a in arrays.items()}
    io["out"] = nc.dram_tensor("out", (P, KB, S), F32, kind="ExternalOutput").ap()
    build(nc, io)
    r = run_bass_kernel_spmd(nc, [{f"in_{n}": a for n, a in arrays.items()}], core_ids=[0])
    out = r.results[0]["out"]
    return np.ascontiguousarray(out.transpose(2, 1, 0).reshape(1, S, D))
```

```python
import math
from contextlib import ExitStack

import numpy as np
import concourse.bass as bass
from concourse import mybir

F32 = mybir.dt.float32
F32R = mybir.dt.float32r
BF16 = mybir.dt.bfloat16
I32 = mybir.dt.int32
ALU = mybir.AluOpType
ACT = mybir.ActivationFunctionType
AX = mybir.AxisListType

P = 128
DEPTH = 2
D = 1024
KB = D // P
S = 512
TILE = 2048
TM = 256
EPS = 1e-6

HEADS = 4
ROT = 16
DFF = 4096
CHUNKS = DFF // D
MIX_TILES = 10
MODS = 3 * D // P
LAYER_TILES = MIX_TILES + 4 + 8 * CHUNKS + 1 + 4 + 1
C_GMIX, C_GMLP, C_GPLE, C_GSUB, C_CW, C_CB, C_BA, C_BX, C_LRU, C_LQ, C_LK, C_LI, C_1LI = (
    0, 8, 16, 24, 25, 41, 45, 49, 53, 57, 59, 61, 62)
NLP = 63
XR, GR, Q0, K0, V0 = 0, 4, 8, 12, 16
CTX = 256
T = CTX + S
HALF = T // 2
GROUPS, HPG, HD, NS = 8, 4, 64, 128
MDI = GROUPS * HPG * HD
CHUNK = 128
NC = T // CHUNK
CTX_CHUNKS = CTX // CHUNK
TAPS, CW = 5, T + 2
KVH, REP = 4, 4
T_LAYERS = DEPTH * LAYER_TILES
T_DT, T_XS0, T_BC0, T_G0 = (T_LAYERS + n for n in range(4))
G_TILES = 4
T_ATT = T_G0 + G_TILES * GROUPS - 2
C2_GF, C2_NW, C2_MB, C2_FN, C2_CP, C2_MN, C2_DTB, C2_QN, C2_KN = 0, 8, 24, 72, 80, 272, 288, 289, 290
NP2 = 291
K_G, K_NB, K_EXLA, K_TE, K_DEC = (2 * NC * n for n in range(5))
TWO_PI_1, TWO_PI_2 = 6.28125, 0.0019350051879882812
TWO_PI_3 = 2 * math.pi - TWO_PI_1 - TWO_PI_2
MAGIC = 12582912.0


def sbuf_map(nc, top):
    base = 16 * 1024 + 128
    def at(name, kib, shape, dt=F32):
        return nc.alloc_sbuf_tensor_at(name, shape, dt, offset=base + int(kib * 1024))
    return at


class Chain:

    def __init__(self, eng, sem, base=0):
        self.eng, self.sem, self.base, self.n = eng, sem, base, 0

    def __call__(self, ins):
        self.n += 1
        ins.then_inc(self.sem, 1)
        self.eng.wait_ge(self.sem, self.base + self.n)


def build(nc, io, stage=2):
    NT = io["wstream"].shape[0]
    at = sbuf_map(nc, None)

    wraw = at("wraw", 0, [P, 2, TILE])
    whi = at("whi", 16, [P, 2, TILE], F32R)
    wlo = at("wlo", 32, [P, 2, TILE], F32R)
    h = at("h", 48, [P, KB, S])
    uhi = at("uhi", 64, [P, KB, S], F32R)
    ulo = at("ulo", 80, [P, KB, S], F32R)
    proj = at("proj", 96, [P, 20, S])
    hidhi = at("hidhi", 96, [P, KB, S], F32R)
    hidlo = at("hidlo", 112, [P, KB, S], F32R)
    phi = at("phi", 128, [P, 2, S], F32R)
    plo = at("plo", 132, [P, 2, S], F32R)
    oyhi = at("oyhi", 136, [P, KB, S], F32R)
    oylo = at("oylo", 152, [P, KB, S], F32R)
    pp = at("pp", 168, [P, KB, S])
    modraw = at("modraw", 184, [P, KB, P])
    pT = at("pT", 184, [P, 2, S])
    gw = at("gw", 188, [P, 8, P])
    acc2 = at("acc2", 192, [P, 2, S])
    rstd = at("rstd", 196, [P, S])
    ropeC = at("ropeC", 198, [P, S])
    ropeS = at("ropeS", 200, [P, S])
    ident = at("ident", 202, [P, P])
    rperm = at("rperm", 202.5, [P, P])
    ones = at("ones", 203, [P, P])
    identb = at("identb", 203.5, [P, P], BF16)
    maskb = at("maskb", 203.75, [P, P], BF16)
    lpall = at("lpall", 204, [P, DEPTH, NLP])
    lp = at("lp", 204.5, [P, NLP])
    small = at("small", 204.75, [P, 64])
    modsb = at("modsb", 205, [P, 48, 2])
    cvec = at("cvec", 205.375, [P, KB, 2])
    misc = at("misc", 206.75, [P, 16])
    modrow = at("modrow", 206.8125, [2, P])
    xc = at("xc", 136, [P, 4, S])
    gi = at("gi", 152, [P, 4, S])
    asq = at("asq", 160, [P, 4, S])
    ga = at("ga", 168, [P, 4, S])
    gt = at("gt", 176, [P, 4, S])
    vtok = at("vtok", 64, [P, 4, S])
    pexp = at("pexp", 72, [P, 2, 2, S])
    patt = at("patt", 80, [P, 2, S])
    pattT = at("pattT", 84, [P, 2, S])
    osb = at("osb", 88, [P, HEADS, S])
    osq = at("osq", 128, [P, HEADS, S])
    orst = at("orst", 136, [P, HEADS, S])
    rtmp = at("rtmp", 192, [P, 2, S])
    sqmlp = at("sqmlp", 168, [P, 2, S])
    sqple = at("sqple", 136, [P, 2, S])
    hm = [at(f"hm{i}", 168 + 4 * i, [P, 2, S]) for i in range(2)]
    hsq = [at(f"hsq{i}", 176 + 4 * i, [P, 2, S]) for i in range(2)]
    gm = [at(f"gm{i}", 96 + 4 * i, [P, 2, S]) for i in range(2)]
    gth = [at(f"gth{i}", 104 + 4 * i, [P, 2, S]) for i in range(2)]
    posi = at("posi", 96, [P, S], I32)
    maskf = at("maskf", 104, [P, P])
    angt = [at(f"angt{i}", 98 + 2 * i, [P, S]) for i in range(3)]

    inhi = at("inhi", 48, [P, KB, T], F32R)
    inlo = at("inlo", 72, [P, KB, T], F32R)
    oacc = at("oacc", 96, [P, KB, T])
    hres = at("hres", 144, [P, KB, T])
    sqb = at("sqb", 120, [P, KB, T])
    tin = at("tin", 168, [P, 2, T])
    masktmp = at("masktmp", 174, [P, 2, P])
    convd = at("convd", 120, [P, 4, 772])
    ck = at("ck", 132.125, [P, T])
    raw = [at(f"raw{i}", 135.125 + 3.125 * i, [P, 776]) for i in range(2)]
    zs = at("zs", 141.375, [P, 2, T])
    uh = at("uh", 147.375, [P, 2, T], F32R)
    ul = at("ul", 153.375, [P, 2, T], F32R)
    ast = at("ast", 159.375, [P, 10, 256])
    xcb = at("xcb", 169.375, [P, NC, 384])
    sqz = at("sqz", 169.375, [P, 2, T])
    ebuf = at("ebuf", 178.375, [P, 2, HPG, P])
    btok = at("btok", 178.375, [P, NC, NS])
    xte = at("xte", 147.375, [P, NC, 2, HPG, HD])
    wdec = at("wdec", 184.375, [P, HPG, P])
    offs = at("offs", 186.375, [P, 2, HPG, HD])
    stmp = at("stmp", 188.375, [P, HPG, HD])
    acc = at("acc", 189.375, [P, T])
    rs2 = at("rs2", 186.375, [P, T])
    tab = at("tab", 192.375, [P, 10 * NC, 32])
    triF = at("triF", 199.875, [P, P])
    triB = at("triB", 200.375, [P, P])
    drow = at("drow", 200.875, [P, 32])
    modv = [at(f"modv{i}", 201 + 0.1875 * i, [P, 24, 2]) for i in range(2)]
    modA = at("modA", 201.375, [P, KB, 2])
    arow = at("arow", 201.5, [P, 64])
    mask2 = at("mask2", 202.5, [P, 2, P], BF16)
    p2 = at("p2", 203.75, [P, NP2])
    tabg = at("tabg", 205.5, [P, 10 * NC, HPG])
    cpg = at("cpg", 206.4375, [P, 24])
    mng = at("mng", 206.5625, [P, 2])
    dtw = [at(f"dtw{i}", 174 + 1.5 * i, [P, NC, 64]) for i in range(8)]
    dtT = at("dtT", 171, [64, T])
    qb_ = at("qb", 120, [P, KB, S])
    kf = at("kf", 136, [P, 2, T])
    vf = at("vf", 142, [P, 2, T])
    gs = at("gs", 148, [P, KB, S])
    qsq = at("qsq", 164, [P, KB, S])
    ksq = at("ksq", 180, [P, 2, T])
    cosT = at("cosT", 190, [P, S])
    sinT = at("sinT", 192, [P, S])
    rt2 = at("rt2", 194, [P, 2, S])
    bones = at("bones", 198, [P, P])
    perm2 = at("perm2", 198.5, [P, P])
    ohi = at("ohi", 48, [P, KB, S], F32R)
    olo = at("olo", 64, [P, KB, S], F32R)
    vtok2 = at("vtok2", 80, [P, NC, 256])
    vaug = at("vaug", 86, [P, NC, P])
    kk = at("kk", 89, [64, T])
    nmx = at("nmx", 92, [P, 2, 4, 2])
    nm4 = at("nm4", 92.125, [P, 2, 4])
    K1 = [at(f"K1{i}", 164 + 6 * i, [P, T], F32R) for i in range(2)]
    K2 = [at(f"K2{i}", 167 + 6 * i, [P, T], F32R) for i in range(2)]
    Q1 = [at(f"Q1{i}", (176, 180, 142)[i], [P, S], F32R) for i in range(3)]
    Q2 = [at(f"Q2{i}", (178, 182, 144)[i], [P, S], F32R) for i in range(3)]
    qq = at("qq", 92.5, [64, S])
    pT2 = at("pT2", 184, [P, NC, S])
    osum = at("osum", 196, [P, S])
    hback = at("hback", 120, [P, KB, T])
    sq4 = at("sq4", 144, [P, KB, T])
    rs5 = at("rs5", 190, [P, S])
    hfin = at("hfin", 120, [P, KB, S])

    hspill = nc.dram_tensor("hspill", (P, KB, T), F32, kind="Internal").ap() if stage > 1 else None

    ps = nc.alloc_psum_tensor("ps", [P, 8, 512], F32)
    TWO = lambda s: ps[:, 2 * s:2 * s + 2, :]

    def sem(name):
        return nc.alloc_semaphore(name)

    wfree, wsplit, tile_done, pool_go, wraw_read = (sem(n) for n in (
        "wfree", "wsplit", "tile_done", "pool_go", "wraw_read"))
    wland = [sem(f"wland{i}") for i in range(2)]
    cst = sem("cst_loaded")
    init_a, init_d = sem("init_a"), sem("init_d")
    layer_go = sem("layer_go")
    lw = [sem(f"layer_weights{i}") for i in range(2)]
    LN = ["lp_copied", "lsp", "lsa", "dots_r", "lam_r", "uhi_r", "ulo_r", "sq_r", "acc_r", "ssq_r", "sqrt_r", "rstd_r",
          "h_r", "d_step", "a_step", "mod_dma", "mod_ps", "mod_row", "mod_T", "mod_ev", "proj_r", "xc_r", "gate_ps", "gate_t", "lru_a",
          "lru_d", "rope_ps", "rope_rd", "rope_r", "v_ps", "v_r", "qk_r", "nmax_r", "exp_r", "att_r", "attT_r",
          "attTc", "pv_r", "o_r", "oss_r", "orst_r", "on_r", "ohi_r", "oy_r", "yhi_r", "m_r", "sqh_r", "hlo_r",
          "pp_ps", "phi_r", "p_r", "pp_r", "g_r", "gth_r", "layer_done"]
    Ls = {n: sem("L_" + n) for n in LN}
    lo_num, hi_num = Ls[LN[0]].num, Ls[LN[-1]].num
    assert hi_num - lo_num == len(LN) - 1
    out_s = sem("out_stored")
    ld2, ldc, spill, ld3, ldm = sem("params2_loaded"), sem("ctx_loaded"), sem("residual_dma"), sem("att_tables"), sem("d_loaded")
    a2, d2 = sem("act_step2"), sem("dve_step2")
    n_sq, n_ss, n_rt, n_rs, n_x = sem("norm_squares"), sem("norm_sums"), sem("norm_root"), sem("norm_rstd"), sem("norm_x")
    in_v = sem("in_scaled")
    in_t, in_hi, in_lo = sem("in_normed"), sem("in_hi"), sem("in_lo")
    dt_p, dt_a, dt_d = sem("dt_pe"), sem("dt_act"), sem("dt_dve")
    blk_ps = sem("block_sums")
    z_t, z_rd, x_rd, o_rd = sem("z_tanh"), sem("z_read"), sem("conv_in_read"), sem("out_read")
    cv_c, cv_t, cv_r, pads = sem("conv_done"), sem("conv_tanh"), sem("conv_silu"), sem("pads_zero")
    pre_ps, tok_r, ck_r, tabg_r = sem("tokens_turned"), sem("tokens_held"), sem("C_held"), sem("group_tables")
    xte_r, st_ps, sc_r, scan_r = sem("x_to_end"), sem("chunk_states"), sem("states_held"), sem("states_scanned")
    la_ps, ex_r, off_ps, offs_r = sem("log_decay"), sem("decay"), sem("off_sums"), sem("off_held")
    W_r, y_ps, y_rd = sem("weights_ready"), sem("y_sums"), sem("y_read")
    uh_r, u_r, sqz_r, acc_r2 = sem("u_hi"), sem("u_ready"), sem("y_squares"), sem("y_squares_added")
    a_rd, g_t, g_rd, ln_r, rsh_r = sem("kvq_read"), sem("g_tanh"), sem("g_read"), sem("head_log"), sem("head_rstd")
    qn_r, rp_ps, rp_rd, rp_r = sem("qk_normed"), sem("rope2_sums"), sem("rope2_read"), sem("rope2_done")
    ssh, vt_ps, vt_r = sem("head_sums"), sem("v_turned"), sem("v_held")
    k_hi, k_lo, q_hi, q_lo, va_r = sem("k_hi"), sem("k_lo"), sem("q_hi"), sem("q_lo"), sem("v_of_head")
    s_ps, mx_r, mx_ps, mxh_r, mxl_r = sem("scores"), sem("max_ready"), sem("max_row"), sem("max_hi"), sem("max_lo")
    sT_ps, p_r2, o_ps, o_ev, oy2 = sem("scoresT"), sem("probs"), sem("head_out"), sem("head_out_read"), sem("o_gated")
    oh_r, ol_r, hf_r, fin = sem("o_hi"), sem("o_lo"), sem("final_h"), sem("final_out")

    g_step, h_step = sem("group_step"), sem("heads_step")
    act_go = sem("act_go")
    mxf_r = sem("head_max_ready")
    SLOT_F = {0: 0, 1: 1, 2: 2, 3: 3, 4: 4}
    SLOT_B = {0: 5, 1: 6, 3: 7, 4: 8, 5: 9}
    PREV_F = [None, 0, 1, 2, 3, 4]
    PREV_B = [SLOT_B[1], None, SLOT_B[3], SLOT_B[4], SLOT_B[5], SLOT_B[0]]

    CREDIT = 2

    def first_tile(l):
        return l * LAYER_TILES

    block = nc.Block()
    ctx = ExitStack()
    ctx.enter_context(block)

    @block.sync
    def _(sp):
        for dst, name in ((h, "x"), (cvec, "cvec"), (lpall, "lparams")):
            sp.dma_start(dst[:, :, :], io[name]).then_inc(cst, 16)
        for dst, a, b in ((ident, 0, 128), (rperm, 128, 256), (misc, 256, 272), (maskf, 272, 400)):
            sp.dma_start(dst[:, :], io["consts"][:, a:b]).then_inc(cst, 16)
        sp.dma_start(posi[:, :], io["positions"].partition_broadcast(P)).then_inc(cst, 16)
        with sp.Fori(0, NT // 2) as i:
            for s in range(2):
                sp.wait_ge(wfree, i * 2 + (s + 1))
                sp.dma_start(wraw[:, s, :], io["wstream"][bass.ds(i * 2 + s, 1), :, :].rearrange("a p n -> p (a n)")
                             ).then_inc(wland[s], 16)
        if stage == 1:
            sp.wait_ge(layer_go, DEPTH)
            sp.dma_start(io["out"], h[:, :, :]).then_inc(out_s, 16)
            sp.wait_ge(out_s, 16)
        else:
            for j in range(2):
                sp.wait_ge(fin, 4 * j + 4)
                sp.dma_start(io["out"][:, 4 * j:4 * j + 4, :], hfin[:, 4 * j:4 * j + 4, :]).then_inc(out_s, 16)
            sp.wait_ge(out_s, 32)

    @block.gpsimd
    def _(pool):
        pool.sem_inc(wfree, CREDIT)
        with pool.Fori(0, NT // 2) as i:
            for s in range(2):
                pool.wait_ge(wland[s], i * 16 + 16)
                pool.wait_ge(tile_done, i * 2 + (s + 1))
                pool.sem_inc(pool_go, 1)
                pool.tensor_scalar(whi[:, s, :], wraw[:, s, :], 1.0, 0.0, ALU.mult, ALU.add).then_inc(wraw_read, 1)
                pool.wait_ge(wraw_read, i * 2 + (s + 1))
                pool.tensor_tensor(wlo[:, s, :], wraw[:, s, :], whi[:, s, :].bitcast(F32), ALU.subtract
                                   ).then_inc(wsplit, 1)
                pool.wait_ge(wsplit, i * 2 + (s + 1))
                pool.sem_inc(wfree, 1)

    T_OUT, T_MLP = MIX_TILES, MIX_TILES + 4
    MOD_AT = 4
    T_PP = T_MLP + 8 * CHUNKS
    T_GATE = T_PP + 1

    @block.tensor
    def _(pe):
        L = Ls
        pe.sem_inc(tile_done, CREDIT)
        pe.wait_ge(init_d, INIT_D)
        pe.wait_ge(init_a, INIT_A)

        def tile_wait(l, k):
            pe.wait_ge(wsplit, l * LAYER_TILES + (k + 1))

        released = [None, None]

        def banks_wait(s, read):
            if released[s]:
                pe.wait_ge(L[released[s][0]], released[s][1])
            released[s] = read

        def tile(l, k, bank, hi, lo, read, korder=range(KB), kwait=None):
            w = k % 2
            tile_wait(l, k)
            banks_wait(bank, read)
            for m in range(2):
                n = 0
                for kb in korder:
                    if m == 0 and kwait:
                        kwait(kb)
                    c = kb * TM + m * P
                    for a, b in ((whi, hi), (wlo, hi), (whi, lo)):
                        mm = pe.matmul(ps[:, 2 * bank + m, :], a[:, w, c:c + P], b[:, kb, :],
                                       start=(n == 0), stop=(n == 3 * KB - 1))
                        n += 1
            mm.then_inc(tile_done, 1)

        def norm_sum(n):
            pe.wait_ge(L["acc_r"], 3 * n)
            if n > 1:
                pe.wait_ge(L["sqrt_r"], n - 1)
            for m in range(2):
                mm = pe.matmul(ps[:, 4, :], ones[:, :], acc2[:, m, :], start=(m == 0), stop=(m == 1))
            mm.then_inc(L["ssq_r"], 1)

        def mod_block(m):
            pe.wait_ge(L["mod_dma"], 16 * (m + 1))
            if m:
                pe.wait_ge(L["mod_row"], m)
            for kb in range(KB):
                mm = pe.matmul(ps[0:2, 5, 0:P], cvec[:, kb, :], modraw[:, kb, :], start=(kb == 0), stop=(kb == KB - 1))
            mm.then_inc(L["mod_ps"], 1)

        def mod_turn(m):
            pe.wait_ge(L["mod_row"], m + 1)
            if m:
                pe.wait_ge(L["mod_ev"], m)
            else:
                pe.wait_ge(L["sqrt_r"], 2)
            pe.transpose(ps[:, 4, 0:2], modrow[:, :], ident[0:2, 0:2]).then_inc(L["mod_T"], 1)

        def modulation(n):
            m = n - MOD_AT
            if 1 <= m <= MODS:
                mod_turn(m - 1)
            if 0 <= m < MODS:
                mod_block(m)

        with pe.Fori(0, DEPTH) as l:
            released[:] = [None, None]

            def pair(j):
                tile(l, j, j % 2, uhi, ulo, ("proj_r", j + 1),
                     kwait=(lambda kb: pe.wait_ge(L["ulo_r"], kb + 1)) if j == 0 else None)
                if j == 0:
                    norm_sum(1)
                    pe.wait_ge(L["lsp"], 1)
                    pe.matmul(ps[:, 6, 0:2], ones[:, :], small[:, 0:2], start=True, stop=True).then_inc(L["dots_r"], 1)

            for j in range(4):
                pair(j)
            pe.wait_ge(L["xc_r"], 4)
            pe.wait_ge(lw[0], l * 16 + 16)
            for n in range(8):
                if n >= 2:
                    pe.wait_ge(L["gate_t"], n - 1)
                elif n == 0:
                    pe.wait_ge(L["lam_r"], 1)
                pe.matmul(ps[:, 6 + n % 2, :], gw[:, n, :], xc[:, n % 4, :], start=True, stop=True
                          ).then_inc(L["gate_ps"], 1)
            for j in range(4, 8):
                pair(j)

            rope_n = [0]

            def rope(m):
                n = rope_n[0]
                rope_n[0] += 1
                pe.wait_ge(L["rope_rd"], n - 1) if n >= 2 else pe.wait_ge(L["gate_t"], 8)
                pe.wait_ge(L["proj_r"], m // 2 + 1)
                pe.matmul(ps[:, 6 + n % 2, :], rperm[:, :], proj[:, m, :], start=True, stop=True
                          ).then_inc(L["rope_ps"], 1)

            for m in range(Q0, Q0 + 4):
                rope(m)
            for j in range(8, 10):
                pair(j)
            for m in range(K0, K0 + 4):
                rope(m)
            for t in range(4):
                pe.wait_ge(L["proj_r"], 10)
                for hd in range(HEADS):
                    mm = pe.transpose(ps[:, t, hd * P:(hd + 1) * P], proj[:, V0 + hd, t * P:(t + 1) * P], ident[:, :])
                mm.then_inc(L["v_ps"], 1)
            units = [(hd, qb) for hd in range(HEADS) for qb in range(4)]

            def scores(n):
                hd, qb = units[n]
                p, w = n % 2, (qb + 1) * P
                if n < 2:
                    pe.wait_ge(L["v_r"], 2 * n + 2)
                else:
                    pe.wait_ge(L["exp_r"], 2 * (n - 1))
                pe.wait_ge(L["rope_r"], 8)
                for c in range(2):
                    q = proj[64 * c:64 * c + 64, Q0 + hd, qb * P:(qb + 1) * P]
                    pe.matmul(ps[:, 2 * p + c, 0:w], q, proj[64 * c:64 * c + 64, K0 + hd, 0:w], start=True, stop=False)
                    mm = pe.matmul(ps[:, 2 * p + c, qb * P:w], identb[:, :], maskb[:, :], start=False, stop=True)
                mm.then_inc(L["qk_r"], 1)

            def turn(n):
                hd, qb = units[n]
                pe.wait_ge(L["att_r"], n + 1)
                pe.wait_ge(L["attTc"], n - 1) if n >= 2 else pe.wait_ge(L["rope_rd"], 8)
                for kb in range(qb + 1):
                    mm = pe.transpose(ps[:, 6 + n % 2, kb * P:(kb + 1) * P], patt[:, n % 2, kb * P:(kb + 1) * P],
                                      ident[:, :])
                mm.then_inc(L["attT_r"], 1)

            def values(n):
                hd, qb = units[n]
                pe.wait_ge(L["attTc"], n + 1)
                if qb == 0:
                    if hd >= 2:
                        pe.wait_ge(L["o_r"], 2 * (hd - 1))
                    elif hd == 0:
                        pe.wait_ge(L["sqrt_r"], 1)
                for kb in range(qb + 1):
                    mm = pe.matmul(ps[:, 4 + hd % 2, qb * P:(qb + 1) * P], vtok[:, kb, hd * P:(hd + 1) * P],
                                   pattT[:, n % 2, kb * P:(kb + 1) * P], start=(kb == 0), stop=(kb == qb))
                mm.then_inc(L["pv_r"], 1)

            N = len(units)
            scores(0)
            scores(1)
            for n in range(N):
                if n + 2 < N:
                    scores(n + 2)
                turn(n)
                if n:
                    values(n - 1)
            values(N - 1)
            for hd in range(HEADS):
                pe.wait_ge(L["o_r"], 2 * (hd + 1))
                if hd == 0:
                    pe.wait_ge(L["exp_r"], 2 * N)
                pe.matmul(ps[:, hd, :], ones[:, :], osq[:, hd, :], start=True, stop=True).then_inc(L["oss_r"], 1)
            for j in range(4):
                if j == 0:
                    released[:] = [("orst_r", 1)] * 2

                def owait(kb):
                    if kb == 4:
                        pe.wait_ge(L["oy_r"], 1)
                    if kb < 4:
                        pe.wait_ge(L["oy_r"], kb + 2)
                tile(l, T_OUT + j, j % 2, oyhi, oylo, ("h_r", j + 1), korder=[4, 5, 6, 7, 0, 1, 2, 3], kwait=owait if j == 0 else None)
            b = 0
            for c in range(CHUNKS):
                for j in range(4):
                    tile(l, T_MLP + 8 * c + j, b % 2, uhi, ulo, ("m_r", 4 * c + j + 1),
                         kwait=(lambda kb: pe.wait_ge(L["ulo_r"], KB + kb + 1)) if c == 0 and j == 0 else None)
                    b += 1
                    if c == 0 and j == 0:
                        norm_sum(2)
                    modulation(8 * c + j)
                for j in range(4):
                    tile(l, T_MLP + 8 * c + 4 + j, b % 2, hidhi, hidlo, ("h_r", 4 + 4 * c + j + 1),
                         kwait=(lambda kb: pe.wait_ge(L["hlo_r"], 4 * c + kb // 2 + 1)) if j == 0 else None)
                    b += 1
                    modulation(8 * c + 4 + j)
            tile_wait(l, T_PP)
            pe.wait_ge(L["p_r"], 1)
            for g in range(4):
                banks_wait(g % 2, ("pp_r", g + 1))
                for m in range(2):
                    n = 0
                    for kb in range(2):
                        c = kb * D + (2 * g + m) * P
                        for x, y in ((whi, phi), (wlo, phi), (whi, plo)):
                            mm = pe.matmul(ps[:, 2 * (g % 2) + m, :], x[:, T_PP % 2, c:c + P], y[:, kb, :],
                                           start=(n == 0), stop=(n == 5))
                            n += 1
                mm.then_inc(L["pp_ps"] if g < 3 else tile_done, 1)
            for j in range(4):
                tile(l, T_GATE + j, j % 2, uhi, ulo, ("g_r", j + 1),
                     kwait=(lambda kb: pe.wait_ge(L["ulo_r"], 2 * KB + kb + 1)) if j == 0 else None)
                if j == 0:
                    pe.wait_ge(L["mod_ev"], MODS)
                    norm_sum(3)
            pe.wait_ge(tile_done, l * LAYER_TILES + (LAYER_TILES - 1 + CREDIT))
            pe.sem_inc(tile_done, 1)
            pe.sem_inc(L["layer_done"], 1)
            pe.wait_ge(layer_go, l + 1)

        if stage == 1:
            return

        def done_wait(k):
            pe.wait_ge(tile_done, k + (1 + CREDIT))

        def norm_sums(n, sq, src, t):
            if n > 1:
                pe.wait_ge(n_rt, n - 1)
            w = HALF if t > 512 else t
            for b in range(KB):
                if b % 2 == 0:
                    pe.wait_ge(n_sq, 4 * (sq - 1) + b // 2 + 1)
                for half in range(t // w):
                    mm = pe.matmul(ps[:, 6 + half, 0:w], ones[:, :], src[:, b, half * w:(half + 1) * w],
                                   start=(b == 0), stop=(b == KB - 1))
            mm.then_inc(n_ss, 1)

        norm_sums(1, 1, sqb, S)
        norm_sums(2, 2, sqb, T)

        def dense(s, off, width, src, kbs, last, q, read, kwait=None, parts=(0, 1)):
            hi, lo = src
            if read:
                read()
            N = 3 * len(kbs)
            for group_of in ([parts] if len(parts) == 2 else [[x] for x in parts]):
                n = 0
                for i, kb in enumerate(kbs):
                    if kwait:
                        kwait(kb)
                    c = off(i)
                    for a, b in ((whi, hi), (wlo, hi), (whi, lo)):
                        for half in group_of:
                            mm = pe.matmul(ps[0:width, q + half, 0:HALF], a[:, s, c:c + width],
                                           b[:, kb, half * HALF:(half + 1) * HALF], start=(n == 0), stop=(n == N - 1))
                        n += 1
            if 1 in parts:
                mm.then_inc(tile_done if last else blk_ps, 1)

        IN, U = (inhi, inlo), (uh, ul)
        EIGHT = range(KB)

        def wait_split(k):
            pe.wait_ge(wsplit, k + 1)

        pe.wait_ge(ld2, 6 * 16)
        wait_split(T_DT)
        dense(T_DT % 2, lambda i: i * 64, 64, IN, EIGHT, True, 0, None, lambda kb: pe.wait_ge(in_lo, kb + 1))

        def turn_dt():
            pe.wait_ge(dt_d, 1)
            for c in range(NC):
                mm = pe.transpose(ps[:, 4, c * 64:(c + 1) * 64], dtT[:, c * P:(c + 1) * P], ident[0:64, 0:64])
            mm.then_inc(dt_p, 1)

        wait_split(T_XS0)
        dense(T_XS0 % 2, lambda i: i * TM, P, IN, EIGHT, False, 2, None)
        turn_dt()
        dense(T_XS0 % 2, lambda i: i * TM + P, P, IN, EIGHT, True, 0, lambda: pe.wait_ge(dt_d, 1))
        wait_split(T_BC0)
        dense(T_BC0 % 2, lambda i: i * TM, P, IN, EIGHT, False, 2, lambda: pe.wait_ge(x_rd, 1))
        pe.wait_ge(dt_d, DT_G)
        for d, tri in enumerate((triF, triB)):
            pe.matmul(ps[:, 5, 0:384].rearrange("p (c n) -> p c n", c=NC)[:, :, 32 * d:32 * d + 32], tri[:, :],
                      tab[:, K_G:K_G + 2 * NC, :].rearrange("p (c d) r -> p d c r", d=2)[:, d], start=True, stop=True)
        pe.matmul(ps[:, 6, 0:384], ones[:, :], tab[:, K_G:K_G + 2 * NC, :].rearrange("p c r -> p (c r)"),
                  start=True, stop=True).then_inc(dt_p, 1)
        dense(T_BC0 % 2, lambda i: i * TM + P, P, IN, EIGHT, True, 0, lambda: pe.wait_ge(x_rd, 2))

        def group(g, last):
            kt = g * G_TILES + T_G0
            nb = 3 if last else 10
            blk0 = g * 10 + 2

            def last_reads():
                pe.wait_ge(x_rd, g * 4 + 4)
                pe.wait_ge(o_rd, g * 8 + 8)
            wait_split(kt)
            dense(T_G0 % 2, lambda i: i * TM, P, IN, EIGHT, False, 2,
                  lambda: (pe.wait_ge(x_rd, g * 4 + 3), pe.wait_ge(o_rd, g * 8 + 7)))
            last_reads()
            pe.wait_ge(cv_r, g * 4 + 4)
            pe.wait_ge(y_rd, g * 6 + 6)
            for c in range(NC):
                q = 4 + c % 4
                if c >= 4:
                    pe.wait_ge(tok_r, g * 6 + (c - 3))
                else:
                    pe.wait_ge(y_rd, g * 6 + 6)
                t0 = c * P + (2 if c >= CTX_CHUNKS else 0)
                for b in range(2):
                    pe.transpose(ps[:, q, b * P:(b + 1) * P], convd[:, b, t0:t0 + P], ident[:, :])
                pe.matmul(ps[:, q, 256:384], convd[:, 2, t0:t0 + P], convd[:, 3, t0:t0 + P], start=True, stop=True)
                pe.transpose(ps[:, q, 384:512], convd[:, 2, t0:t0 + P], ident[:, :]).then_inc(pre_ps, 1)
            SX, SB = (T_G0 + 1) % 2, (T_G0 + 2) % 2
            ahead = {
                "x0": (SX, 0, False, 0, lambda: wait_split(kt + 1)),
                "x1": (SX, P, True, 0, lambda: pe.wait_ge(x_rd, g * 4 + 5)),
                "b": (SB, 0, False, 2, lambda: (wait_split(kt + 2), pe.wait_ge(z_rd, g * 2 + 2))),
                "c": (SB, P, True, 0, lambda: pe.wait_ge(x_rd, g * 4 + 6))}

            def next_half(name, part):
                if not last:
                    slot, o, end, q, read = ahead[name]
                    dense(slot, lambda i: i * TM + o, P, IN, EIGHT, end, q, read if part == 0 else None, None, (part,))

            next_half("x0", 0)
            for c in range(NC):
                pe.wait_ge(xte_r, g * 6 + (c + 1))
                if c < 4:
                    pe.wait_ge(tok_r, g * 6 + (c + 3))
                else:
                    pe.wait_ge(sc_r, g * 6 + (c - 3))
                for d in range(2):
                    if (d, c) in ((0, 5), (1, 2)):
                        continue
                    mm = pe.matmul(ps[:, 4 + (c + 2) % 4, d * 256:(d + 1) * 256], btok[:, c, :],
                                   xte[:, c, d, :, :].rearrange("p r n -> p (r n)"), start=True, stop=True)
                mm.then_inc(st_ps, 1)

            def log_decay(c):
                pe.wait_ge(sc_r, g * 6 + 6) if c == 0 else pe.wait_ge(ex_r, g * 6 + c)
                pe.wait_ge(tabg_r, g + 1)
                for d, tri in enumerate((triF, triB)):
                    pe.matmul(ps[:, 4 + d, :], identb[:, :], mask2[:, d:d + 1, :].broadcast_to([P, HPG, P]),
                              start=True, stop=False)
                    for r in range(HPG):
                        mm = pe.matmul(ps[:, 4 + d, r * P:(r + 1) * P],
                                       tabg[:, K_G + 2 * c + d, r:r + 1].broadcast_to([P, P]), tri[:, :],
                                       start=False, stop=(r == HPG - 1))
                mm.then_inc(la_ps, 1)

            def off_part(c):
                pe.wait_ge(scan_r, g + 1)
                pe.wait_ge(ck_r, g + 1)
                if c:
                    pe.wait_ge(offs_r, g * 6 + c)
                for d, slot in enumerate((PREV_F[c], PREV_B[c])):
                    if slot is not None:
                        mm = pe.matmul(ps[:, 6, d * 256:(d + 1) * 256], ck[:, c * P:(c + 1) * P], ast[:, slot, :],
                                       start=True, stop=True)
                mm.then_inc(off_ps, 1)

            def y_part(c):
                pe.wait_ge(offs_r, g * 6 + (c + 1))
                pe.wait_ge(W_r, g * 6 + (c + 1))
                pe.wait_ge(y_rd, g * 6 + (6 + c))
                base = (c % 2) * 256
                for b in range(2):
                    q = base + b * P
                    pe.matmul(ps[:, 7, q:q + P], offs[:, 0, 2 * b:2 * b + 2, :].rearrange("p r n -> p (r n)"), ident[:, :],
                              start=True, stop=False)
                    for r in range(2):
                        x0 = (2 * b + r) * HD
                        mm = pe.matmul(ps[64 * r:64 * r + 64, 7, q:q + P], xcb[:, c, x0:x0 + HD], wdec[:, 2 * b + r, :],
                                       start=False, stop=True)
                mm.then_inc(y_ps, 1)

            log_decay(0)
            dense(T_G0 % 2, lambda i: i * TM + P, P, IN, EIGHT, True, 2, lambda: pe.wait_ge(z_rd, g * 2 + 1))
            off_part(0)
            for c, (name, part) in enumerate((("x0", 1), ("x1", 0), ("x1", 1), ("b", 0), ("b", 1), ("c", 0))):
                next_half(name, part)
                if c + 1 < NC:
                    log_decay(c + 1)
                y_part(c)
                if c + 1 < NC:
                    off_part(c + 1)
            next_half("c", 1)
            k = 1 if last else 3
            wait_split(kt + k)
            pe.wait_ge(u_r, g * 2 + 2)
            for j in range(KB):
                if j >= 2:
                    read = lambda: pe.wait_ge(o_rd, g * 8 + (8 + j - 1))
                elif last:
                    read = lambda: pe.wait_ge(z_rd, g * 2 + 2)
                else:
                    read = lambda: pe.wait_ge(x_rd, g * 4 + (7 + j))
                dense((T_G0 + k) % 2, lambda i: i * D + j * P, P, U, range(2), j == KB - 1, 2 - 2 * (j % 2), read)

        with pe.Fori(0, GROUPS - 1) as g:
            group(g, False)
        group(GROUPS - 1, True)

        pe.wait_ge(acc_r2, GROUPS + 1)
        pe.wait_ge(y_rd, 6 * GROUPS + 6)
        for half in range(2):
            mm = pe.matmul(ps[:, 6 + half, 0:HALF], ones[:, :], acc[:, half * HALF:(half + 1) * HALF],
                           start=True, stop=True)
        mm.then_inc(n_ss, 1)
        norm_sums(4, 3, sq4, T)

        pe.wait_ge(o_rd, 8 * GROUPS + 8)
        for m, k in ((0, 0), (1, 0), (0, 1), (1, 1)):
            if m == 0:
                wait_split(T_ATT + k)
            u = 2 * k + m
            dense((T_ATT + k) % 2, lambda i: i * TM + m * P, P, IN, EIGHT, m == 1, 2 * m,
                  (lambda: pe.wait_ge(a_rd, u - 1)) if u >= 2 else None,
                  (lambda kb: pe.wait_ge(in_lo, KB + kb + 1)) if u == 0 else None)

        def lat_tile(k, unit, src, t0, read, kwait=None):
            hi, lo = src
            wait_split(k)
            read()
            q = 2 * (unit % 2)
            for m in range(2):
                n = 0
                for kb in EIGHT:
                    if kwait and m == 0:
                        kwait(kb)
                    c = kb * TM + m * P
                    for a, b in ((whi, hi), (wlo, hi), (whi, lo)):
                        mm = pe.matmul(ps[:, q + m, :], a[:, k % 2, c:c + P], b[:, kb, t0:t0 + S],
                                       start=(n == 0), stop=(n == 3 * KB - 1))
                        n += 1
            mm.then_inc(tile_done, 1)

        def q_tile(j):
            lat_tile(T_ATT + 2 + j, j, IN, CTX, lambda: pe.wait_ge(a_rd, 3 + j))

        def head_sums_q(b0):
            pe.wait_ge(a_rd, 4 + b0 // 2 + 2)
            pe.wait_ge(ln_r, 1 + b0 // 4)
            for b in range(4):
                mm = pe.matmul(ps[:, 4 + b, :], bones[:, :], qsq[:, b0 + b, :], start=True, stop=True)
            mm.then_inc(ssh, 1)

        q_tile(0)
        q_tile(1)
        pe.wait_ge(ld3, 16 * 4)
        pe.wait_ge(a_rd, 2)
        pe.wait_ge(n_rt, 4)
        for m in range(2):
            for half in range(2):
                mm = pe.matmul(ps[:, 4 + 2 * m + half, 0:HALF], bones[:, :], ksq[:, m, half * HALF:(half + 1) * HALF],
                               start=True, stop=True)
        mm.then_inc(ssh, 1)
        q_tile(2)
        head_sums_q(0)
        q_tile(3)
        head_sums_q(4)
        for j in range(4):
            lat_tile(T_ATT + 6 + j, j, IN, CTX,
                     lambda: pe.wait_ge(a_rd, 7 + j) if j < 2 else pe.wait_ge(g_rd, j - 1))
        pe.wait_ge(ln_r, 3)
        for n in range(10):
            pe.wait_ge(qn_r, 1 if n < 2 else 2 + (n - 2) // 4)
            if n >= 4:
                pe.wait_ge(rp_rd, n - 3)
            src = kf[:, n, CTX:T] if n < 2 else qb_[:, n - 2, :]
            pe.matmul(ps[:, 4 + n % 4, :], perm2[:, :], src, start=True, stop=True).then_inc(rp_ps, 1)
        pe.wait_ge(g_rd, 4)
        for c in range(NC):
            if c >= 4:
                pe.wait_ge(vt_r, c - 3)
            for b in range(2):
                mm = pe.transpose(ps[:, c % 4, b * P:(b + 1) * P], vf[:, b, c * P:(c + 1) * P], ident[:, :])
            mm.then_inc(vt_ps, 1)
        pe.wait_ge(vt_r, NC)
        pe.wait_ge(rp_rd, 10)

        with pe.Fori(0, 2) as i:
            def score_max(h, t):
                j, p = h // REP, h % 3
                if t == 0:
                    if h % REP == 0:
                        pe.wait_ge(k_lo, i * 2 + (j + 1))
                    pe.wait_ge(q_lo, i * 8 + (h + 1))
                q = 2 * (t % 2)
                n = 4 * h + t
                if n >= 2:
                    pe.wait_ge(mx_r, i * 32 + (n - 1))
                for half in range(2):
                    ks = slice(half * HALF, (half + 1) * HALF)
                    pe.matmul(ps[:, q + half, 0:HALF], Q1[p][:, t * P:(t + 1) * P], K1[j][:, ks],
                              start=True, stop=False)
                    mm = pe.matmul(ps[:, q + half, 0:HALF], Q2[p][0:64, t * P:(t + 1) * P], K2[j][0:64, ks],
                                   start=False, stop=True)
                mm.then_inc(s_ps, 1)

            def max_row(h):
                pe.wait_ge(mxf_r, i * 8 + (h + 1))
                if h:
                    pe.wait_ge(mxl_r, i * 8 + h)
                for t in range(4):
                    mm = pe.matmul(ps[:, 4, t * P:(t + 1) * P], nm4[:, h % 2, t:t + 1].broadcast_to([P, P]), ident[:, :],
                                   start=True, stop=True)
                mm.then_inc(mx_ps, 1)

            def attend(h):
                j, p = h // REP, h % 3
                pe.wait_ge(mxl_r, i * 8 + (h + 1))

                def pv(kb):
                    pe.wait_ge(p_r2, i * 48 + (6 * h + kb + 1))
                    if kb == 0:
                        pe.wait_ge(va_r, i * 2 + (j + 1))
                        if h:
                            pe.wait_ge(o_ev, i * 8 + h)
                    return pe.matmul(ps[:, 7, :], vaug[:, kb, :], pT2[:, kb, :], start=(kb == 0), stop=(kb == NC - 1))

                for kb in range(NC):
                    n = 6 * h + kb
                    if n >= 2:
                        pe.wait_ge(p_r2, i * 48 + (n - 1))
                    pe.matmul(ps[:, 5 + kb % 2, :], K1[j][:, kb * P:(kb + 1) * P], Q1[p][:, :], start=True, stop=False)
                    pe.matmul(ps[:, 5 + kb % 2, :], K2[j][:, kb * P:(kb + 1) * P], Q2[p][:, :], start=False, stop=True
                              ).then_inc(sT_ps, 1)
                    if h + 1 < 8 and kb < 4:
                        score_max(h + 1, kb)
                    if kb == NC - 1 and h + 1 < 8:
                        max_row(h + 1)
                    if kb:
                        pv(kb - 1)
                pv(NC - 1).then_inc(o_ps, 1)

            for t in range(4):
                score_max(0, t)
            max_row(0)
            for h in range(8):
                attend(h)
        for j in range(4):
            lat_tile(T_ATT + 10 + j, j, (ohi, olo), 0, (lambda: pe.wait_ge(hf_r, j - 1)) if j >= 2 else (
                lambda: pe.wait_ge(mx_r, 64)), (lambda kb: pe.wait_ge(ol_r, kb + 1)) if j == 0 else None)
        norm_sums(5, 4, sqb, S)

    @block.scalar
    def _(act):
        L = Ls
        A = act.activation
        act.wait_ge(cst, CST)
        A(small[:, 0:16], cvec[:, :, :].rearrange("p a b -> p (a b)"), ACT.Tanh, scale=0.5).then_inc(init_a, 1)
        act.wait_ge(init_d, D_ANGLE)
        A(ropeS[:, :], angt[0][:, :], ACT.Sin).then_inc(init_a, 1)
        A(ropeC[:, :], angt[0][:, :], ACT.Abs).then_inc(init_a, 1)
        act.wait_ge(init_a, 3)
        A(ropeC[:, :], ropeC[:, :], ACT.Sin, scale=-1.0, bias=misc[:, 2:3]).then_inc(init_a, 1)
        act.wait_ge(init_d, INIT_D)

        with act.Fori(0, DEPTH) as l:
            st = Chain(act, L["a_step"])

            def tile_wait(k):
                act.wait_ge(tile_done, l * LAYER_TILES + (k + 1 + CREDIT))

            act.dma_start(gw[:, :, :], io["gates"][bass.ds(l, 1)].rearrange("a p j n -> p (a j) n")).then_inc(lw[0], 16)
            act.dma_start(pT[:, :, :], io["pT"][bass.ds(l, 1)].rearrange("a p j n -> p (a j) n")).then_inc(lw[1], 16)
            act.wait_ge(L["lp_copied"], 1)
            st(A(small[:, 4:8], lp[:, C_LRU:C_LRU + 4], ACT.Abs))
            A(small[:, 8:12], small[:, 4:8], ACT.Exp, scale=-1.0).then_inc(L["lsa"], 1)

            def rounded(j, g):
                for b in (2 * j, 2 * j + 1):
                    A(uhi[:, b, :], h[:, b, :], ACT.Copy, scale=lp[:, g + b:g + b + 1]).then_inc(L["uhi_r"], 1)

            def squared(n, j, tmp):
                if j == 0 and n > 1:
                    act.wait_ge(L["ssq_r"], n - 1)
                if j > 1:
                    act.wait_ge(L["acc_r"], 3 * (n - 1) + j - 1)
                A((tmp if j else acc2)[:, :, :], h[:, 2 * j:2 * j + 2, :], ACT.Square).then_inc(L["sq_r"], 1)

            def prepare(n, j, g, tmp, h_at):
                act.wait_ge(L["h_r"], h_at)
                rounded(j, g)
                squared(n, j, tmp)

            def norm_root(n):
                act.wait_ge(L["ssq_r"], n)
                if n > 1:
                    act.wait_ge(L["rstd_r"], n - 1)
                A(rstd[:, :], ps[:, 4, :], ACT.Sqrt, scale=1.0 / D, bias=misc[:, 0:1]).then_inc(L["sqrt_r"], 1)

            def mod_fetch(m):
                act.dma_start(modraw[:, :, :], io["modw"][bass.ds(l * MODS + m, 1)].rearrange("a p j n -> p (a j) n")
                              ).then_inc(L["mod_dma"], 16)

            def modulation(n):
                m = n - MOD_AT
                if 1 <= m <= MODS:
                    act.wait_ge(L["mod_T"], m)
                    A(modsb[:, bass.ds(l * MODS + (m - 1), 1), :].rearrange("p a b -> p (a b)"), ps[:, 4, 0:2],
                      ACT.Copy).then_inc(L["mod_ev"], 1)
                if 0 <= m < MODS:
                    act.wait_ge(L["mod_ps"], m + 1)
                    A(modrow[:, :], ps[0:2, 5, 0:P], ACT.Copy).then_inc(L["mod_row"], 1)
                    if m + 1 < MODS:
                        mod_fetch(m + 1)

            for j in range(4):
                rounded(j, C_GMIX)
            for j in range(4):
                squared(1, j, sqmlp)
            norm_root(1)
            act.wait_ge(L["dots_r"], 1)
            A(small[:, 2:4], ps[:, 6, 0:2], ACT.Exp).then_inc(L["lam_r"], 1)
            for b in range(2):
                act.wait_ge(L["proj_r"], 3 + b)
                A(gt[:, 2 * b:2 * b + 2, :], proj[:, GR + 2 * b:GR + 2 * b + 2, :], ACT.Square).then_inc(L["lru_a"], 1)
            act.wait_ge(L["lsp"], 2)
            for n in range(8):
                act.wait_ge(L["gate_ps"], n + 1)
                A((ga if n < 4 else gi)[:, n % 4, :], ps[:, 6 + n % 2, :], ACT.Tanh, scale=0.5,
                  bias=small[:, 16 + n:17 + n]).then_inc(L["gate_t"], 1)
            act.wait_ge(L["lru_d"], 1)
            A(gt[:, :, :], gt[:, :, :], ACT.Tanh).then_inc(L["lru_a"], 1)
            act.wait_ge(L["lru_d"], 2)
            st(A(gt[:, :, :], ga[:, :, :], ACT.Tanh, scale=-1.0))
            st(A(ga[:, :, :], ga[:, :, :], ACT.Exp))
            A(asq[:, :, :], ga[:, :, :], ACT.Square).then_inc(L["lru_a"], 1)
            act.wait_ge(L["lru_d"], 3)
            A(gt[:, :, :], gt[:, :, :], ACT.Sqrt, scale=0.25).then_inc(L["lru_a"], 1)
            act.wait_ge(L["lru_d"], 4)
            A(oyhi[:, 4:8, :], ga[:, :, :], ACT.Copy).then_inc(L["yhi_r"], 1)
            for t in range(4):
                act.wait_ge(L["v_ps"], t + 1)
                A(vtok[:, t, :], ps[:, t, :], ACT.Copy).then_inc(L["v_r"], 1)

            def exps(n):
                p, w = n % 2, (n % 4 + 1) * P
                act.wait_ge(L["nmax_r"], n + 1)
                if n >= 2:
                    act.wait_ge(L["att_r"], n - 1)
                for c in range(2):
                    A(pexp[:, p, c, 0:w], ps[:, 2 * p + c, 0:w], ACT.Exp, bias=small[:, 44 + 2 * p + c:45 + 2 * p + c],
                      accum_out=small[:, 48 + 2 * p + c:49 + 2 * p + c]).then_inc(L["exp_r"], 1)

            def head_out(hd):
                act.wait_ge(L["pv_r"], 4 * hd + 4)
                A(osb[:, hd, :], ps[:, 4 + hd % 2, :], ACT.Copy).then_inc(L["o_r"], 1)
                A(osq[:, hd, :], ps[:, 4 + hd % 2, :], ACT.Square).then_inc(L["o_r"], 1)

            exps(0)
            for n in range(16):
                if n + 1 < 16:
                    exps(n + 1)
                act.wait_ge(L["attT_r"], n + 1)
                if n >= 2:
                    act.wait_ge(L["pv_r"], n - 1)
                w = (n % 4 + 1) * P
                A(pattT[:, n % 2, 0:w], ps[:, 6 + n % 2, 0:w], ACT.Copy).then_inc(L["attTc"], 1)
                if n % 4 == 0 and n:
                    head_out(n // 4 - 1)
            head_out(3)
            act.wait_ge(L["oss_r"], 4)
            A(orst[:, :, :], ps[:, 0:4, :], ACT.Ln, scale=1.0 / P, bias=misc[:, 0:1]).then_inc(L["orst_r"], 1)
            act.wait_ge(L["orst_r"], 1)
            A(orst[:, :, :], orst[:, :, :], ACT.Exp, scale=-0.5).then_inc(L["orst_r"], 1)
            for hd in range(HEADS):
                act.wait_ge(L["on_r"], hd + 1)
                A(oyhi[:, hd, :], osb[:, hd, :], ACT.Copy).then_inc(L["ohi_r"], 1)
            for j in range(4):
                prepare(2, j, C_GMLP, sqmlp, j + 1)
            norm_root(2)
            act.wait_ge(lw[1], l * 16 + 16)
            A(phi[:, :, :], pT[:, :, :], ACT.Copy).then_inc(L["phi_r"], 1)
            act.wait_ge(L["p_r"], 1)
            mod_fetch(0)
            for c in range(CHUNKS):
                for j in range(4):
                    n = 4 * c + j
                    act.wait_ge(L["m_r"], n + 1)
                    if n >= 2:
                        act.wait_ge(L["hlo_r"], n - 1)
                    A(hsq[n % 2][:, :, :], hm[n % 2][:, :, :], ACT.Square).then_inc(L["sqh_r"], 1)
                    A(hidhi[:, 2 * j:2 * j + 2, :], hm[n % 2][:, :, :], ACT.Square).then_inc(L["sqh_r"], 1)
                    modulation(8 * c + j)
                for j in range(4):
                    modulation(8 * c + 4 + j)
            for j in range(4):
                prepare(3, j, C_GPLE, sqple, 4 + 4 * (CHUNKS - 1) + j + 1)
            for g in range(4):
                act.wait_ge(L["pp_ps"], g + 1) if g < 3 else tile_wait(T_PP)
                A(pp[:, 2 * g:2 * g + 2, :], TWO(g % 2), ACT.Copy).then_inc(L["pp_r"], 1)
            norm_root(3)
            for j in range(4):
                act.wait_ge(L["g_r"], j + 1)
                A(gth[j % 2][:, :, :], gm[j % 2][:, :, :], ACT.Tanh, scale=0.5).then_inc(L["gth_r"], 1)
            act.wait_ge(L["gth_r"], 4)
            act.sem_inc(L["layer_done"], 1)
            act.wait_ge(layer_go, l + 1)

        if stage == 1:
            return

        def done_wait(k):
            act.wait_ge(tile_done, k + (1 + CREDIT))

        def halves(x):
            return x.rearrange("p (a n) -> p a n", a=2)

        for dst, src in ((p2[:, :], io["params2"]), (triF[:, :], io["consts2"][:, 0:128]),
                         (triB[:, :], io["consts2"][:, 128:256]),
                         (masktmp[:, :, :].rearrange("p a b -> p (a b)"), io["consts2"][:, 256:512]),
                         (drow[:, :], io["m_d"].partition_broadcast(P)),
                         (arow[:, :], io["m_a_log"].partition_broadcast(P))):
            act.dma_start(dst, src).then_inc(ld2, 16)
        act.dma_start(hres[:, :, 0:CTX], io["ctx"]).then_inc(ldc, 16)
        for j in range(4):
            A(sqb[:, 2 * j:2 * j + 2, 0:S], h[:, 2 * j:2 * j + 2, :], ACT.Square).then_inc(n_sq, 1)

        def root(n, dst, src, scale):
            act.wait_ge(n_ss, n)
            if n > 1:
                act.wait_ge(n_rs, n - 1)
            A(dst, src, ACT.Sqrt, scale=scale, bias=misc[:, 0:1]).then_inc(n_rt, 1)

        root(1, rstd[:, :], ps[:, 6, :], 1.0 / D)
        act.wait_ge(ldc, 16)
        for j in range(4):
            act.wait_ge(n_x, 2 * j + 2)
            A(sqb[:, 2 * j:2 * j + 2, :], hres[:, 2 * j:2 * j + 2, :], ACT.Square).then_inc(n_sq, 1)
        act.dma_start(hspill, hres[:, :, :]).then_inc(spill, 16)
        both = ps[:, 6:8, 0:HALF]
        root(2, halves(rs2[:, :]), both, 1.0 / D)

        def make_in(i):
            for b in range(KB):
                act.wait_ge(in_t, KB * i + b + 1)
                for t0, t1, c in ((0, CTX, 1), (CTX, T, 0)):
                    ins = A(tin[:, b % 2, t0:t1], tin[:, b % 2, t0:t1], ACT.Identity, scale=modA[:, b, c:c + 1],
                            bias=modv[i][:, b, c:c + 1])
                ins.then_inc(in_v, 1)
                act.wait_ge(in_v, KB * i + b + 1)
                A(inhi[:, b, :], tin[:, b % 2, :], ACT.Copy).then_inc(in_hi, 1)
        make_in(0)

        def copy_in(s, b, blk, tile_no):
            if b % 2 == 0:
                act.wait_ge(blk_ps, blk)
            else:
                done_wait(tile_no)
            if b >= 2:
                act.wait_ge(cv_r, s * 4 + (b - 1))
            q = 2 if b == 2 or (b == 0 and isinstance(s, int)) else 0
            r = raw[b % 2]
            A(r[:, 2:2 + CTX], ps[:, q, 0:CTX], ACT.Copy)
            A(r[:, 4 + CTX:4 + HALF], ps[:, q, CTX:HALF], ACT.Copy)
            A(r[:, 4 + HALF:4 + T], ps[:, q + 1, 0:HALF], ACT.Copy).then_inc(x_rd, 1)

        def conv_tanh(s, b):
            act.wait_ge(cv_c, s * 4 + (b + 1))
            A(raw[b % 2][:, 2:2 + CTX], convd[:, b, 0:CTX], ACT.Tanh)
            A(raw[b % 2][:, 4 + CTX:4 + T], convd[:, b, 2 + CTX:2 + T], ACT.Tanh).then_inc(cv_t, 1)

        act.wait_ge(dt_d, 2)
        A(dtw[1][:, :, :], dtw[0][:, :, :], ACT.Abs).then_inc(dt_a, 1)
        act.wait_ge(dt_a, 1)
        A(dtw[1][:, :, :], dtw[1][:, :, :], ACT.Exp, scale=-1.0).then_inc(dt_a, 1)
        A(arow[:, :], arow[:, :], ACT.Exp).then_inc(dt_a, 1)
        act.wait_ge(pads, 1)
        copy_in(0, 0, 1, None)
        copy_in(0, 1, None, T_XS0)
        conv_tanh(0, 0)
        conv_tanh(0, 1)
        copy_in(0, 2, 2, None)
        act.wait_ge(dt_d, DT_C)
        flat = lambda k: tab[:, k:k + 2 * NC, :].rearrange("p c r -> p (c r)")
        w = lambda n: dtw[n][:, :, :].rearrange("p c r -> p (c r)")
        A(w(6), w(6), ACT.Ln).then_inc(dt_a, 1)
        A(flat(K_EXLA), w(3), ACT.Exp)
        A(flat(K_DEC), w(4), ACT.Exp)
        A(w(5), w(5), ACT.Exp).then_inc(dt_a, 1)
        copy_in(0, 3, None, T_BC0)
        conv_tanh(0, 2)
        conv_tanh(0, 3)
        act.wait_ge(spill, 16)

        def group(g, last):
            kt = g * G_TILES + T_G0
            blk0 = g * 10 + 2
            def z_tanh(b):
                if b == 0:
                    act.wait_ge(blk_ps, blk0 + 1)
                else:
                    done_wait(kt)
                A(halves(zs[:, b, :]), ps[:, 2:4, 0:HALF], ACT.Tanh, scale=0.5).then_inc(z_t, 1)

            act.wait_ge(acc_r2, g + 1)
            z_tanh(0)
            act.wait_ge(cv_r, g * 4 + 4)
            act.wait_ge(y_rd, g * 6 + 6)
            A(ck[:, 0:CTX], convd[:, 3, 0:CTX], ACT.Copy)
            A(ck[:, CTX:T], convd[:, 3, CTX + 2:T + 2], ACT.Copy).then_inc(ck_r, 1)
            for c in range(NC):
                act.wait_ge(pre_ps, g * 6 + (c + 1))
                A(xcb[:, c, :], ps[:, 4 + c % 4, 0:384], ACT.Copy)
                A(btok[:, c, :], ps[:, 4 + c % 4, 384:512], ACT.Copy).then_inc(tok_r, 1)

            for c in range(NC):
                act.wait_ge(st_ps, g * 6 + (c + 1))
                q = 4 + (c + 2) % 4
                for slots, d in ((SLOT_F, 0), (SLOT_B, 1)):
                    if c in slots:
                        ins = A(ast[:, slots[c], :], ps[:, q, d * 256:(d + 1) * 256], ACT.Copy)
                ins.then_inc(sc_r, 1)

            def decays(c):
                act.wait_ge(la_ps, g * 6 + (c + 1))
                if c:
                    act.wait_ge(W_r, g * 6 + c)
                for d in range(2):
                    for r in range(HPG):
                        ins = A(ebuf[:, d, r, :], ps[:, 4 + d, r * P:(r + 1) * P], ACT.Exp,
                                bias=tabg[:, K_NB + 2 * c + d, r:r + 1])
                ins.then_inc(ex_r, 1)

            def u_hi(half):
                act.wait_ge(y_rd, g * 6 + (6 + 3 * half + 3))
                for m in range(2):
                    ins = A(uh[:, m, half * HALF:(half + 1) * HALF], zs[:, m, half * HALF:(half + 1) * HALF],
                            ACT.Copy, scale=mng[:, m:m + 1])
                ins.then_inc(uh_r, 1)

            s1 = g + 1
            decays(0)
            z_tanh(1)
            if not last:
                copy_in(s1, 0, blk0 + 2, None)
            decays(1)
            decays(2)
            if not last:
                conv_tanh(s1, 0)
                copy_in(s1, 1, None, kt + 1)
            decays(3)
            decays(4)
            if not last:
                conv_tanh(s1, 1)
                copy_in(s1, 2, blk0 + 3, None)
            decays(5)
            act.wait_ge(tile_done, kt + CREDIT)
            u_hi(0)
            u_hi(1)
            A(sqz[:, :, :], zs[:, :, :], ACT.Square).then_inc(sqz_r, 1)
            if not last:
                copy_in(s1, 3, None, kt + 2)
                conv_tanh(s1, 2)
                conv_tanh(s1, 3)

        with act.Fori(0, GROUPS - 1) as g:
            group(g, False)
        group(GROUPS - 1, True)

        act.wait_ge(u_r, 2 * GROUPS)
        act.wait_ge(sqz_r, GROUPS)
        act.dma_start(hback[:, :, :], hspill).then_inc(spill, 16)
        root(3, halves(rs2[:, :]), both, 1.0 / MDI)
        act.wait_ge(n_rt, 3)
        for dst, src in ((bones, io["consts2"][:, 512:640]), (perm2, io["consts2"][:, 640:768]),
                         (cosT, io["axial"][0]), (sinT, io["axial"][1])):
            act.dma_start(dst[:, :], src).then_inc(ld3, 16)
        for j in range(4):
            act.wait_ge(n_x, KB + 2 * j + 2)
            A(sq4[:, 2 * j:2 * j + 2, :], oacc[:, 2 * j:2 * j + 2, :], ACT.Square).then_inc(n_sq, 1)
        root(4, halves(rs2[:, :]), both, 1.0 / D)
        make_in(1)
        blk0 = 2 + 10 * (GROUPS - 1) + 8
        for n in range(4):
            k, m = n // 2, n % 2
            act.wait_ge(blk_ps, blk0 + k + 1) if m == 0 else done_wait(T_ATT + k)
            src = ps[:, 2 * m:2 * m + 2, 0:HALF]
            ins = A(halves((vf if k else kf)[:, m, :]), src, ACT.Copy)
            if k == 0:
                ins = A(halves(ksq[:, m, :]), src, ACT.Square)
            ins.then_inc(a_rd, 1)

        def q_tile(j):
            done_wait(T_ATT + 2 + j)
            A(qb_[:, 2 * j:2 * j + 2, :], TWO(j % 2), ACT.Copy)
            A(qsq[:, 2 * j:2 * j + 2, :], TWO(j % 2), ACT.Square).then_inc(a_rd, 1)

        q_tile(0)
        q_tile(1)
        act.wait_ge(ssh, 1)
        k4 = ksq[:, :, :].rearrange("p m (a n) -> p (m a) n", a=2)
        A(k4, ps[:, 4:8, 0:HALF], ACT.Ln, scale=1.0 / HD, bias=misc[:, 0:1]).then_inc(ln_r, 1)
        q_tile(2)
        q_tile(3)
        for n in range(2):
            act.wait_ge(ssh, 2 + n)
            A(qsq[:, 4 * n:4 * n + 4, :], ps[:, 4:8, :], ACT.Ln, scale=1.0 / HD, bias=misc[:, 0:1]).then_inc(ln_r, 1)
        act.wait_ge(ln_r, 3)
        A(ksq[:, :, :], ksq[:, :, :], ACT.Exp, scale=-0.5).then_inc(rsh_r, 1)
        for n in range(2):
            A(qsq[:, 4 * n:4 * n + 4, :], qsq[:, 4 * n:4 * n + 4, :], ACT.Exp, scale=-0.5).then_inc(rsh_r, 1)
        for j in range(4):
            done_wait(T_ATT + 6 + j)
            A(gs[:, 2 * j:2 * j + 2, :], TWO(j % 2), ACT.Tanh, scale=0.5).then_inc(g_t, 1)
        for c in range(NC):
            act.wait_ge(vt_ps, c + 1)
            A(vtok2[:, c, :], ps[:, c % 4, 0:256], ACT.Copy).then_inc(vt_r, 1)
        act.wait_ge(rp_r, 10)
        act.wait_ge(vt_r, NC)

        with act.Fori(0, 2) as i:
            def split_q(hq, part):
                r0 = 64 * (hq % 2)
                src = qb_[r0:r0 + 64, bass.ds(i * 4 + hq // 2, 1), :].rearrange("p a n -> p (a n)")
                if part == 0:
                    if hq:
                        act.wait_ge(q_lo, i * 8 + hq)
                    if hq > 2:
                        act.wait_ge(o_ps, i * 8 + (hq - 2))
                    act.sem_inc(act_go, 1)
                    A(qq[:, :], src, ACT.Copy)
                elif part == 1:
                    A(Q1[hq % 3][0:64, :], src, ACT.Copy)
                else:
                    A(Q1[hq % 3][64:128, :], src, ACT.Copy).then_inc(q_hi, 1)

            def max_hi(hq):
                act.wait_ge(mx_ps, i * 8 + (hq + 1))
                A(Q2[hq % 3][64:128, :], ps[64:128, 4, :], ACT.Copy).then_inc(mxh_r, 1)

            def ones_and_v(j):
                if j:
                    act.wait_ge(o_ps, i * 8 + 4 * j)
                act.sem_inc(act_go, 1)
                A(vaug[:, :, 0:64], vtok2[:, :, bass.ds(i * 128 + 64 * j, 64)], ACT.Copy).then_inc(va_r, 1)

            def o_hi(b):
                act.wait_ge(oy2, i * 4 + (b + 1))
                act.sem_inc(act_go, 1)
                A(ohi[:, bass.ds(i * 4 + b, 1), :], qb_[:, bass.ds(i * 4 + b, 1), :], ACT.Copy).then_inc(oh_r, 1)

            def split_k(j):
                src = kf[64 * j:64 * j + 64, bass.ds(i, 1), :].rearrange("p a n -> p (a n)")
                if j:
                    act.wait_ge(k_lo, i * 2 + j)
                act.sem_inc(act_go, 1)
                A(kk[:, :], src, ACT.Copy)
                A(K1[j][0:64, :], src, ACT.Copy)
                A(K2[j][0:64, :], src, ACT.Copy).then_inc(k_hi, 1)
            for part in range(3):
                split_q(0, part)
            split_k(0)
            ones_and_v(0)
            for part in range(3):
                split_q(1, part)
            max_hi(0)
            for hq in range(8):
                if hq:
                    act.wait_ge(o_ps, i * 8 + hq)
                for kb in range(NC):
                    act.wait_ge(sT_ps, i * 48 + (6 * hq + kb + 1))
                    A(pT2[:, kb, :], ps[:, 5 + kb % 2, :], ACT.Exp).then_inc(p_r2, 1)
                    if kb < 3 and hq + 2 < 8:
                        split_q(hq + 2, kb)
                if hq + 1 < 8:
                    max_hi(hq + 1)
                if hq == 1:
                    split_k(1)
                if hq % 2 == 0 and hq:
                    o_hi(hq // 2 - 1)
                act.wait_ge(o_ps, i * 8 + (hq + 1))
                act.sem_inc(act_go, 1)
                r0 = 64 * (hq % 2)
                A(qb_[r0:r0 + 64, bass.ds(i * 4 + hq // 2, 1), :].rearrange("p a n -> p (a n)"), ps[0:64, 7, :],
                  ACT.Copy)
                A(osum[r0:r0 + 64, :], ps[64:128, 7, :], ACT.Copy).then_inc(o_ev, 1)
                if hq == 3:
                    ones_and_v(1)
            o_hi(3)

        for n in range(4):
            act.wait_ge(hf_r, n + 1)
            A(sqb[:, 2 * n:2 * n + 2, 0:S], oacc[:, 2 * n:2 * n + 2, CTX:T], ACT.Square).then_inc(n_sq, 1)
        root(5, rs5[:, :], ps[:, 6, :], 1.0 / D)

    @block.vector
    def _(dve):
        L = Ls
        V = dve
        st = Chain(dve, init_d)
        st(V.memset(ones[:, :], 1.0))
        dve.wait_ge(cst, CST)
        st(V.tensor_copy(identb[:, :], ident[:, :]))
        st(V.tensor_copy(maskb[:, :], maskf[:, :]))
        st(V.tensor_copy(angt[0][:, :], posi[:, :]))
        st(V.tensor_scalar(angt[0][:, :], angt[0][:, :], misc[:, 1:2], None, ALU.mult))
        st(V.tensor_scalar(angt[1][:, :], angt[0][:, :], 1.0 / (2 * math.pi), MAGIC, ALU.mult, ALU.add))
        st(V.tensor_scalar(angt[1][:, :], angt[1][:, :], MAGIC, None, ALU.subtract))
        for part in (TWO_PI_1, TWO_PI_2, TWO_PI_3):
            st(V.scalar_tensor_tensor(out=angt[0][:, :], in0=angt[1][:, :], scalar=-part, in1=angt[0][:, :],
                                      op0=ALU.mult, op1=ALU.add))
        st(V.tensor_scalar(angt[0][:, :], angt[0][:, :], 3.1415925, -3.1415925, ALU.min, ALU.max))
        assert st.n == D_ANGLE
        dve.wait_ge(init_a, 1)
        cv = cvec[:, :, :].rearrange("p a b -> p (a b)")
        st(V.scalar_tensor_tensor(out=cv, in0=small[:, 0:16], scalar=1.0, in1=cv, op0=ALU.add, op1=ALU.mult))
        st(V.tensor_scalar(cv, cv, 0.5, None, ALU.mult))
        assert st.n == D_SILU
        dve.wait_ge(init_a, INIT_A)
        st(V.tensor_scalar(ropeS[:, :], ropeS[:, :], misc[:, 3:4], None, ALU.mult))
        assert st.n == INIT_D

        with dve.Fori(0, DEPTH) as l:
            st = Chain(dve, L["d_step"])

            def tile_wait(k):
                dve.wait_ge(tile_done, l * LAYER_TILES + (k + 1 + CREDIT))

            st(V.tensor_copy(lp[:, :], lpall[:, bass.ds(l, 1), :].rearrange("p a n -> p (a n)")))
            dve.sem_inc(L["lp_copied"], 1)
            V.tensor_tensor(small[:, 0:2], lp[:, C_LQ:C_LQ + 2], lp[:, C_LK:C_LK + 2], ALU.mult).then_inc(L["lsp"], 1)

            def rest(n, j, g):
                for b in (2 * j, 2 * j + 1):
                    dve.wait_ge(L["uhi_r"], KB * (n - 1) + b + 1)
                    V.scalar_tensor_tensor(out=ulo[:, b, :], in0=h[:, b, :], scalar=lp[:, g + b:g + b + 1],
                                           in1=uhi[:, b, :].bitcast(F32), op0=ALU.mult, op1=ALU.subtract
                                           ).then_inc(L["ulo_r"], 1)

            def add_squares(n, j, tmp):
                if j:
                    dve.wait_ge(L["sq_r"], 4 * (n - 1) + j + 1)
                    if j > 1:
                        dve.wait_ge(L["acc_r"], 3 * (n - 1) + j - 1)
                    V.tensor_tensor(acc2[:, :, :], acc2[:, :, :], tmp[:, :, :], ALU.add).then_inc(L["acc_r"], 1)

            def prepare(n, j, g, tmp):
                rest(n, j, g)
                add_squares(n, j, tmp)

            def norm_recip(n):
                dve.wait_ge(L["sqrt_r"], n)
                V.reciprocal(rstd[:, :], rstd[:, :]).then_inc(L["rstd_r"], 1)
                dve.wait_ge(L["rstd_r"], n)

            rstd2 = rstd[:, :].unsqueeze(1).broadcast_to([P, 2, S])

            for j in range(4):
                rest(1, j, C_GMIX)
            for j in range(4):
                add_squares(1, j, sqmlp)
            norm_recip(1)
            dve.wait_ge(L["lsa"], 1)
            softplus(V, st, small[:, 12:16], small[:, 8:12], small[:, 28:32], small[:, 32:36], small[:, 36:40])
            st(V.tensor_scalar(small[:, 28:32], lp[:, C_LRU:C_LRU + 4], -1.0, 0.0, ALU.mult, ALU.max))
            st(V.tensor_tensor(small[:, 12:16], small[:, 12:16], small[:, 28:32], ALU.add))
            st(V.tensor_scalar(small[:, 24:28], small[:, 12:16], -4.0, None, ALU.mult))
            V.tensor_scalar(small[:, 16:24], lp[:, C_BA:C_BA + 8], 0.5, None, ALU.mult).then_inc(L["lsp"], 1)


            def lambdas():
                dve.wait_ge(L["lam_r"], 1)
                st(V.tensor_tensor(small[:, 40:41], small[:, 3:4], small[:, 2:3], ALU.subtract))
                st(V.tensor_tensor(small[:, 40:41], small[:, 40:41], lp[:, C_LI:C_LI + 1], ALU.subtract))
                st(V.tensor_tensor(small[:, 41:42], lp[:, C_GSUB:C_GSUB + 1], lp[:, C_1LI:C_1LI + 1], ALU.mult))

            def mix_out(j):
                tile_wait(j)
                V.tensor_tensor(proj[:, 2 * j:2 * j + 2, :], TWO(j % 2), rstd2, ALU.mult).then_inc(L["proj_r"], 1)

            def conv(b):
                x = proj[:, XR + b, :]
                tap = lambda i: lp[:, C_CW + 4 * i + b:C_CW + 4 * i + b + 1]
                st(V.tensor_scalar(xc[:, b, :], x, tap(3), lp[:, C_CB + b:C_CB + b + 1], ALU.mult, ALU.add))
                for i in (1, 2, 3):
                    ins = V.scalar_tensor_tensor(out=xc[:, b, i:], in0=x[:, 0:S - i], scalar=tap(3 - i),
                                                 in1=xc[:, b, i:], op0=ALU.mult, op1=ALU.add)
                    if i < 3:
                        st(ins)
                ins.then_inc(L["xc_r"], 1)

            mix_out(0)
            lambdas()
            dve.wait_ge(L["proj_r"], 1)
            conv(0)
            conv(1)
            mix_out(1)
            dve.wait_ge(L["proj_r"], 2)
            conv(2)
            conv(3)
            mix_out(2)
            mix_out(3)
            c0 = math.sqrt(2 / math.pi)
            dve.wait_ge(L["lru_a"], 2)
            st(V.tensor_scalar(gt[:, :, :], gt[:, :, :], 0.044715 * c0, c0, ALU.mult, ALU.add))
            V.tensor_tensor(gt[:, :, :], gt[:, :, :], proj[:, GR:GR + 4, :], ALU.mult).then_inc(L["lru_d"], 1)
            for b in range(4):
                dve.wait_ge(L["gate_t"], b + 1)
                st(V.tensor_scalar(ga[:, b, :], ga[:, b, :], small[:, 24 + b:25 + b], small[:, 24 + b:25 + b],
                                   ALU.mult, ALU.add))
            dve.wait_ge(L["lru_a"], 3)
            V.scalar_tensor_tensor(out=proj[:, GR:GR + 4, :], in0=gt[:, :, :], scalar=1.0, in1=proj[:, GR:GR + 4, :],
                                   op0=ALU.add, op1=ALU.mult).then_inc(L["lru_d"], 1)
            dve.wait_ge(L["gate_t"], 8)
            st(V.scalar_tensor_tensor(out=xc[:, :, :], in0=gi[:, :, :], scalar=1.0, in1=xc[:, :, :],
                                      op0=ALU.add, op1=ALU.mult))
            mix_out(4)
            dve.wait_ge(L["lru_a"], 4)
            V.scalar_tensor_tensor(out=gt[:, :, :], in0=asq[:, :, :], scalar=1.0, in1=gt[:, :, :],
                                   op0=ALU.add, op1=ALU.mult).then_inc(L["lru_d"], 1)
            mix_out(5)
            dve.wait_ge(L["lru_a"], 5)
            st(V.tensor_tensor(xc[:, :, :], gt[:, :, :], xc[:, :, :], ALU.mult))
            for b in range(4):
                ins = V.tensor_tensor_scan(asq[:, b, :], ga[:, b, :], xc[:, b, :], 0.0, ALU.mult, ALU.add)
                if b < 3:
                    ins.then_inc(L["d_step"], 1)
                    st.n += 1
                else:
                    st(ins)
            V.scalar_tensor_tensor(out=ga[:, :, :], in0=asq[:, :, :], scalar=0.5, in1=proj[:, GR:GR + 4, :],
                                   op0=ALU.mult, op1=ALU.mult).then_inc(L["lru_d"], 1)
            mix_out(6)

            rope_n = [0]

            def rope(m, scale):
                n = rope_n[0]
                rope_n[0] += 1
                dve.wait_ge(L["rope_ps"], n + 1)
                V.scalar_tensor_tensor(out=rtmp[:, n % 2, :], in0=ps[:, 6 + n % 2, :], scalar=scale, in1=ropeS[:, :],
                                       op0=ALU.mult, op1=ALU.mult).then_inc(L["rope_rd"], 1)
                st(V.scalar_tensor_tensor(out=proj[:, m, :], in0=proj[:, m, :], scalar=scale, in1=ropeC[:, :],
                                          op0=ALU.mult, op1=ALU.mult))
                dve.wait_ge(L["rope_rd"], n + 1)
                V.tensor_tensor(proj[:, m, :], proj[:, m, :], rtmp[:, n % 2, :], ALU.add).then_inc(L["rope_r"], 1)

            dve.wait_ge(L["yhi_r"], 1)
            dve.wait_ge(L["lru_d"], 4)
            V.tensor_tensor(oylo[:, 4:8, :], ga[:, :, :], oyhi[:, 4:8, :].bitcast(F32), ALU.subtract
                            ).then_inc(L["oy_r"], 1)
            mix_out(7)
            for m in range(Q0, Q0 + 4):
                rope(m, 0.125)
            mix_out(8)
            mix_out(9)
            for m in range(K0, K0 + 4):
                rope(m, 1.0)

            def nmax(n):
                p, w = n % 2, (n % 4 + 1) * P
                dve.wait_ge(L["qk_r"], n + 1)
                if n >= 2:
                    dve.wait_ge(L["exp_r"], 2 * (n - 1))
                V.tensor_reduce(small[:, 44 + 2 * p:46 + 2 * p], ps[:, 2 * p:2 * p + 2, 0:w], AX.X, ALU.max,
                                negate=True).then_inc(L["nmax_r"], 1)

            def combine(n):
                p, w = n % 2, (n % 4 + 1) * P
                dve.wait_ge(L["exp_r"], 2 * n + 2)
                if n >= 2:
                    dve.wait_ge(L["att_r"], n - 1)
                r1, r2 = 52 + 2 * p, 53 + 2 * p
                st(V.reciprocal(small[:, r1:r2 + 1], small[:, 48 + 2 * p:50 + 2 * p]))
                st(V.tensor_tensor(small[:, r2:r2 + 1], small[:, r2:r2 + 1], small[:, 40:41], ALU.mult))
                if n >= 2:
                    dve.wait_ge(L["attT_r"], n - 1)
                st(V.tensor_scalar(patt[:, p, 0:w], pexp[:, p, 0, 0:w], small[:, r1:r1 + 1], None, ALU.mult))
                V.scalar_tensor_tensor(out=patt[:, p, 0:w], in0=pexp[:, p, 1, 0:w], scalar=small[:, r2:r2 + 1],
                                       in1=patt[:, p, 0:w], op0=ALU.mult, op1=ALU.add).then_inc(L["att_r"], 1)

            nmax(0)
            for n in range(16):
                if n + 1 < 16:
                    nmax(n + 1)
                combine(n)
            dve.wait_ge(L["orst_r"], 2)
            for hd in range(HEADS):
                V.scalar_tensor_tensor(out=osb[:, hd, :], in0=osb[:, hd, :], scalar=small[:, 41:42],
                                       in1=orst[:, hd, :], op0=ALU.mult, op1=ALU.mult).then_inc(L["on_r"], 1)
            for hd in range(HEADS):
                dve.wait_ge(L["ohi_r"], hd + 1)
                V.tensor_tensor(oylo[:, hd, :], osb[:, hd, :], oyhi[:, hd, :].bitcast(F32), ALU.subtract
                                ).then_inc(L["oy_r"], 1)

            def add_to_h(j, bank, k, count):
                tile_wait(k)
                V.tensor_tensor(h[:, 2 * j:2 * j + 2, :], h[:, 2 * j:2 * j + 2, :], TWO(bank), ALU.add
                                ).then_inc(L["h_r"], 1)
                dve.wait_ge(L["h_r"], count)

            for j in range(4):
                add_to_h(j, j % 2, T_OUT + j, j + 1)
                prepare(2, j, C_GMLP, sqmlp)
            norm_recip(2)
            dve.wait_ge(L["phi_r"], 1)
            V.tensor_tensor(plo[:, :, :], pT[:, :, :], phi[:, :, :].bitcast(F32), ALU.subtract).then_inc(L["p_r"], 1)
            for c in range(CHUNKS):
                for j in range(4):
                    n = 4 * c + j
                    tile_wait(T_MLP + 8 * c + j)
                    if n >= 2:
                        dve.wait_ge(L["sqh_r"], 2 * (n - 1))
                    V.scalar_tensor_tensor(out=hm[n % 2][:, :, :], in0=TWO(n % 2), scalar=0.0, in1=rstd2,
                                           op0=ALU.max, op1=ALU.mult).then_inc(L["m_r"], 1)
                    dve.wait_ge(L["sqh_r"], 2 * n + 2)
                    V.tensor_tensor(hidlo[:, 2 * j:2 * j + 2, :], hsq[n % 2][:, :, :],
                                    hidhi[:, 2 * j:2 * j + 2, :].bitcast(F32), ALU.subtract).then_inc(L["hlo_r"], 1)
                for j in range(4):
                    add_to_h(j, j % 2, T_MLP + 8 * c + 4 + j, 4 + 4 * c + j + 1)
                    if c == CHUNKS - 1:
                        prepare(3, j, C_GPLE, sqple)
            norm_recip(3)
            for j in range(4):
                tile_wait(T_GATE + j)
                V.tensor_tensor(gm[j % 2][:, :, :], TWO(j % 2), rstd2, ALU.mult).then_inc(L["g_r"], 1)
                dve.wait_ge(L["gth_r"], j + 1)
                if j == 0:
                    dve.wait_ge(L["pp_r"], 4)
                g = gth[j % 2]
                st(V.scalar_tensor_tensor(out=g[:, :, :], in0=g[:, :, :], scalar=1.0, in1=pp[:, 2 * j:2 * j + 2, :],
                                          op0=ALU.add, op1=ALU.mult))
                st(V.scalar_tensor_tensor(out=h[:, 2 * j:2 * j + 2, :], in0=g[:, :, :], scalar=0.5,
                                          in1=h[:, 2 * j:2 * j + 2, :], op0=ALU.mult, op1=ALU.add))
            dve.wait_ge(L["layer_done"], 2)
            dve.sem_clear(range(lo_num, hi_num + 1))
            dve.sem_inc(layer_go, 1)

        if stage == 1:
            return

        def done_wait(k):
            dve.wait_ge(tile_done, k + (1 + CREDIT))

        def halves(x):
            return x.rearrange("p (a n) -> p a n", a=2)

        st = Chain(dve, d2)
        dve.wait_ge(ld2, 6 * 16)
        st(V.tensor_copy(mask2[:, :, :], masktmp[:, :, :]))

        def recip(n, x):
            dve.wait_ge(n_rt, n)
            V.reciprocal(x, x).then_inc(n_rs, 1)
            dve.wait_ge(n_rs, n)

        recip(1, rstd[:, :])
        for b in range(KB):
            V.scalar_tensor_tensor(out=hres[:, b, CTX:T], in0=h[:, b, :], scalar=p2[:, C2_GF + b:C2_GF + b + 1],
                                   in1=rstd[:, :], op0=ALU.mult, op1=ALU.mult).then_inc(n_x, 1)
        for i in range(2):
            mb = p2[:, C2_MB + 24 * i:C2_MB + 24 * i + 24].unsqueeze(2).broadcast_to([P, 24, 2])
            st(V.tensor_tensor(modv[i][:, :, :], modsb[:, 24 * i:24 * i + 24, :], mb, ALU.add))

        def norm_gain(i):
            nw = p2[:, C2_NW + 8 * i:C2_NW + 8 * i + 8].unsqueeze(2).broadcast_to([P, KB, 2])
            st(V.tensor_scalar(modA[:, :, :], modv[i][:, 8:16, :], 1.0, None, ALU.add))
            st(V.tensor_tensor(modA[:, :, :], modA[:, :, :], nw, ALU.mult))

        SEG = ((0, CTX, 1), (CTX, T, 0))

        def make_in(i, src):
            def lo(b):
                dve.wait_ge(in_hi, KB * i + b + 1)
                V.tensor_tensor(inlo[:, b, :], tin[:, b % 2, :], inhi[:, b, :].bitcast(F32), ALU.subtract
                                ).then_inc(in_lo, 1)
            for b in range(KB):
                if b >= 2:
                    dve.wait_ge(in_lo, KB * i + b - 1)
                V.tensor_tensor(tin[:, b % 2, :], src[:, b, :], rs2[:, :], ALU.mult).then_inc(in_t, 1)
                if b:
                    lo(b - 1)
            lo(KB - 1)

        norm_gain(0)
        for b in range(4):
            st(V.memset(oacc[:, 2 * b:2 * b + 2, :], 0.0))
        st(V.tensor_scalar(p2[:, C2_CP:C2_CP + 192], p2[:, C2_CP:C2_CP + 192], 0.5, None, ALU.mult))
        recip(2, rs2[:, :])
        make_in(0, hres)
        for r in raw:
            V.memset(r[:, 0:2], 0.0)
            V.memset(r[:, 2 + CTX:4 + CTX], 0.0)
            ins = V.memset(r[:, 4 + T:6 + T], 0.0)
        ins.then_inc(pads, 1)
        dt = Chain(dve, dt_d)
        done_wait(T_DT)
        dt(V.tensor_scalar(halves(dtT[:, :]), ps[0:64, 0:2, 0:HALF], p2[0:64, C2_DTB:C2_DTB + 1], None, ALU.add))
        w = lambda n: dtw[n][:, :, :].rearrange("p c r -> p (c r)")
        dve.wait_ge(dt_p, 1)
        dt(V.tensor_copy(w(0), ps[:, 4, 0:384]))
        dve.wait_ge(dt_a, 3)
        softplus(V, dt, w(2), w(1), w(3), w(4), w(5))
        dt(V.tensor_scalar(w(0), w(0), 0.0, None, ALU.max))
        dt(V.tensor_tensor(w(2), w(2), w(0), ALU.add))
        dt(V.scalar_tensor_tensor(out=tab[:, K_G:K_G + 2 * NC, :].rearrange("p (c d) r -> p c (d r)", d=2),
                                  in0=dtw[2][:, :, :], scalar=-1.0, in1=arow[:, :].unsqueeze(1).broadcast_to([P, NC, 64]),
                                  op0=ALU.mult, op1=ALU.mult))
        assert dt.n == DT_G

        def load_params(g, k):
            k(V.tensor_copy(cpg[:, :], p2[:, bass.ds(g * 24 + C2_CP, 24)]))

        def conv_start(s, b, k):
            dve.wait_ge(x_rd, s * 4 + (b + 1))
            if not isinstance(s, int):
                dve.wait_ge(pre_ps, s * 6)
                dve.wait_ge(ck_r, s)
            o, r = convd[:, b, 0:CW], raw[b % 2]
            q = lambda n: cpg[:, 6 * b + n:6 * b + n + 1]
            k(V.tensor_scalar(o, r[:, 0:CW], q(0), q(5), ALU.mult, ALU.add))

        def conv_tap(b, n, k):
            o, r = convd[:, b, 0:CW], raw[b % 2]
            ins = V.scalar_tensor_tensor(out=o, in0=r[:, n:n + CW], scalar=cpg[:, 6 * b + n:6 * b + n + 1], in1=o,
                                         op0=ALU.mult, op1=ALU.add)
            if n < TAPS - 1:
                k(ins)
            else:
                ins.then_inc(cv_c, 1)

        def conv(s, b, k):
            conv_start(s, b, k)
            for n in range(1, TAPS):
                conv_tap(b, n, k)

        def silu(s, b):
            dve.wait_ge(cv_t, s * 4 + (b + 1))
            V.scalar_tensor_tensor(out=convd[:, b, 0:CW], in0=raw[b % 2][:, 2:2 + CW], scalar=1.0,
                                   in1=convd[:, b, 0:CW], op0=ALU.add, op1=ALU.mult).then_inc(cv_r, 1)

        dve.sem_inc(y_rd, 6)
        dve.sem_inc(o_rd, 8)
        load_params(0, st)
        conv(0, 0, st)
        conv(0, 1, st)
        silu(0, 0)
        silu(0, 1)
        conv(0, 2, st)
        dve.wait_ge(dt_p, 2)
        dt(V.tensor_copy(w(3), ps[:, 5, 0:384]))
        dt(V.tensor_copy(w(4), ps[:, 6, 0:384]))
        dt(V.tensor_tensor(w(5), w(4), w(3), ALU.subtract))
        dt(V.tensor_scalar(w(6), w(2), 1e-37, None, ALU.max))
        assert dt.n == DT_C
        dve.wait_ge(dt_a, 5)
        flat = lambda k: tab[:, k:k + 2 * NC, :].rearrange("p c r -> p (c r)")
        dt(V.tensor_tensor(flat(K_NB), w(6), w(3), ALU.subtract))
        dt(V.tensor_tensor(flat(K_TE), w(5), w(2), ALU.mult))
        conv(0, 3, st)
        silu(0, 2)
        silu(0, 3)
        V.memset(acc[:, :], 0.0).then_inc(acc_r2, 1)
        dve.wait_ge(spill, 16)

        def group(g, last):
            kt = g * G_TILES + T_G0
            k = Chain(dve, g_step, g * GROUP_STEPS)

            def z_gate(b):
                dve.wait_ge(z_t, g * 2 + (b + 1))
                V.scalar_tensor_tensor(out=halves(zs[:, b, :]), in0=halves(zs[:, b, :]), scalar=1.0,
                                       in1=ps[:, 2:4, 0:HALF], op0=ALU.add, op1=ALU.mult).then_inc(z_rd, 1)

            z_gate(0)
            k(V.tensor_copy(mng[:, :], p2[:, bass.ds(g * 2 + C2_MN, 2)]))
            V.tensor_copy(tabg[:, :, :], tab[:, :, bass.ds(g * HPG, HPG)]).then_inc(tabg_r, 1)
            dve.wait_ge(tabg_r, g + 1)
            x4 = lambda c: xcb[:, c, 0:256].rearrange("p (r n) -> p r n", r=HPG)
            for c in range(NC):
                dve.wait_ge(tok_r, g * 6 + (c + 1))
                te = tabg[:, K_TE + 2 * c:K_TE + 2 * c + 2, :].unsqueeze(3).broadcast_to([P, 2, HPG, HD])
                V.tensor_tensor(xte[:, c, :, :, :], x4(c).unsqueeze(1).broadcast_to([P, 2, HPG, HD]), te, ALU.mult
                                ).then_inc(xte_r, 1)

            steps = [(0, 1, SLOT_F[0], SLOT_F[1]), (0, 2, SLOT_F[1], SLOT_F[2]), (0, 3, SLOT_F[2], SLOT_F[3]),
                     (0, 4, SLOT_F[3], SLOT_F[4]), (1, 0, SLOT_B[1], SLOT_B[0]), (1, 5, SLOT_B[0], SLOT_B[5]),
                     (1, 4, SLOT_B[5], SLOT_B[4]), (1, 3, SLOT_B[4], SLOT_B[3])]
            dve.wait_ge(sc_r, g * 6 + 6)
            a4 = lambda n: ast[:, n, :].rearrange("p (r n) -> p r n", r=HPG)
            for n, (d, c, before, after) in enumerate(steps):
                dec = tabg[:, K_DEC + 2 * c + d, :].unsqueeze(2).broadcast_to([P, HPG, HD])
                k(V.tensor_tensor(stmp[:, :, :], a4(before), dec, ALU.mult))
                ins = V.tensor_tensor(a4(after), a4(after), stmp[:, :, :], ALU.add)
                if n < len(steps) - 1:
                    k(ins)
            ins.then_inc(scan_r, 1)
            dve.wait_ge(scan_r, g + 1)
            z_gate(1)
            dve.wait_ge(z_rd, g * 2 + 2)

            def chunk(c):
                dve.wait_ge(off_ps, g * 6 + (c + 1))
                if c:
                    dve.wait_ge(y_ps, g * 6 + c)
                ds = [d for d, slot in enumerate((PREV_F[c], PREV_B[c])) if slot is not None]
                n, d0 = len(ds), ds[0]
                ex = tabg[:, K_EXLA + 2 * c + d0:K_EXLA + 2 * c + d0 + n, :].unsqueeze(3).broadcast_to([P, n, HPG, HD])
                src = ps[:, 6, d0 * 256:(d0 + n) * 256].rearrange("p (d r n) -> p d r n", d=n, r=HPG)
                k(V.tensor_tensor(offs[:, 0:n, :, :], src, ex, ALU.mult))
                if n == 2:
                    k(V.tensor_tensor(offs[:, 0, :, :], offs[:, 0, :, :], offs[:, 1, :, :], ALU.add))
                dr = drow[:, bass.ds(g * HPG, HPG)].unsqueeze(2).broadcast_to([P, HPG, HD])
                k(V.tensor_tensor(stmp[:, :, :], x4(c), dr, ALU.mult))
                V.tensor_tensor(offs[:, 0, :, :], offs[:, 0, :, :], stmp[:, :, :], ALU.add).then_inc(offs_r, 1)
                dve.wait_ge(ex_r, g * 6 + (c + 1))
                k(V.tensor_tensor(ebuf[:, 0, :, :], ebuf[:, 0, :, :], ebuf[:, 1, :, :], ALU.add))
                cb = xcb[:, c, 256:384].unsqueeze(1).broadcast_to([P, HPG, P])
                V.tensor_tensor(wdec[:, :, :], ebuf[:, 0, :, :], cb, ALU.mult).then_inc(W_r, 1)

            def gate_y(c):
                dve.wait_ge(y_ps, g * 6 + (c + 1))
                z = zs[:, :, c * P:(c + 1) * P]
                V.scalar_tensor_tensor(out=z, in0=ps[:, 7, (c % 2) * 256:(c % 2) * 256 + 256]
                                       .rearrange("p (b n) -> p b n", b=2), scalar=0.5, in1=z,
                                       op0=ALU.mult, op1=ALU.mult).then_inc(y_rd, 1)

            def u_lo(half):
                dve.wait_ge(uh_r, g * 2 + (half + 1))
                for m in range(2):
                    cols = slice(half * HALF, (half + 1) * HALF)
                    ins = V.scalar_tensor_tensor(out=ul[:, m, cols], in0=zs[:, m, cols], scalar=mng[:, m:m + 1],
                                                 in1=uh[:, m, cols].bitcast(F32), op0=ALU.mult, op1=ALU.subtract)
                ins.then_inc(u_r, 1)

            s1 = g + 1
            chunk(0)
            gate_y(0)
            if not last:
                load_params(s1, k)
            chunk(1)
            if not last:
                conv(s1, 0, k)
            gate_y(1)
            chunk(2)
            if not last:
                silu(s1, 0)
            gate_y(2)
            chunk(3)
            if not last:
                conv(s1, 1, k)
            gate_y(3)
            chunk(4)
            if not last:
                silu(s1, 1)
            gate_y(4)
            chunk(5)
            gate_y(5)
            u_lo(0)
            u_lo(1)
            blk = g * 10 + (3 if last else 5)

            def out_add(j):
                if j < KB - 1:
                    dve.wait_ge(blk_ps, blk + j + 1)
                else:
                    done_wait(kt + (1 if last else 3))
                q = 2 - 2 * (j % 2)
                V.tensor_tensor(halves(oacc[:, j, :]), halves(oacc[:, j, :]), ps[:, q:q + 2, 0:HALF], ALU.add
                                ).then_inc(o_rd, 1)

            def squares(m):
                dve.wait_ge(sqz_r, g + 1)
                ins = V.tensor_tensor(acc[:, :], acc[:, :], sqz[:, m, :], ALU.add)
                if m:
                    ins.then_inc(acc_r2, 1)
                else:
                    k(ins)

            if last:
                squares(0)
                squares(1)
                for j in range(KB):
                    out_add(j)
            else:
                conv_start(s1, 2, k)
                conv_tap(2, 1, k)
                out_add(0)
                conv_tap(2, 2, k)
                out_add(1)
                conv_tap(2, 3, k)
                out_add(2)
                conv_tap(2, 4, k)
                out_add(3)
                conv_start(s1, 3, k)
                out_add(4)
                silu(s1, 2)
                out_add(5)
                squares(0)
                out_add(6)
                out_add(7)
                conv_tap(3, 1, k)
                conv_tap(3, 2, k)
                conv_tap(3, 3, k)
                conv_tap(3, 4, k)
                squares(1)
                silu(s1, 3)
            dve.wait_ge(o_rd, g * 8 + 16)
            dve.wait_ge(acc_r2, g + 2)
            if not last:
                assert k.n == GROUP_STEPS, k.n

        with dve.Fori(0, GROUPS - 1) as g:
            group(g, False)
        group(GROUPS - 1, True)

        recip(3, rs2[:, :])
        dve.wait_ge(spill, 32)
        for b in range(KB):
            st(V.tensor_tensor(oacc[:, b, :], oacc[:, b, :], rs2[:, :], ALU.mult))
            for t0, t1, c in SEG:
                ins = V.scalar_tensor_tensor(out=oacc[:, b, t0:t1], in0=oacc[:, b, t0:t1], scalar=modv[0][:, 16 + b, c:c + 1],
                                             in1=hback[:, b, t0:t1], op0=ALU.mult, op1=ALU.add)
            ins.then_inc(n_x, 1)
        dve.wait_ge(n_x, 2 * KB)
        norm_gain(1)
        recip(4, rs2[:, :])
        make_in(1, oacc)
        dve.wait_ge(rsh_r, 1)
        for m in range(2):
            ins = V.scalar_tensor_tensor(out=kf[:, m, :], in0=kf[:, m, :], scalar=p2[:, C2_KN:C2_KN + 1],
                                         in1=ksq[:, m, :], op0=ALU.mult, op1=ALU.mult)
        ins.then_inc(qn_r, 1)
        for n in range(2):
            dve.wait_ge(rsh_r, 2 + n)
            V.scalar_tensor_tensor(out=qb_[:, 4 * n:4 * n + 4, :], in0=qb_[:, 4 * n:4 * n + 4, :],
                                   scalar=p2[:, C2_QN:C2_QN + 1], in1=qsq[:, 4 * n:4 * n + 4, :],
                                   op0=ALU.mult, op1=ALU.mult).then_inc(qn_r, 1)
        dve.wait_ge(qn_r, 3)
        for x in K2:
            st(V.memset(x[64:128, :].bitcast(F32), 0.0))
            st(V.memset(x[64:65, :].bitcast(F32), 1.0))
            st(V.memset(x[96:97, :].bitcast(F32), 1.0))
        for j in range(4):
            dve.wait_ge(g_t, j + 1)
            x = gs[:, 2 * j:2 * j + 2, :]
            V.scalar_tensor_tensor(out=x, in0=x, scalar=1.0, in1=TWO(j % 2), op0=ALU.add, op1=ALU.mult
                                   ).then_inc(g_rd, 1)
        for n in range(10):
            x, f = (kf[:, n, CTX:T], 1.0) if n < 2 else (qb_[:, n - 2, :], HD ** -0.5)
            dve.wait_ge(rp_ps, n + 1)
            V.scalar_tensor_tensor(out=rt2[:, n % 2, :], in0=ps[:, 4 + n % 4, :], scalar=f, in1=sinT[:, :],
                                   op0=ALU.mult, op1=ALU.mult).then_inc(rp_rd, 1)
            st(V.scalar_tensor_tensor(out=x, in0=x, scalar=f, in1=cosT[:, :], op0=ALU.mult, op1=ALU.mult))
            dve.wait_ge(rp_rd, n + 1)
            V.tensor_tensor(x, x, rt2[:, n % 2, :], ALU.add).then_inc(rp_r, 1)
            if n >= 1:
                dve.wait_ge(rp_r, n)
        dve.wait_ge(rp_r, 10)
        dve.wait_ge(vt_r, NC)
        st(V.memset(vaug[:, :, 64:128], 1.0))

        with dve.Fori(0, 2) as i:
            k = Chain(dve, h_step, i * HEAD_STEPS)
            def k_split(j):
                dve.wait_ge(k_hi, i * 2 + (j + 1))
                V.tensor_tensor(K1[j][64:128, :], kk[:, :], K1[j][0:64, :].bitcast(F32), ALU.subtract
                                ).then_inc(k_lo, 1)

            def q_split(hq):
                p = hq % 3
                dve.wait_ge(q_hi, i * 8 + (hq + 1))
                V.tensor_tensor(Q2[p][0:64, :], qq[:, :], Q1[p][0:64, :].bitcast(F32), ALU.subtract
                                ).then_inc(q_lo, 1)

            def sum_recip(b, t):
                dve.wait_ge(o_ev, i * 8 + (2 * b + 2))
                k(V.reciprocal(osum[:, t * P:(t + 1) * P], osum[:, t * P:(t + 1) * P]))

            def maxima(hq, b=None):
                p = hq % 2
                if hq > 1:
                    dve.wait_ge(mx_ps, i * 8 + (hq - 1))
                for t in range(4):
                    dve.wait_ge(s_ps, i * 32 + (4 * hq + t + 1))
                    q = 2 * (t % 2)
                    V.tensor_reduce(nmx[:, p, t, :], ps[:, q:q + 2, 0:HALF], AX.X, ALU.max).then_inc(mx_r, 1)
                    if b is not None and t < 3:
                        sum_recip(b, t)
                dve.wait_ge(mx_r, i * 32 + (4 * hq + 4))
                V.tensor_reduce(nm4[:, p, :], nmx[:, p, :, :], AX.X, ALU.max, negate=True).then_inc(mxf_r, 1)
                dve.wait_ge(mxf_r, i * 8 + (hq + 1))

            def gated(b):
                x = qb_[:, bass.ds(i * 4 + b, 1), :].rearrange("p a n -> p (a n)")
                g = gs[:, bass.ds(i * 4 + b, 1), :].rearrange("p a n -> p (a n)")
                k(V.tensor_tensor(x, x, osum[:, :], ALU.mult))
                V.scalar_tensor_tensor(out=x, in0=x, scalar=0.5, in1=g, op0=ALU.mult, op1=ALU.mult).then_inc(oy2, 1)

            def o_lo(b):
                dve.wait_ge(oh_r, i * 4 + (b + 1))
                sl = bass.ds(i * 4 + b, 1)
                V.tensor_tensor(olo[:, sl, :], qb_[:, sl, :], ohi[:, sl, :].bitcast(F32), ALU.subtract).then_inc(ol_r, 1)

            def max_lo(hq):
                p = hq % 3
                dve.wait_ge(mxh_r, i * 8 + (hq + 1))
                V.tensor_tensor(Q2[p][96:128, :], ps[96:128, 4, :], Q2[p][96:128, :].bitcast(F32), ALU.subtract
                                ).then_inc(mxl_r, 1)

            q_split(0)
            k_split(0)
            q_split(1)
            maxima(0)
            max_lo(0)
            for hq in range(8):
                pair = hq // 2 - 1 if hq % 2 == 0 and hq else None
                if hq + 1 < 8:
                    maxima(hq + 1, pair)
                if hq + 2 < 8:
                    q_split(hq + 2)
                if hq + 1 < 8:
                    max_lo(hq + 1)
                if hq == 1:
                    k_split(1)
                if pair is not None:
                    sum_recip(pair, 3)
                    gated(pair)
                if hq % 2 == 1 and hq > 1:
                    o_lo(hq // 2 - 1)
            for t in range(4):
                sum_recip(3, t)
            gated(3)
            o_lo(3)
            dve.wait_ge(ol_r, i * 4 + 4)
            assert k.n == HEAD_STEPS, k.n

        for j in range(4):
            done_wait(T_ATT + 10 + j)
            for m in range(2):
                b = 2 * j + m
                ins = V.scalar_tensor_tensor(out=oacc[:, b, CTX:T], in0=ps[:, 2 * (j % 2) + m, :],
                                             scalar=modv[1][:, 16 + b, 0:1], in1=oacc[:, b, CTX:T],
                                             op0=ALU.mult, op1=ALU.add)
            ins.then_inc(hf_r, 1)
        dve.wait_ge(hf_r, 4)
        recip(5, rs5[:, :])
        for b in range(KB):
            V.scalar_tensor_tensor(out=hfin[:, b, :], in0=oacc[:, b, CTX:T], scalar=p2[:, C2_FN + b:C2_FN + b + 1],
                                   in1=rs5[:, :], op0=ALU.mult, op1=ALU.mult).then_inc(fin, 1)

    ctx.close()


D_ANGLE, D_SILU, INIT_D, INIT_A = 11, 13, 14, 4
CST = 16 * 8
DT_G, DT_C = 18, 22
GROUP_STEPS, HEAD_STEPS = 56, 20


def softplus(V, st, out, e, z, z2, p):
    st(V.tensor_scalar(z, e, 2.0, None, ALU.add))
    st(V.reciprocal(z, z))
    st(V.tensor_tensor(z, z, e, ALU.mult))
    st(V.tensor_tensor(z2, z, z, ALU.mult))
    st(V.tensor_scalar(p, z2, 1.0 / 15, None, ALU.mult))
    for n in (13, 11, 9, 7, 5, 3):
        st(V.scalar_tensor_tensor(out=p, in0=p, scalar=1.0 / n, in1=z2, op0=ALU.add, op1=ALU.mult))
    st(V.scalar_tensor_tensor(out=p, in0=p, scalar=1.0, in1=z, op0=ALU.add, op1=ALU.mult))
    st(V.tensor_scalar(out, p, 2.0, None, ALU.mult))


def cut(w):
    k, m = w.shape
    w = w.reshape(k // D, KB, P, m // TM, TM).transpose(0, 3, 2, 1, 4)
    return w.reshape(-1, P, TILE)


def cut_wide(w):
    k, m = w.shape
    return w.reshape(k // TM, 2, P, m).transpose(0, 2, 1, 3).reshape(-1, P, TILE)


def columns(v):
    return v.reshape(-1, P).T


def feature_major(x):
    return np.ascontiguousarray(x.T.reshape(-1, P, x.shape[0]).transpose(1, 0, 2))


def consts():
    c = np.zeros((P, 400), np.float32)
    c[:, 0:128] = np.eye(P)
    for half in (0, 64):
        for i in range(ROT // 2):
            c[half + i, 128 + half + 8 + i] = 1
            c[half + 8 + i, 128 + half + i] = 1
            inv = np.float32(500000.0) ** (-np.float32(i) * np.float32(2.0) / np.float32(ROT))
            c[half + i, 257] = c[half + 8 + i, 257] = inv
            c[half + i, 259], c[half + 8 + i, 259] = -1, 1
    c[:, 256] = EPS
    c[:, 258] = math.pi / 2
    c[:, 272:400] = np.where(np.arange(P)[None, :] > np.arange(P)[:, None], -1e30, 0)
    return c


def layer_tiles(i, l):
    w_in = i["w_in"][l]
    w_in = np.concatenate([w_in[:, 1536:2560], w_in[:, 0:1536]], 1)
    mix, out = cut(w_in), cut(i["w_out"][l])
    up = cut(i["w_mlp_in"][l]).reshape(CHUNKS, 4, P, TILE)
    down = cut(i["w_mlp_out"][l]).reshape(CHUNKS, 4, P, TILE)
    mlp = np.stack([up, down], 1).reshape(-1, P, TILE)
    return [mix, out, mlp, cut_wide(i["w_ple_proj"][l]), cut(i["w_ple_gate"][l]), np.zeros((1, P, TILE), np.float32)]


def layer_params(i, l):
    t = np.zeros((P, NLP), np.float32)
    for c, name in ((C_GMIX, "g_mix"), (C_GMLP, "g_mlp"), (C_GPLE, "g_ple"), (C_CB, "conv_b"), (C_BA, "b_gate_a"),
                    (C_BX, "b_gate_x"), (C_LRU, "lru_lambda"), (C_GSUB, "g_subln")):
        v = columns(i[name][l])
        t[:, c:c + v.shape[1]] = v
    for tap in range(4):
        t[:, C_CW + 4 * tap:C_CW + 4 * tap + 4] = columns(i["conv_w"][l, tap])
    for c, name in ((C_LQ, "lam_q"), (C_LK, "lam_k")):
        for n in range(2):
            t[64 * n:64 * n + 64, c + n] = i[name][l, n]
    lam_init = 0.8 - 0.6 * math.exp(-0.3 * l)
    t[:, C_LI], t[:, C_1LI] = lam_init, 1.0 - lam_init
    return t


def gate_blocks(i, l):
    t = np.zeros((P, 8, P), np.float32)
    for n, name in enumerate(("w_gate_a", "w_gate_x")):
        for g in range(8):
            r = 64 * (g % 2)
            t[r:r + 64, 4 * n + g // 2, r:r + 64] = i[name][l, g]
    return t


def second_tiles(i):
    w, out = i["m_in_w_2"][0], cut_wide(i["m_out_w_2"][0])
    conv0 = MDI
    b0, c0, dt0 = 2 * MDI, 2 * MDI + GROUPS * NS, 2 * MDI + 2 * GROUPS * NS
    dt = np.zeros((1, P, TILE), np.float32)
    dt[0, :, 0:KB * 64] = w[:, dt0:].reshape(KB, P, 64).transpose(1, 0, 2).reshape(P, KB * 64)
    z = lambda g: cut(w[:, 256 * g:256 * g + 256])
    x = lambda g: cut(w[:, conv0 + 256 * g:conv0 + 256 * g + 256])
    bc = lambda g: cut(np.concatenate([w[:, b0 + NS * g:b0 + NS * (g + 1)], w[:, c0 + NS * g:c0 + NS * (g + 1)]], 1))
    tiles = [dt, x(0), bc(0)]
    for g in range(GROUPS):
        tiles.append(z(g))
        if g + 1 < GROUPS:
            tiles += [x(g + 1), bc(g + 1)]
        tiles.append(out[g:g + 1])
    a = i["a_in_w_2"][0]
    a = np.concatenate([a[:, D:D + 512], a[:, 0:D], a[:, D + 512:]], 1)
    tiles += [cut(a), cut(i["a_out_w_2"][0])]
    n = sum(len(t) for t in tiles)
    if n % 2:
        tiles.append(np.zeros((1, P, TILE), np.float32))
    return tiles


def params2(i):
    t = np.zeros((P, NP2), np.float32)
    for c, v in ((C2_GF, i["g_final"]), (C2_NW, i["norm_w_2"].reshape(-1)), (C2_MB, i["mod_b_2"].reshape(-1)),
                 (C2_FN, i["final_norm_w_2"]), (C2_MN, i["m_norm_w_2"][0])):
        v = columns(v)
        t[:, c:c + v.shape[1]] = v
    taps = np.concatenate([i["m_conv_w_2"][0], i["m_conv_b_2"]])
    cols = np.stack([columns(v) for v in taps], 2)
    for g in range(GROUPS):
        for n, b in enumerate((2 * g, 2 * g + 1, 2 * GROUPS + g, 3 * GROUPS + g)):
            c = C2_CP + 24 * g + 6 * n
            t[:, c:c + 6] = cols[:, b]
    t[0:64, C2_DTB] = i["m_dt_bias_2"][0].reshape(-1)
    t[:, C2_QN] = np.tile(i["a_q_norm_2"][0], 2)
    t[:, C2_KN] = np.tile(i["a_k_norm_2"][0], 2)
    return t


def consts2():
    c = np.zeros((P, 768), np.float32)
    a, b = np.arange(P)[:, None], np.arange(P)[None, :]
    c[:, 0:128] = a <= b
    c[:, 128:256] = a >= b
    c[:, 256:384] = np.where(a <= b, 0, -1e30)
    c[:, 384:512] = np.where(a >= b, 0, -1e30)
    c[:, 512:640] = a // 64 == b // 64
    c[:, 640:768] = (a ^ 16) == b
    return c


def axial():
    half = 32
    inv = np.float32(10000.0) ** (-np.arange(0, half, 2, dtype=np.float32) / np.float32(half))
    d = np.arange(P) % 64
    t = np.arange(S)
    pos = np.where((d // 32 == 0)[:, None], (t // 64)[None, :], (t % 64)[None, :]).astype(np.float32)
    ang = pos * inv[d % 16][:, None]
    sign = np.where(d % 32 < 16, -1, 1)[:, None]
    return np.stack([np.cos(ang), sign * np.sin(ang)]).astype(np.float32)


def host_arrays(i):
    i = {k: np.asarray(v) for k, v in i.items()}
    tiles = []
    for l in range(DEPTH):
        tiles += layer_tiles(i, l)
    a = {
        "wstream": tiles,
        "x": feature_major(i["x"][0]),
        "positions": i["positions"].reshape(S),
        "cvec": np.ascontiguousarray(np.stack([columns(i["c_2"][0]), columns(i["c_ctx_2"])], 2)),
        "lparams": np.ascontiguousarray(np.stack([layer_params(i, l) for l in range(DEPTH)], 1)),
        "gates": np.stack([gate_blocks(i, l) for l in range(DEPTH)]),
        "pT": np.stack([feature_major(i["p"][l, 0]) for l in range(DEPTH)]),
        "consts": consts(),
        "modw": np.ascontiguousarray(i["mod_w_2"].reshape(DEPTH, KB, P, MODS, P).transpose(0, 3, 2, 1, 4)
                                     .reshape(DEPTH * MODS, P, KB, P)),
        "ctx": feature_major(i["ctx_2"][0]),
        "m_d": i["m_d_2"][0],
        "m_a_log": i["m_a_log_2"][0].reshape(-1),
        "params2": params2(i),
        "consts2": consts2(),
        "axial": axial(),
    }
    tiles += second_tiles(i)
    a["wstream"] = np.concatenate(a["wstream"])
    return a


def kernel(**inputs):
    import concourse.bacc as bacc
    from concourse.bass_utils import run_bass_kernel_spmd

    arrays = host_arrays(inputs)
    nc = bacc.Bacc("TRN2", target_bir_lowering=False, num_devices=1)
    io = {n: nc.dram_tensor(f"in_{n}", a.shape, mybir.dt.from_np(a.dtype), kind="ExternalInput").ap()
          for n, a in arrays.items()}
    io["out"] = nc.dram_tensor("out", (P, KB, S), F32, kind="ExternalOutput").ap()
    build(nc, io)
    r = run_bass_kernel_spmd(nc, [{f"in_{n}": a for n, a in arrays.items()}], core_ids=[0])
    out = r.results[0]["out"]
    return np.ascontiguousarray(out.transpose(2, 1, 0).reshape(1, S, D))
```
